# Optimizing a Trainium2 kernel written in Bass

```python
import jax, jax.numpy as jnp
from jax import lax
import numpy as np

D_MODEL = 2048
BATCH = 1
SEQ = 512
DEPTH = 1

GRID_W = 64
CTX_LEN = 256
HEAD_DIM = 64
A_HEADS = 8
B_HEADS = 8
B_KV_HEADS = 2
C_HEADS = 16
A_WIDTH = A_HEADS * HEAD_DIM
B_WIDTH = B_HEADS * HEAD_DIM
B_KV_WIDTH = B_KV_HEADS * HEAD_DIM
C_WIDTH = C_HEADS * HEAD_DIM
MIX_WIDTH = A_WIDTH + B_WIDTH + C_WIDTH
NA_KH = 8
NA_KW = 16
DECAY_LORA = 64
ICLR_LORA = 64
GATE_LORA = 160
D_FF = 5632
ROPE_PAIRS = HEAD_DIM // 4
ROPE_THETA = 10000.0
Q_BLOCK = 128
NORM_EPS = 1e-6
LNX_EPS = 64e-5
RW_SIZES = (3 * C_WIDTH, 2 * DECAY_LORA, 2 * ICLR_LORA, GATE_LORA)
RW_COLS = sum(RW_SIZES)
IN_SIZES = (A_WIDTH, A_WIDTH, A_WIDTH, B_WIDTH, B_KV_WIDTH, B_KV_WIDTH, RW_COLS)
IN_COLS = sum(IN_SIZES)

kernel_name = 'hybrid_natten_gqa_rwkv7_dit_block'

def split_cols(z, sizes):
    return jnp.split(z, np.cumsum(sizes)[:-1].tolist(), axis=-1)

def rms_normalize(x, eps=NORM_EPS):
    xf = x.astype(jnp.float32)
    return xf * lax.rsqrt(jnp.mean(xf * xf, axis=-1, keepdims=True) + eps)

def rmsnorm(x, gain):
    return (rms_normalize(x) * gain.astype(jnp.float32)).astype(x.dtype)

def group_rmsnorm(parts, gain):
    y = jnp.concatenate([rms_normalize(p) for p in parts], axis=-1)
    return (y * gain.astype(jnp.float32)).astype(parts[0].dtype)

def heads(z, n):
    return z.reshape(z.shape[:2] + (n, HEAD_DIM))

def shift_prev(f):
    pad = [(0, 0)] * f.ndim
    pad[1] = (1, 0)
    return jnp.pad(f[:, :-1], pad)

def shift_next(f):
    pad = [(0, 0)] * f.ndim
    pad[1] = (0, 1)
    return jnp.pad(f[:, 1:], pad)

def dwconv3(f, w, b):
    return shift_prev(f) * w[0] + f * w[1] + shift_next(f) * w[2] + b

def rope_tables(length):
    pos = jnp.arange(length)
    inv_freq = ROPE_THETA ** (-jnp.arange(ROPE_PAIRS, dtype=jnp.float32) / ROPE_PAIRS)
    ang_row = (pos // GRID_W).astype(jnp.float32)[:, None] * inv_freq[None, :]
    ang_col = (pos % GRID_W).astype(jnp.float32)[:, None] * inv_freq[None, :]
    ang = jnp.concatenate([ang_row, ang_col], axis=-1)
    return jnp.cos(ang), jnp.sin(ang)

def apply_rope(x, cos, sin):
    B_, L, H, Dh = x.shape
    xs = x.astype(jnp.float32).reshape(B_, L, H, 2, 2, ROPE_PAIRS)
    x1, x2 = xs[..., 0, :], xs[..., 1, :]
    c = cos.reshape(L, 2, ROPE_PAIRS)[None, :, None]
    s = sin.reshape(L, 2, ROPE_PAIRS)[None, :, None]
    out = jnp.stack([x1 * c - x2 * s, x1 * s + x2 * c], axis=-2)
    return out.reshape(B_, L, H, Dh).astype(x.dtype)

def dense_attention(q, k, v):
    B_, T, Hq, Dh = q.shape
    Hk = k.shape[2]
    qg = q.reshape(B_, T, Hk, Hq // Hk, Dh)
    s = jnp.einsum('btkgd,bskd->bkgts', qg, k).astype(jnp.float32) * (Dh ** -0.5)
    p = jax.nn.softmax(s, axis=-1).astype(v.dtype)
    o = jnp.einsum('bkgts,bskd->btkgd', p, v)
    return o.reshape(B_, T, Hq * Dh)

def gqa_block_sweep(q, k, v, k_ctx, v_ctx):
    B_, L, H, Dh = q.shape
    k_all = jnp.concatenate([k_ctx, k], axis=1)
    v_all = jnp.concatenate([v_ctx, v], axis=1)
    q_blocks = jnp.moveaxis(q.reshape(B_, L // Q_BLOCK, Q_BLOCK, H, Dh), 1, 0)
    o = lax.map(lambda qb: dense_attention(qb, k_all, v_all), q_blocks)
    return jnp.moveaxis(o, 0, 1).reshape(B_, L, H * Dh)

def neighborhood_attention(q, k, v, k_ctx, v_ctx, rpb):
    B_, L, H, Dh = q.shape
    rows = L // GRID_W
    kh = min(NA_KH, rows)
    scale = Dh ** -0.5
    qg = q.reshape(B_, rows, GRID_W, H, Dh)
    row_ids = jnp.arange(rows)
    row_start = jnp.clip(row_ids - kh // 2, 0, rows - kh)
    key_rows = row_start[:, None] + jnp.arange(kh)[None, :]
    k_blk = k.reshape(B_, rows, GRID_W, H, Dh)[:, key_rows]
    v_blk = v.reshape(B_, rows, GRID_W, H, Dh)[:, key_rows]
    col = jnp.arange(GRID_W)
    col_start = jnp.clip(col - NA_KW // 2, 0, GRID_W - NA_KW)
    in_win = (col[None, :] >= col_start[:, None]) & (col[None, :] < col_start[:, None] + NA_KW)
    row_off = key_rows - row_ids[:, None] + (NA_KH - 1)
    col_off = jnp.clip(col[None, :] - col[:, None], -(NA_KW - 1), NA_KW - 1) + (NA_KW - 1)
    bias = rpb.astype(jnp.float32)[:, row_off[:, None, :, None], col_off[None, :, None, :]]
    s = jnp.einsum('bixhd,bijyhd->bhixjy', qg, k_blk).astype(jnp.float32) * scale + bias
    s = jnp.where(in_win[:, None, :], s, -jnp.inf)
    s_ctx = jnp.einsum('bixhd,bchd->bhixc', qg, k_ctx).astype(jnp.float32) * scale
    m = jnp.maximum(jnp.max(s, axis=(-2, -1)), jnp.max(s_ctx, axis=-1))
    e_loc = jnp.exp(s - m[..., None, None])
    e_ctx = jnp.exp(s_ctx - m[..., None])
    denom = jnp.sum(e_loc, axis=(-2, -1)) + jnp.sum(e_ctx, axis=-1)
    p_loc = (e_loc / denom[..., None, None]).astype(v.dtype)
    p_ctx = (e_ctx / denom[..., None]).astype(v.dtype)
    o = jnp.einsum('bhixjy,bijyhd->bixhd', p_loc, v_blk) + jnp.einsum('bhixc,bchd->bixhd', p_ctx, v_ctx)
    return o.reshape(B_, L, H * Dh)

def rwkv7_features(f, mu_rkv, mu_w, mu_a, mu_g, w0, w2, a0, a2, g2, k_k, k_a):
    B_, T, _ = f.shape
    rkv, wd, ad, gd = split_cols(f, RW_SIZES)
    rkv_nb = jnp.stack([shift_prev(rkv), shift_next(rkv)], axis=2)
    rkv = rkv[:, :, None] + mu_rkv * (rkv_nb - rkv[:, :, None])
    wd = wd.reshape(B_, T, 2, DECAY_LORA)
    wd = wd + mu_w * (jnp.stack([shift_prev(wd[:, :, 0]), shift_next(wd[:, :, 1])], axis=2) - wd)
    ad = ad.reshape(B_, T, 2, ICLR_LORA)
    ad = ad + mu_a * (jnp.stack([shift_prev(ad[:, :, 0]), shift_next(ad[:, :, 1])], axis=2) - ad)
    gd = gd + mu_g[0] * (shift_prev(gd) - gd) + mu_g[1] * (shift_next(gd) - gd)
    r, k, v = jnp.split(rkv, 3, axis=-1)
    w_log = -jax.nn.softplus(-(w0 + jnp.einsum('btdr,drc->btdc', jnp.tanh(wd), w2))) - 0.5
    decay = jnp.exp(-jnp.exp(w_log.astype(jnp.float32)))
    a = jax.nn.sigmoid(a0 + jnp.einsum('btdr,drc->btdc', ad, a2))
    g = jax.nn.sigmoid(gd) @ g2
    hd = lambda z: z.reshape(B_, T, 2, C_HEADS, HEAD_DIM)
    kk = hd(k * k_k).astype(jnp.float32)
    kk = kk / jnp.maximum(jnp.sqrt(jnp.sum(kk * kk, axis=-1, keepdims=True)), 1e-12)
    k = k * (1 + (a - 1) * k_a)
    return hd(r), hd(decay), hd(k), hd(v), kk, hd(a), g

def rwkv7_scan(state0, r, decay, k, v, kk, a):
    def to_time_major(z):
        z = jnp.concatenate([z[:, :, :1], jnp.flip(z[:, :, 1:], axis=1)], axis=2)
        return jnp.moveaxis(z.astype(jnp.float32), 1, 0)
    xs = tuple(to_time_major(z) for z in (r, decay, k, v, -kk, kk * a))

    def step(S, inp):
        r_t, w_t, k_t, v_t, a_t, b_t = inp
        sa = jnp.einsum('bdhvk,bdhk->bdhv', S, a_t)
        S = S * w_t[..., None, :] + sa[..., None] * b_t[..., None, :] + v_t[..., None] * k_t[..., None, :]
        return S, jnp.einsum('bdhvk,bdhk->bdhv', S, r_t)

    state, ys = lax.scan(step, state0, xs)
    ys = jnp.moveaxis(ys, 0, 1)
    ys = jnp.concatenate([ys[:, :, :1], jnp.flip(ys[:, :, 1:], axis=1)], axis=2)
    return ys, state

def rwkv7_readout(ys, r, k, v, g, r_k, lnx_g, lnx_b):
    B_, T = ys.shape[:2]
    y = jnp.sum(ys, axis=2)
    mean = jnp.mean(y, axis=-1, keepdims=True)
    var = jnp.mean(jnp.square(y - mean), axis=-1, keepdims=True)
    y = ((y - mean) * lax.rsqrt(var + LNX_EPS)).reshape(B_, T, C_WIDTH) * lnx_g + lnx_b
    bonus = jnp.sum(r * k * r_k, axis=-1, keepdims=True) * v
    y = y + jnp.sum(bonus, axis=2).reshape(B_, T, C_WIDTH)
    return (y * g).astype(g.dtype)

def rwkv7_mixer(f_ctx, f_lat, mu_rkv, mu_w, mu_a, mu_g, w0, w2, a0, a2, g2, k_k, k_a, r_k, lnx_g, lnx_b):
    fc = rwkv7_features(f_ctx, mu_rkv, mu_w, mu_a, mu_g, w0, w2, a0, a2, g2, k_k, k_a)
    fl = rwkv7_features(f_lat, mu_rkv, mu_w, mu_a, mu_g, w0, w2, a0, a2, g2, k_k, k_a)
    state0 = jnp.zeros((f_ctx.shape[0], 2, C_HEADS, HEAD_DIM, HEAD_DIM), jnp.float32)
    ys_c, state_c = rwkv7_scan(state0, *fc[:6])
    ys_l, _ = rwkv7_scan(state_c, *fl[:6])
    out_c = rwkv7_readout(ys_c, fc[0], fc[2], fc[3], fc[6], r_k, lnx_g, lnx_b)
    out_l = rwkv7_readout(ys_l, fl[0], fl[2], fl[3], fl[6], r_k, lnx_g, lnx_b)
    return out_c, out_l

def conv_glu(xn, up, conv_w, conv_b, down):
    u, val = jnp.split(xn @ up, 2, axis=-1)
    u = dwconv3(u, conv_w, conv_b)
    return (jax.nn.gelu(u, approximate=False) * val) @ down

def setup_inputs(seed: int = 0) -> dict:
    key = jax.random.key(seed)
    ks = iter(jax.random.split(key, 48))
    D = D_MODEL

    def nrm(shape, s):
        return jax.random.normal(next(ks), shape, jnp.float32) * s

    def uni(shape):
        return jax.random.uniform(next(ks), shape, jnp.float32)

    return {
        'x': nrm((BATCH, SEQ, D), 1.0),
        'c': nrm((BATCH, D), 1.0),
        'ctx': nrm((BATCH, CTX_LEN, D), 1.0),
        'c_ctx': nrm((D,), 1.0),
        'ada_w': nrm((DEPTH, D, 6 * D), 0.5 * D ** -0.5),
        'ada_b': nrm((DEPTH, 6 * D), 0.02),
        'norm1_g': 1.0 + nrm((DEPTH, D), 0.02),
        'norm2_g': 1.0 + nrm((DEPTH, D), 0.02),
        'w_in': nrm((DEPTH, D, IN_COLS), D ** -0.5),
        'na_rpb': nrm((DEPTH, A_HEADS, 2 * NA_KH - 1, 2 * NA_KW - 1), 0.2),
        'q_gain': 1.0 + nrm((DEPTH, HEAD_DIM), 0.02),
        'k_gain': 1.0 + nrm((DEPTH, HEAD_DIM), 0.02),
        'rw_mu_rkv': uni((DEPTH, 2, 3 * C_WIDTH)),
        'rw_mu_w': uni((DEPTH, 2, DECAY_LORA)),
        'rw_mu_a': uni((DEPTH, 2, ICLR_LORA)),
        'rw_mu_g': uni((DEPTH, 2, GATE_LORA)),
        'rw_w0': -2.0 + nrm((DEPTH, 2, C_WIDTH), 0.5),
        'rw_w2': nrm((DEPTH, 2, DECAY_LORA, C_WIDTH), 0.5 * DECAY_LORA ** -0.5),
        'rw_a0': nrm((DEPTH, 2, C_WIDTH), 0.2),
        'rw_a2': nrm((DEPTH, 2, ICLR_LORA, C_WIDTH), ICLR_LORA ** -0.5),
        'rw_g2': nrm((DEPTH, GATE_LORA, C_WIDTH), GATE_LORA ** -0.5),
        'rw_k_k': 0.85 + nrm((DEPTH, C_WIDTH), 0.05),
        'rw_k_a': 1.0 + nrm((DEPTH, C_WIDTH), 0.05),
        'rw_r_k': nrm((DEPTH, C_HEADS, HEAD_DIM), 0.1),
        'rw_lnx_g': 1.0 + nrm((DEPTH, C_WIDTH), 0.02),
        'rw_lnx_b': nrm((DEPTH, C_WIDTH), 0.02),
        'grp_g': 1.0 + nrm((DEPTH, MIX_WIDTH), 0.02),
        'w_out': nrm((DEPTH, MIX_WIDTH, D), MIX_WIDTH ** -0.5),
        'ffn_up': nrm((DEPTH, D, 2 * D_FF), D ** -0.5),
        'ffn_conv_w': nrm((DEPTH, 3, D_FF), 0.5),
        'ffn_conv_b': nrm((DEPTH, D_FF), 0.02),
        'ffn_down': nrm((DEPTH, D_FF, D), D_FF ** -0.5),
        'final_g': 1.0 + nrm((D,), 0.02),
    }

def reference(x, c, ctx, c_ctx, ada_w, ada_b, norm1_g, norm2_g, w_in, na_rpb, q_gain, k_gain,
              rw_mu_rkv, rw_mu_w, rw_mu_a, rw_mu_g, rw_w0, rw_w2, rw_a0, rw_a2, rw_g2,
              rw_k_k, rw_k_a, rw_r_k, rw_lnx_g, rw_lnx_b, grp_g, w_out,
              ffn_up, ffn_conv_w, ffn_conv_b, ffn_down, final_g):
    L = x.shape[1]
    cos, sin = rope_tables(L)
    h, hc = x, ctx
    cond_lat = jax.nn.silu(c)[:, None, :]
    cond_ctx = jax.nn.silu(c_ctx)[None, None, :]
    for l in range(DEPTH):
        update_ctx = l < DEPTH - 1
        sh1, sc1, gt1, sh2, sc2, gt2 = jnp.split(cond_lat @ ada_w[l] + ada_b[l], 6, axis=-1)
        csh1, csc1, cgt1, csh2, csc2, cgt2 = jnp.split(cond_ctx @ ada_w[l] + ada_b[l], 6, axis=-1)

        xn = rmsnorm(h, norm1_g[l]) * (1 + sc1) + sh1
        xnc = rmsnorm(hc, norm1_g[l]) * (1 + csc1) + csh1
        qa, ka, va, qb, kb, vb, fr = split_cols(xn @ w_in[l], IN_SIZES)
        qac, kac, vac, qbc, kbc, vbc, frc = split_cols(xnc @ w_in[l], IN_SIZES)

        ka_c, va_c = heads(kac, A_HEADS), heads(vac, A_HEADS)
        out_a = neighborhood_attention(heads(qa, A_HEADS), heads(ka, A_HEADS), heads(va, A_HEADS),
                                       ka_c, va_c, na_rpb[l])
        kb_c = rmsnorm(heads(kbc, B_KV_HEADS), k_gain[l])
        vb_c = heads(vbc, B_KV_HEADS)
        q_b = apply_rope(rmsnorm(heads(qb, B_HEADS), q_gain[l]), cos, sin)
        k_b = apply_rope(rmsnorm(heads(kb, B_KV_HEADS), k_gain[l]), cos, sin)
        out_b = gqa_block_sweep(q_b, k_b, heads(vb, B_KV_HEADS), kb_c, vb_c)
        out_c_ctx, out_c = rwkv7_mixer(frc, fr, rw_mu_rkv[l], rw_mu_w[l], rw_mu_a[l], rw_mu_g[l],
                                       rw_w0[l], rw_w2[l], rw_a0[l], rw_a2[l], rw_g2[l],
                                       rw_k_k[l], rw_k_a[l], rw_r_k[l], rw_lnx_g[l], rw_lnx_b[l])
        mix = group_rmsnorm((out_a, out_b, out_c), grp_g[l]) @ w_out[l]
        h = h + gt1 * mix

        xn2 = rmsnorm(h, norm2_g[l]) * (1 + sc2) + sh2
        h = h + gt2 * conv_glu(xn2, ffn_up[l], ffn_conv_w[l], ffn_conv_b[l], ffn_down[l])

        if update_ctx:
            out_a_c = dense_attention(heads(qac, A_HEADS), ka_c, va_c)
            out_b_c = dense_attention(rmsnorm(heads(qbc, B_HEADS), q_gain[l]), kb_c, vb_c)
            mix_c = group_rmsnorm((out_a_c, out_b_c, out_c_ctx), grp_g[l]) @ w_out[l]
            hc = hc + cgt1 * mix_c
            xnc2 = rmsnorm(hc, norm2_g[l]) * (1 + csc2) + csh2
            hc = hc + cgt2 * conv_glu(xnc2, ffn_up[l], ffn_conv_w[l], ffn_conv_b[l], ffn_down[l])
    return rmsnorm(h, final_g)


_drawn_inputs = setup_inputs


def setup_inputs(seed=0):
    import zlib

    import numpy as np

    out = dict(_drawn_inputs(seed))
    spreads = {}
    factors = {'norm1_g': 7.018,
     'norm2_g': 8.0,
     'na_rpb': 7.485,
     'q_gain': 8.0,
     'k_gain': 8.0,
     'rw_mu_w': 64.0,
     'rw_w2': 31.28,
     'rw_a0': 3.339,
     'rw_k_k': 64.0,
     'rw_k_a': 4.143,
     'rw_lnx_g': 64.0,
     'rw_lnx_b': 64.0,
     'grp_g': 8.0,
     'ffn_conv_b': 8.0,
     'final_g': 2.732,
     'rw_w0': 8.0}
    for name, (base, spread) in spreads.items():
        noise = np.random.default_rng([zlib.crc32(name.encode()), seed]).standard_normal(out[name].shape)
        drawn = base * np.exp(spread * noise) if base else spread * noise
        out[name] = __import__('jax').numpy.asarray(drawn.astype(out[name].dtype))
    for name, factor in factors.items():
        out[name] = (out[name] * factor).astype(out[name].dtype)
    return out
```

```python
from contextlib import ExitStack

import numpy as np

import concourse.bass as bass
from concourse import mybir

F32 = mybir.dt.float32
F32R = mybir.dt.float32r
ALU = mybir.AluOpType
ACT = mybir.ActivationFunctionType
AX_X = mybir.AxisListType.X

P = 128
D = 2048
KT = D // P
LAT = 512
CTX = 256
TOK = CTX + LAT
HD = 64
GRID = 64
ROWS = LAT // GRID
NAW = 16
RPB_C = 2 * NAW - 1
RPB_R = 15
AH = 8
BH = 8
CW = 1024
PAIRS = CW // P
DFF = 5632
FT = DFF // P
GLORA = 160
IN_COLS = 5792
EPS = 1e-6
LNX_EPS = 64e-5
CH = 64
BT = 256
CPB = BT // CH
NB = TOK // BT
NLEV = 5

QA, KA, VA, QB, KVB, RW_R, RW_K, RW_V, RW_WD, RW_AD, RW_GD = 0, 4, 8, 12, 16, 18, 26, 34, 42, 43, 44
F_ROWS = 46 * P

VEC = {}
_at = 0
for _n, _w in (("norm1_g", KT), ("norm2_g", KT), ("final_g", KT), ("c", KT), ("c_ctx", KT), ("ada_b", 96), ("grp_g", KT),
               ("conv_w0", FT), ("conv_w1", FT), ("conv_w2", FT), ("conv_b", FT), ("q_gain", 1), ("k_gain", 1),
               ("mu_w", 1), ("mu_a", 1), ("mu_g0", 2), ("mu_g1", 2)):
    VEC[_n] = _at
    _at += _w
NVEC = _at
PV = {}
_at = 0
for _n, _w in (("mu_r", 2), ("mu_k", 2), ("mu_v", 2), ("w0", 2), ("a0", 2), ("k_k", 1), ("k_a", 1), ("r_k", 1),
               ("lnx_g", 1), ("lnx_b", 1)):
    PV[_n] = _at
    _at += _w
NPV = _at


def shape_constants():
    out = {}
    eye = np.eye(P, dtype=np.float32)
    out["ident"] = eye
    block = np.zeros((P, P), np.float32)
    block[:HD, :HD] = 1.0
    block[HD:, HD:] = 1.0
    out["head_ones"] = block
    pairs = HD // 4
    inv = np.float32(10000.0) ** (-np.arange(pairs, dtype=np.float32) / np.float32(pairs))
    t = np.arange(LAT)
    pos = np.stack([t // GRID, t % GRID]).astype(np.float32)
    cos = np.zeros((P, LAT), np.float32)
    sin = np.zeros((P, LAT), np.float32)
    swap = np.zeros((P, P), np.float32)
    for p in range(P):
        axis, half, i = (p % HD) // 32, (p % 32) // pairs, p % pairs
        ang = pos[axis] * inv[i]
        cos[p], sin[p] = np.cos(ang), np.sin(ang)
        if half == 0:
            swap[p + pairs, p] = -1.0
        else:
            swap[p - pairs, p] = 1.0
    out["rope"] = np.stack([cos, sin], 1)
    out["rope_swap"] = swap
    x = np.arange(GRID)[:, None]
    y = np.arange(GRID)[None, :]
    start = np.clip(x - NAW // 2, 0, GRID - NAW)
    inside = (y >= start) & (y < start + NAW)
    win = np.where(inside, np.float32(0.0), np.float32(-1e30)).astype(np.float32)
    out["window"] = np.concatenate([win, win], 0)
    s = np.arange(CH)[:, None]
    u = np.arange(CH)[None, :]
    masks = [(s < u), (s <= u), (s == u)]
    for lev in range(NLEV + 1):
        w = 1 << lev
        masks.append((s // (2 * w) == u // (2 * w)) & (s // w % 2 == 0) & (u // w % 2 == 1))
    upper = np.stack([m.astype(np.float32) for m in masks[:3]], 1)
    out["mask_upper"] = np.concatenate([upper, upper], 0)
    lower = np.zeros((P, NLEV + 1, P), np.float32)
    for lev, m in enumerate(masks[3:]):
        for d in range(2):
            lower[d * CH:(d + 1) * CH, lev, d * CH:(d + 1) * CH] = m.T
    out["mask_levels"] = lower
    return out


class Ctx:

    def __init__(self, nc):
        self.nc = nc
        self.held = {}

    def sb(self, stack, name, shape, dt=F32):
        return stack.enter_context(self.nc.sbuf_tensor(name, shape, dt))

    def ps(self, stack, name, shape):
        return stack.enter_context(self.nc.psum_tensor(name, shape, F32))

    def sems(self, stack, *names):
        if id(stack) not in self.held:
            self.held[id(stack)] = []
            stack.callback(self.clear_held, id(stack))
        got = [stack.enter_context(self.nc.semaphore(n)) for n in names]
        self.held[id(stack)] += got
        return got

    def clear_held(self, key):
        clear(self.nc, dict(enumerate(self.held.pop(key))))


def modulation(g, k, vec, small, ident, mod):
    nc = g.nc
    NBLK = 6 * D // 512
    QK = KT // 4
    aw = k["ada_w"].rearrange("(q p) n -> p q n", p=P)
    with ExitStack() as st:
        raw = [g.sb(st, f"ada_raw{i}", [P, 4, 512]) for i in range(4)]
        hi = [g.sb(st, f"ada_hi{i}", [P, 4, 512], F32R) for i in range(2)]
        lo = [g.sb(st, f"ada_lo{i}", [P, 4, 512], F32R) for i in range(2)]
        sig = g.sb(st, "cond_sigmoid", [P, 2 * KT])
        silu = g.sb(st, "cond_silu", [P, 2 * KT])
        cond = g.sb(st, "cond_parts", [P, KT, P], F32R)
        rows = g.sb(st, "ada_rows", [4, NBLK * 512])
        sel = g.sb(st, "sum_parts", [4, 2])
        acc = g.ps(st, "ada_acc", [P, 512])
        colp = g.ps(st, "ada_cols", [P, 2 * 96])
        sig_done, silu_done, cond_done, rows_done, col_ready, mod_done, sel_in = g.sems(
            st, "cond_sig_done", "cond_silu_done", "cond_done", "ada_rows_done", "ada_col_ready",
            "mod_done", "ada_sel_in")
        landed = g.sems(st, *[f"ada_landed{i}" for i in range(4)])
        hi_done, lo_done, used = g.sems(st, "ada_hi_done", "ada_lo_done", "ada_used")
        n_slot = NBLK * QK
        with nc.Block() as block:

            @block.sync
            def _(sp):
                sp.dma_start(sel[:], k["sum_parts"]).then_inc(sel_in, 16)
                sp.sem_inc(lo_done, 4)
                with sp.Fori(0, NBLK) as b:
                    for q in range(QK):
                        sp.wait_ge(lo_done, b * QK + (q + 1))
                        sp.dma_start(raw[q][:], aw[:, 4 * q:4 * q + 4, bass.ts(b, 512)]).then_inc(landed[q], 16)

            @block.scalar
            def _(act):
                act.activation(sig[:], vec[:, VEC["c"]:VEC["c"] + 2 * KT], ACT.Sigmoid).then_inc(sig_done, 1)
                act.wait_ge(silu_done, 2)
                for s in range(2):
                    act.copy(cond[:, :, 2 * s], silu[:, s * KT:(s + 1) * KT]).then_inc(cond_done, 1)
                with act.Fori(0, NBLK) as b:
                    for q in range(QK):
                        act.wait_ge(landed[q], b * 16 + 16)
                        act.wait_ge(used, b * QK + (q + 1))
                        act.copy(hi[q % 2][:], raw[q][:]).then_inc(hi_done, 1)

            @block.vector
            def _(dve):
                dve.memset(cond[:].bitcast(F32), 0.0).then_inc(silu_done, 1)
                dve.wait_ge(sig_done, 1)
                dve.tensor_tensor(silu[:], sig[:], vec[:, VEC["c"]:VEC["c"] + 2 * KT], ALU.mult).then_inc(silu_done, 1)
                dve.wait_ge(cond_done, 2)
                for s in range(2):
                    dve.tensor_tensor(cond[:, :, 2 * s + 1], silu[:, s * KT:(s + 1) * KT],
                                      cond[:, :, 2 * s].bitcast(F32), ALU.subtract).then_inc(cond_done, 1)
                with dve.Fori(0, NBLK) as b:
                    for q in range(QK):
                        dve.wait_ge(hi_done, b * QK + (q + 1))
                        dve.tensor_tensor(lo[q % 2][:], raw[q][:], hi[q % 2][:].bitcast(F32), ALU.subtract).then_inc(lo_done, 1)
                    dve.wait_ge(used, b * QK + (QK + 2))
                    dve.tensor_copy(rows[:, bass.ts(b, 512)], acc[0:4, :]).then_inc(rows_done, 1)
                dve.wait_ge(col_ready, 1)
                dve.tensor_tensor(mod[:, :, :], colp[:].rearrange("p (j s) -> p s j", s=2),
                                  vec[:, VEC["ada_b"]:VEC["ada_b"] + 96].unsqueeze(1).to_broadcast([P, 2, 96]),
                                  ALU.add).then_inc(mod_done, 1)

            @block.tensor
            def _(pe):
                pe.sem_inc(used, 2)
                pe.sem_inc(rows_done, 1)
                pe.wait_ge(cond_done, 4)
                with pe.Fori(0, NBLK) as b:
                    for q in range(QK):
                        if q == 0:
                            pe.wait_ge(rows_done, b + 1)
                        pe.wait_ge(lo_done, b * QK + (q + 5))
                        for j in range(4):
                            for part, w in enumerate((hi, lo)):
                                m = pe.matmul(acc[:], cond[:, 4 * q + j, :], w[q % 2][:, j, :],
                                              start=(q == 0 and j == 0 and part == 0),
                                              stop=(q == QK - 1 and j == 3 and part == 1))
                        m.then_inc(used, 1)
                pe.wait_ge(rows_done, NBLK + 1)
                pe.wait_ge(sel_in, 16)
                for j in range(96):
                    m = pe.matmul(colp[:, 2 * j:2 * j + 2], rows[:, j * P:(j + 1) * P], sel[:], start=True, stop=True)
                m.then_inc(col_ready, 1)


def load_transposed(g, src, n_pairs, dst, ident, tag):
    nc = g.nc
    with ExitStack() as st:
        rows = [g.sb(st, f"{tag}_rows{i}", [P, D]) for i in range(2)]
        tp = [g.ps(st, f"{tag}_tp{i}", [P, 4, P]) for i in range(4)]
        landed = g.sems(st, f"{tag}_landed0", f"{tag}_landed1")
        turned, (act_out, dve_out) = g.sems(st, f"{tag}_turned")[0], g.sems(st, f"{tag}_act_out", f"{tag}_dve_out")
        with nc.Block() as block:

            @block.sync
            def _(sp):
                sp.sem_inc(turned, 4 * 2)
                with sp.Fori(0, n_pairs) as i:
                    for u in range(2):
                        sp.wait_ge(turned, i * 8 + (4 * u + 4))
                        sp.dma_start(rows[u][:], src[bass.ds(i * 256 + u * P, P), :]).then_inc(landed[u], 16)

            @block.tensor
            def _(pe):
                with pe.Fori(0, n_pairs) as i:
                    for u in range(2):
                        pe.wait_ge(landed[u], i * 16 + 16)
                        for q in range(4):
                            pe.wait_ge((act_out, dve_out)[q % 2], i * 4 + (2 * u + q // 2 + 1))
                            for j in range(4):
                                m = pe.transpose(tp[q][:, j, :], rows[u][:, (4 * q + j) * P:(4 * q + j + 1) * P], ident[:])
                            m.then_inc(turned, 1)

            def copies(eng, copy, par, out):
                eng.sem_inc(out, 2)
                with eng.Fori(0, n_pairs) as i:
                    for u in range(2):
                        for q in (par, par + 2):
                            eng.wait_ge(turned, i * 8 + (4 * u + q + 9))
                            copy(dst[:, 4 * q:4 * q + 4, bass.ds(i * 256 + u * P, P)], tp[q][:]).then_inc(out, 1)

            @block.scalar
            def _(act):
                copies(act, act.copy, 0, act_out)

            @block.vector
            def _(dve):
                copies(dve, dve.tensor_copy, 1, dve_out)


def norm_split(g, src, n, ones, eps, gain, shift, hi, lo, tag, out=None):
    nc = g.nc
    with ExitStack() as st:
        sq = g.sb(st, f"{tag}_sq", [P, 2, n])
        scaled = g.sb(st, f"{tag}_scaled", [P, 2, n])
        rms = g.sb(st, f"{tag}_rms", [P, n])
        inv = g.sb(st, f"{tag}_inv", [P, n])
        acc = g.ps(st, f"{tag}_acc", [P, 512])
        sq_done, summed, rms_done, inv_done, scaled_done, hi_done, lo_done = g.sems(
            st, *[f"{tag}_{x}" for x in ("sq_done", "summed", "rms_done", "inv_done", "scaled_done", "hi_done", "lo_done")])
        with nc.Block() as block:

            @block.scalar
            def _(act):
                for k in range(KT):
                    if k >= 2:
                        act.wait_ge(summed, k - 1)
                    act.activation(sq[:, k % 2, :], src[:, k, :], ACT.Square).then_inc(sq_done, 1)
                act.wait_ge(summed, KT)
                act.activation(rms[:], acc[:, 0:n], ACT.Sqrt, bias=eps[:, 0:1], scale=1.0 / D).then_inc(rms_done, 1)
                if out is None:
                    for k in range(KT):
                        act.wait_ge(scaled_done, k + 1)
                        act.activation(hi[:, k, :], scaled[:, k % 2, :], ACT.Identity,
                                       bias=shift[:, k:k + 1]).then_inc(hi_done, 1)

            @block.tensor
            def _(pe):
                for k in range(KT):
                    pe.wait_ge(sq_done, k + 1)
                    pe.matmul(acc[:, 0:n], ones[:], sq[:, k % 2, :], start=(k == 0), stop=(k == KT - 1)).then_inc(summed, 1)

            def part(dve, k):
                dve.wait_ge(hi_done, k + 1)
                dve.scalar_tensor_tensor(lo[:, k, :], scaled[:, k % 2, :], shift[:, k:k + 1], hi[:, k, :].bitcast(F32),
                                         ALU.add, ALU.subtract).then_inc(lo_done, 1)

            @block.vector
            def _(dve):
                dve.wait_ge(rms_done, 1)
                dve.reciprocal(inv[:], rms[:]).then_inc(inv_done, 1)
                dve.wait_ge(inv_done, 1)
                for k in range(KT):
                    if out is not None:
                        dve.scalar_tensor_tensor(out[:, k, :], src[:, k, :], gain[:, k:k + 1], inv[:], ALU.mult,
                                                 ALU.mult).then_inc(scaled_done, 1)
                        continue
                    if k >= 2:
                        dve.wait_ge(lo_done, k - 1)
                    dve.scalar_tensor_tensor(scaled[:, k % 2, :], src[:, k, :], gain[:, k:k + 1], inv[:], ALU.mult,
                                             ALU.mult).then_inc(scaled_done, 1)
                    if k >= 1:
                        part(dve, k - 1)
                if out is None:
                    part(dve, KT - 1)


class WeightStream:

    def __init__(self, g, st, tag):
        self.raw = [g.sb(st, f"{tag}_raw{i}", [P, 2048]) for i in range(2)]
        self.hi = [g.sb(st, f"{tag}_whi{i}", [P, 2048], F32R) for i in range(2)]
        self.lo = [g.sb(st, f"{tag}_wlo{i}", [P, 2048], F32R) for i in range(2)]
        self.landed = g.sems(st, f"{tag}_w_landed0", f"{tag}_w_landed1")
        self.hi_done, self.lo_done, self.used = g.sems(st, f"{tag}_w_hi_done", f"{tag}_w_lo_done", f"{tag}_w_used")

    def credits(self, sp):
        sp.sem_inc(self.lo_done, 2)
        sp.sem_inc(self.used, 2)

    def load(self, sp, n, s, src):
        sp.wait_ge(self.lo_done, n + (s + 1))
        dst = self.raw[s % 2][:]
        if len(src.shape) == 3:
            dst = dst.rearrange("p (a b) -> p a b", a=src.shape[1])
        sp.dma_start(dst, src).then_inc(self.landed[s % 2], 16)

    def split_hi(self, act, half, n, s):
        act.wait_ge(self.landed[s % 2], half * 16 + (s // 2 + 1) * 16)
        act.wait_ge(self.used, n + (s + 1))
        act.copy(self.hi[s % 2][:], self.raw[s % 2][:]).then_inc(self.hi_done, 1)

    def split_lo(self, dve, n, s):
        dve.wait_ge(self.hi_done, n + (s + 1))
        dve.tensor_tensor(self.lo[s % 2][:], self.raw[s % 2][:], self.hi[s % 2][:].bitcast(F32),
                          ALU.subtract).then_inc(self.lo_done, 1)

    def ready(self, pe, n, s):
        pe.wait_ge(self.lo_done, n + (s + 3))


def three_passes(pe, out, whi, wlo, xhi, xlo, first, last):
    pe.matmul(out, whi, xhi, start=first, stop=False)
    pe.matmul(out, whi, xlo, start=False, stop=False)
    return pe.matmul(out, wlo, xhi, start=False, stop=last)


def input_projection(g, k, xhi, xlo, chi, clo, f_dram):
    nc = g.nc
    segs = [(QA, 4, False), (KA, 8, True), (QB, 4, False), (KVB, 2, True), (RW_R, 8, False), (RW_K, 18, True)]
    total = 46
    w = k["w_in"].rearrange("(k p) n -> p k n", p=P)
    with ExitStack() as st:
        ws = WeightStream(g, st, "win")
        res = [g.sb(st, f"f_tile{i}", [P, TOK]) for i in range(2)]
        lat = [g.ps(st, f"f_lat{i}", [P, 512]) for i in range(2)]
        ctx = [g.ps(st, f"f_ctx{i}", [P, 512]) for i in range(2)]
        lat_out, ctx_out = g.sems(st, "f_lat_out", "f_ctx_out")
        stored = g.sems(st, "f_stored0", "f_stored1")

        def tiles():
            base = 0
            for t0, n, both in segs:
                yield base, t0, n, both
                base += n

        with nc.Block() as block:

            @block.sync
            def _(sp):
                ws.credits(sp)
                sp.sem_inc(stored[0], 16)
                sp.sem_inc(stored[1], 16)
                sp.sem_inc(lat_out, 2)
                sp.sem_inc(ctx_out, 2)
                for base, t0, n, both in tiles():
                    with sp.Fori(0, n // 2) as i:
                        for s in range(2):
                            ws.load(sp, i * 2 + base, s, w[:, :, bass.ds(i * 2 * P + (t0 + s) * P, P)])
                for s, c0 in enumerate((44 * P, IN_COLS - P)):
                    ws.load(sp, total - 2, s, w[:, :, c0:c0 + P])
                ws.load(sp, total, 0, w[:, :, 0:P])

            def act_slot(act, i, base, s, row, both):
                ws.split_hi(act, i + base // 2, i * 2 + base, s + 1)
                act.wait_ge(ws.used, i * 2 + (base + s + 3))
                act.wait_ge(stored[s], i * 16 + (base // 2 + 1) * 16)
                act.copy(res[s][:, CTX:TOK], lat[s][:]).then_inc(lat_out, 1)
                act.wait_ge(lat_out, i * 2 + (base + s + 3))
                act.wait_ge(ctx_out, i * 2 + (base + s + 3))
                act.dma_start(f_dram[row, :], res[s][:]).then_inc(stored[s], 16)

            @block.scalar
            def _(act):
                ws.split_hi(act, 0, 0, 0)
                for base, t0, n, both in tiles():
                    with act.Fori(0, n // 2) as i:
                        for s in range(2):
                            act_slot(act, i, base, s, bass.ds(i * 2 * P + (t0 + s) * P, P), both)
                for s in range(2):
                    act_slot(act, 0, total - 2, s, bass.ds((44 + s) * P, P), False)
                for s in range(2):
                    act.wait_ge(stored[s], 16 + total // 2 * 16)

            def dve_slot(dve, i, base, s):
                ws.split_lo(dve, i * 2 + base, s + 1)
                dve.wait_ge(ws.used, i * 2 + (base + s + 3))
                dve.wait_ge(stored[s], i * 16 + (base // 2 + 1) * 16)
                return res[s][:, 0:CTX], ctx[s][:, 0:CTX]

            @block.vector
            def _(dve):
                ws.split_lo(dve, 0, 0)
                for base, t0, n, both in tiles():
                    with dve.Fori(0, n // 2) as i:
                        for s in range(2):
                            dst, src = dve_slot(dve, i, base, s)
                            if both:
                                dve.tensor_copy(dst, src).then_inc(ctx_out, 1)
                            else:
                                dve.memset(dst, 0.0).then_inc(ctx_out, 1)
                for s in range(2):
                    dst, _ = dve_slot(dve, 0, total - 2, s)
                    dve.memset(dst, 0.0).then_inc(ctx_out, 1)

            def pe_slot(pe, i, base, s, both):
                ws.ready(pe, i * 2 + base, s)
                pe.wait_ge(lat_out, i * 2 + (base + s + 1))
                if both:
                    pe.wait_ge(ctx_out, i * 2 + (base + s + 1))
                for kk in range(KT):
                    a, b = (x[s][:, kk * P:(kk + 1) * P] for x in (ws.hi, ws.lo))
                    m = three_passes(pe, lat[s][:], a, b, xhi[:, kk, :], xlo[:, kk, :], kk == 0, kk == KT - 1)
                if both:
                    for kk in range(KT):
                        a, b = (x[s][:, kk * P:(kk + 1) * P] for x in (ws.hi, ws.lo))
                        m = three_passes(pe, ctx[s][:, 0:CTX], a, b, chi[:, kk, :], clo[:, kk, :], kk == 0, kk == KT - 1)
                m.then_inc(ws.used, 1)

            @block.tensor
            def _(pe):
                for base, t0, n, both in tiles():
                    with pe.Fori(0, n // 2) as i:
                        for s in range(2):
                            pe_slot(pe, i, base, s, both)
                for s in range(2):
                    pe_slot(pe, 0, total - 2, s, False)


LAT_ALL = slice(0, LAT)
KEYS = LAT + CTX
KEY_TILES = KEYS // P
QT = LAT // P
BIAS_ROWS = 14
RPB_PAD = 64


def attention(g, k, f_dram, mix, ident, vec, eps):
    nc = g.nc
    UNITS = 4 * QT
    PIECES = [("q", 0, LAT, True), ("k", 0, LAT, True), ("k", LAT, CTX, False)]
    rpb = k["na_rpb"]
    with ExitStack() as st:
        raw = {n: g.sb(st, f"att_{n}", [P, KEYS if n[1] != "q" else LAT]) for n in ("aq", "ak", "av", "bq", "bk", "bv")}
        qs = g.sb(st, "att_aq_scaled", [P, LAT])
        bqn = g.sb(st, "att_bq_ready", [P, LAT])
        bkn = g.sb(st, "att_bk_ready", [P, KEYS])
        gains = g.sb(st, "att_gains", [P, 2])
        bias = g.sb(st, "att_bias", [P, AH, BIAS_ROWS, GRID])
        bias_now = g.sb(st, "att_bias_now", [P, 2, BIAS_ROWS, GRID])
        window = g.sb(st, "att_window", [P, GRID])
        rope = g.sb(st, "att_rope", [P, 2, LAT])
        swap = g.sb(st, "att_swap", [P, P])
        head_ones = g.sb(st, "att_head_ones", [P, P])
        sq = g.sb(st, "att_sq", [P, LAT])
        rms = g.sb(st, "att_rms", [P, LAT])
        normed = g.sb(st, "att_normed", [P, LAT])
        turned = g.sb(st, "att_turned", [P, LAT])
        vtok = [g.sb(st, f"att_{n}_tok", [P, KEY_TILES, P]) for n in "ab"]
        prob = [g.sb(st, f"att_prob{i}", [P, KEYS]) for i in range(2)]
        pt = [g.sb(st, f"att_prob_t{i}", [P, KEY_TILES, LAT]) for i in range(2)]
        mx = g.sb(st, "att_max", [P, UNITS, 2])
        nm = g.sb(st, "att_negmax", [P, UNITS])
        den = g.sb(st, "att_sum", [P, UNITS])
        rden = g.sb(st, "att_recip", [P, UNITS])
        sc = [g.ps(st, f"att_scores{i}", [P, 1024]) for i in range(2)]
        tp = g.ps(st, "att_tp", [P, 2, 512])
        outp = g.ps(st, "att_out", [P, 512])
        prep = g.ps(st, "att_prep", [P, 512])
        names = ("const_in", "bias_done", "qkv_a_in", "qkv_b_in", "qs_done", "sq_done", "ss_done", "rms_done",
                 "inv_done", "normed_done", "swapped", "turn_parts", "prep_done", "scored", "maxed", "neg_done", "exp_done",
                 "recip_done", "prob_done", "tp_done", "tp_act", "tp_dve", "pv_done", "out_copied")
        S = dict(zip(names, g.sems(st, *["att_" + n for n in names])))
        gains_done, bias_in = g.sems(st, "att_setup_done", "att_bias_in")
        with nc.Block() as block:

            @block.sync
            def _(sp):
                for dst, name in ((window, "window"), (rope, "rope"), (swap, "rope_swap"), (head_ones, "head_ones")):
                    sp.dma_start(dst[:], k[name]).then_inc(S["const_in"], 16)
                for h in range(AH):
                    for half in range(2):
                        off = RPB_PAD + h * RPB_R * RPB_C + (1 - half) * RPB_C + NAW - GRID
                        src = bass.AP(rpb.tensor, off, [[1, GRID], [RPB_C, BIAS_ROWS], [1, GRID]])
                        sp.dma_start(bias[half * HD:(half + 1) * HD, h, :, :], src).then_inc(bias_in, 16)
                sp.wait_ge(S["const_in"], 64)
                sp.wait_ge(bias_in, 16 * 2 * AH)

            @block.vector
            def _(dve):
                dve.tensor_scalar(gains[:, 0:1], vec[:, VEC["q_gain"]:VEC["q_gain"] + 1], float(HD) ** -0.5, None, ALU.mult)
                dve.tensor_copy(gains[:, 1:2], vec[:, VEC["k_gain"]:VEC["k_gain"] + 1]).then_inc(gains_done, 1)
                dve.wait_ge(gains_done, 1)

        def unit(u):
            return u // 8, u // 4 % 2, u % 4

        def keys_in(sp, dst, rows, sem, lo=0, hi=P):
            sp.dma_start(dst[lo:hi, 0:LAT], f_dram[rows, CTX:TOK]).then_inc(sem, 16)
            sp.dma_start(dst[lo:hi, LAT:KEYS], f_dram[rows, 0:CTX]).then_inc(sem, 16)

        with nc.Fori(0, 4) as i:
            with nc.Block() as block:

                @block.sync
                def _(sp):
                    sem = S["qkv_a_in"]
                    sp.dma_start(raw["aq"][:], f_dram[bass.ds(i * P + QA * P, P), CTX:TOK]).then_inc(sem, 16)
                    keys_in(sp, raw["ak"], bass.ds(i * P + KA * P, P), sem)
                    keys_in(sp, raw["av"], bass.ds(i * P + VA * P, P), sem)
                    sem = S["qkv_b_in"]
                    sp.dma_start(raw["bq"][:], f_dram[bass.ds(i * P + QB * P, P), CTX:TOK]).then_inc(sem, 16)
                    for half in range(2):
                        kv = (i // 2) * HD
                        keys_in(sp, raw["bk"], bass.ds(kv + KVB * P, HD), sem, half * HD, half * HD + HD)
                        keys_in(sp, raw["bv"], bass.ds(kv + (KVB + 1) * P, HD), sem, half * HD, half * HD + HD)

                @block.gpsimd
                def _(pool):
                    for hh in range(2):
                        table = bias[:, bass.ds(i * 2 + hh, 1), :, :].rearrange("p o a b -> p (o a) b")
                        pool.tensor_tensor(flip(bias_now[:, hh, :, :]), table,
                                           flip(window[:].unsqueeze(1).to_broadcast([P, BIAS_ROWS, GRID])),
                                           ALU.add).then_inc(S["bias_done"], 1)

                def scores(pe, u):
                    grp, hh, t = unit(u)
                    if u == 0:
                        pe.wait_ge(S["qs_done"], 1)
                    if u == 8:
                        pe.wait_ge(S["prep_done"], 3)
                    if u >= 2:
                        pe.wait_ge(S["exp_done"], u - 1)
                    q, kk = ((qs, raw["ak"]), (bqn, bkn))[grp]
                    hp = slice(hh * HD, hh * HD + HD)
                    pe.matmul(sc[u % 2][:, 0:LAT], q[hp, t * P:(t + 1) * P], kk[hp, 0:LAT], start=True, stop=True)
                    pe.matmul(sc[u % 2][:, LAT:KEYS], q[hp, t * P:(t + 1) * P], kk[hp, LAT:KEYS], start=True,
                              stop=True).then_inc(S["scored"], 1)

                def turn(pe, j, src):
                    if j >= 1:
                        pe.wait_ge(S["tp_act"], j)
                        pe.wait_ge(S["tp_dve"], j)
                    for b in range(KEY_TILES):
                        m = pe.transpose(tp[:, b // 3, b % 3 * P:(b % 3 + 1) * P], src[:, b * P:(b + 1) * P], ident[:])
                    m.then_inc(S["tp_done"], 1)

                def weigh(pe, head):
                    grp, hh = head // 2, head % 2
                    hp = slice(hh * HD, hh * HD + HD)
                    pe.wait_ge(S["tp_act"], 2 + 4 * head + 4)
                    pe.wait_ge(S["tp_dve"], 2 + 4 * head + 4)
                    if head == 2:
                        pe.wait_ge(S["out_copied"], 1)
                    for b in range(KEY_TILES):
                        m = pe.matmul(outp[hp, :], vtok[grp][:, b, hp], pt[head % 2][:, b, :], start=(b == 0),
                                      stop=(b == KEY_TILES - 1))
                    m.then_inc(S["pv_done"], 1)

                def prep_pe(pe, u):
                    if u % 2 == 1 and u // 2 < 3:
                        _, _, n, _ = PIECES[u // 2]
                        pe.wait_ge(S["sq_done"], u // 2 + 1)
                        if u > 1:
                            pe.wait_ge(S["prep_done"], u // 2)
                        pe.matmul(prep[:, 0:n], head_ones[:], sq[:, 0:n], start=True, stop=True).then_inc(S["ss_done"], 1)
                    if u % 2 == 0 and 0 < u // 2 <= 3 and PIECES[u // 2 - 1][3]:
                        pe.wait_ge(S["normed_done"], u // 2)
                        pe.matmul(prep[:, :], swap[:], normed[:], start=True, stop=True).then_inc(S["swapped"], 1)

                @block.tensor
                def _(pe):
                    pe.wait_ge(S["qkv_a_in"], 80)
                    turn(pe, 0, raw["av"])
                    pe.wait_ge(S["qkv_b_in"], 144)
                    turn(pe, 1, raw["bv"])
                    scores(pe, 0)
                    scores(pe, 1)
                    for u in range(UNITS):
                        prep_pe(pe, u)
                        pe.wait_ge(S["prob_done"], u + 1)
                        turn(pe, u + 2, prob[u % 2])
                        if u + 2 < UNITS:
                            scores(pe, u + 2)
                        if u % 4 == 0 and u:
                            weigh(pe, u // 4 - 1)
                    weigh(pe, 3)

                @block.scalar
                def _(act):
                    act.wait_ge(S["qkv_a_in"], 80)
                    act.mul(qs[:], raw["aq"][:], float(HD) ** -0.5).then_inc(S["qs_done"], 1)

                    def copy_out(j):
                        act.wait_ge(S["tp_done"], j + 1)
                        if j < 2:
                            dst = vtok[j][:, 0:3, :]
                        else:
                            head, t = (j - 2) // 4, (j - 2) % 4
                            if head >= 2 and t == 0:
                                act.wait_ge(S["pv_done"], head - 1)
                            dst = pt[head % 2][:, 0:3, t * P:(t + 1) * P]
                        act.copy(dst, tp[:, 0, 0:3 * P].rearrange("p (a b) -> p a b", a=3)).then_inc(S["tp_act"], 1)

                    copy_out(0)
                    copy_out(1)
                    for u in range(UNITS):
                        act.wait_ge(S["neg_done"], u + 1)
                        if u >= 2:
                            act.wait_ge(S["tp_done"], u + 1)
                        act.activation(prob[u % 2][:], sc[u % 2][:, 0:KEYS], ACT.Exp, bias=nm[:, u:u + 1],
                                       accum_out=den[:, u:u + 1]).then_inc(S["exp_done"], 1)
                        if u >= 1:
                            copy_out(u + 1)
                        j = u // 2
                        if u % 2 == 0 and j < 3:
                            name, c0, n, _ = PIECES[j]
                            if j == 0:
                                act.wait_ge(S["qkv_b_in"], 144)
                            act.activation(sq[:, 0:n], raw["b" + name][:, c0:c0 + n], ACT.Square).then_inc(S["sq_done"], 1)
                        if u % 2 == 1 and j < 3:
                            n = PIECES[j][2]
                            act.wait_ge(S["ss_done"], j + 1)
                            act.activation(rms[:, 0:n], prep[:, 0:n], ACT.Sqrt, bias=eps[:, 0:1],
                                           scale=1.0 / HD).then_inc(S["rms_done"], 1)
                    copy_out(UNITS + 1)

                @block.vector
                def _(dve):
                    def copy_out(j):
                        dve.wait_ge(S["tp_done"], j + 1)
                        if j < 2:
                            dst = vtok[j][:, 3:6, :]
                        else:
                            head, t = (j - 2) // 4, (j - 2) % 4
                            if head >= 2 and t == 0:
                                dve.wait_ge(S["pv_done"], head - 1)
                            dst = pt[head % 2][:, 3:6, t * P:(t + 1) * P]
                        dve.tensor_copy(dst, tp[:, 1, 0:3 * P].rearrange("p (a b) -> p a b", a=3)).then_inc(S["tp_dve"], 1)

                    def maximum(u):
                        grp, hh, t = unit(u)
                        dve.wait_ge(S["scored"], u + 1)
                        if grp == 0:
                            if u == 0:
                                dve.wait_ge(S["bias_done"], 2)
                            s = sc[u % 2][:, 0:LAT]
                            b = bias_now[:, hh, 6 - 2 * t:14 - 2 * t, :].rearrange("p a b -> p (a b)")
                            dve.tensor_tensor_reduce(out=s, in0=s, in1=b, scale=1.0, scalar=-3e38, op0=ALU.add, op1=ALU.max,
                                                     accum_out=mx[:, u, 0:1]).then_inc(S["maxed"], 1)
                            dve.reduce_max(mx[:, u, 1:2], sc[u % 2][:, LAT:KEYS], AX_X).then_inc(S["maxed"], 1)
                            dve.wait_ge(S["maxed"], 2 * u + 2)
                            dve.tensor_reduce(nm[:, u:u + 1], mx[:, u, :], AX_X, ALU.max, negate=True).then_inc(S["neg_done"], 1)
                        else:
                            dve.tensor_reduce(nm[:, u:u + 1], sc[u % 2][:, 0:KEYS], AX_X, ALU.max,
                                              negate=True).then_inc(S["neg_done"], 1)

                    def divide(u):
                        dve.wait_ge(S["exp_done"], u + 1)
                        dve.reciprocal(rden[:, u:u + 1], den[:, u:u + 1]).then_inc(S["recip_done"], 1)
                        dve.wait_ge(S["recip_done"], u + 1)
                        dve.tensor_scalar(prob[u % 2][:], prob[u % 2][:], rden[:, u:u + 1], None, ALU.mult).then_inc(S["prob_done"], 1)

                    def prep_dve(u):
                        j = u // 2
                        if u % 2 == 1 and j < 3:
                            name, c0, n, turned_too = PIECES[j]
                            dve.wait_ge(S["rms_done"], j + 1)
                            if j:
                                dve.wait_ge(S["prep_done"], j)
                            dve.reciprocal(sq[:, 0:n], rms[:, 0:n]).then_inc(S["inv_done"], 1)
                            dve.wait_ge(S["inv_done"], j + 1)
                            dst = normed[:, 0:n] if turned_too else bkn[:, c0:c0 + n]
                            gcol = 0 if name == "q" else 1
                            dve.scalar_tensor_tensor(dst, raw["b" + name][:, c0:c0 + n], gains[:, gcol:gcol + 1], sq[:, 0:n],
                                                     ALU.mult, ALU.mult).then_inc(S["normed_done" if turned_too else "prep_done"], 1)
                        j = u // 2 - 1
                        if u % 2 == 0 and 0 <= j < 3 and PIECES[j][3]:
                            dst = (bqn if PIECES[j][0] == "q" else bkn)[:, 0:LAT]
                            dve.wait_ge(S["normed_done"], j + 1)
                            dve.tensor_tensor(dst, normed[:], rope[:, 0, :], ALU.mult).then_inc(S["turn_parts"], 1)
                            dve.wait_ge(S["swapped"], j + 1)
                            dve.tensor_tensor(turned[:], prep[:, :], rope[:, 1, :], ALU.mult).then_inc(S["turn_parts"], 1)
                            dve.wait_ge(S["turn_parts"], 2 * j + 2)
                            dve.tensor_tensor(dst, dst, turned[:], ALU.add).then_inc(S["prep_done"], 1)

                    def copy_result(grp):
                        dve.wait_ge(S["pv_done"], 2 * grp + 2)
                        dve.tensor_copy(mix[:, bass.ds(i + 4 * grp, 1), :].rearrange("p a n -> p (a n)"),
                                        outp[:]).then_inc(S["out_copied"], 1)

                    copy_out(0)
                    copy_out(1)
                    for u in range(UNITS + 1):
                        if u < UNITS:
                            maximum(u)
                        if u >= 1:
                            divide(u - 1)
                        if u >= 2:
                            copy_out(u)
                        if u == 10:
                            copy_result(0)
                        prep_dve(u)
                    copy_out(UNITS + 1)
                    copy_result(1)
                    dve.wait_ge(S["out_copied"], 2)

            clear(nc, S)


CHUNKS = TOK // CH
DECAY = float(np.exp(-0.5))
SL_B, SL_K, SL_BH, SL_KH, SL_A, SL_V = ((0, 0), (0, 1), (1, 0), (1, 1), (2, 0), (2, 1))


def rwkv_lora(g, st, k, f_dram, vec):
    nc = g.nc
    tw = g.sb(st, "rw_tanh_wd", [P, TOK])
    ta = g.sb(st, "rw_ad", [P, TOK])
    sg = g.sb(st, "rw_sig_gd", [P, 2, LAT])
    with ExitStack() as s2:
        pad = [g.sb(s2, f"rw_pad{j}", [P, TOK + 3]) for j in range(4)]
        mixed = g.sb(s2, "rw_mixed", [P, 4, TOK])
        om = g.sb(s2, "rw_one_minus_mu", [P, 4])
        sems = g.sems(s2, "lora_in", "lora_padded", "lora_dve", "lora_scaled", "lora_mixed")
        came, padded, link_sem, scaled, mixed_done = sems
        c1 = slice(1, CTX + 1)
        l1 = slice(CTX + 2, TOK + 2)
        with nc.Block() as block:

            @block.sync
            def _(sp):
                sp.wait_ge(padded, 4)
                for j, t in enumerate((RW_WD, RW_AD)):
                    sp.dma_start(pad[j][:, c1], f_dram[t * P:(t + 1) * P, 0:CTX]).then_inc(came, 16)
                    sp.dma_start(pad[j][:, l1], f_dram[t * P:(t + 1) * P, CTX:TOK]).then_inc(came, 16)
                sp.dma_start(pad[2][:, l1], f_dram[RW_GD * P:(RW_GD + 1) * P, CTX:TOK]).then_inc(came, 16)
                sp.dma_start(pad[3][0:32, l1], f_dram[(RW_GD + 1) * P + 96:(RW_GD + 2) * P, CTX:TOK]).then_inc(came, 16)

            @block.gpsimd
            def _(pool):
                for j in range(4):
                    pool.memset(pad[j][:], 0.0).then_inc(padded, 1)

            @block.vector
            def _(dve):
                link = Link(dve, link_sem)
                mu = vec[:, VEC["mu_w"]:VEC["mu_w"] + 2]
                dve.tensor_scalar(om[:, 0:2], mu, -1.0, 1.0, ALU.mult, ALU.add)
                g0, g1 = vec[:, VEC["mu_g0"]:VEC["mu_g0"] + 2], vec[:, VEC["mu_g1"]:VEC["mu_g1"] + 2]
                link(dve.tensor_tensor(om[:, 2:4], g0, g1, ALU.add))
                link(dve.tensor_scalar(om[:, 2:4], om[:, 2:4], -1.0, 1.0, ALU.mult, ALU.add))
                dve.wait_ge(came, 16 * 6)
                for j in range(2):
                    m = vec[:, VEC["mu_w"] + j:VEC["mu_w"] + j + 1]
                    for sl, o in ((c1, slice(0, CTX)), (l1, slice(CTX, TOK))):
                        link(dve.tensor_scalar(mixed[:, j, o], pad[j][:, sl], om[:, j:j + 1], None, ALU.mult))
                        for half, step in ((0, -1), (1, 1)):
                            hp = slice(half * HD, half * HD + HD)
                            nb = pad[j][hp, sl.start + step:sl.stop + step]
                            link(dve.scalar_tensor_tensor(mixed[hp, j, o], nb, m[hp], mixed[hp, j, o], ALU.mult, ALU.add))
                for j in (2, 3):
                    link(dve.tensor_scalar(mixed[:, j, 0:LAT], pad[j][:, l1], om[:, j:j + 1], None, ALU.mult))
                    for name, step in (("mu_g0", -1), ("mu_g1", 1)):
                        m = vec[:, VEC[name] + j - 2:VEC[name] + j - 1]
                        link(dve.scalar_tensor_tensor(mixed[:, j, 0:LAT], pad[j][:, l1.start + step:l1.stop + step], m,
                                                      mixed[:, j, 0:LAT], ALU.mult, ALU.add))
                dve.nop().then_inc(mixed_done, 1)

            @block.scalar
            def _(act):
                act.wait_ge(mixed_done, 1)
                for dst, j, fn in ((tw, 0, ACT.Tanh), (ta, 1, ACT.Copy)):
                    act.activation(dst[0:HD, :], mixed[0:HD, j, :], fn)
                    for o in (slice(0, CTX), slice(CTX, TOK)):
                        act.activation(flip(dst[HD:P, o]), mixed[HD:P, j, o], fn)
                for j in (0, 1):
                    act.activation(sg[:, j, :], mixed[:, 2 + j, 0:LAT], ACT.Sigmoid)

    return tw, ta, sg


def flip(ap):
    return ap[tuple([slice(None)] * (len(ap.shape) - 1) + [slice(None, None, -1)])]


class Link:

    def __init__(self, eng, sem):
        self.eng, self.sem, self.n = eng, sem, 0

    def __call__(self, ins):
        self.n += 1
        ins.then_inc(self.sem, 1)
        self.eng.wait_ge(self.sem, self.n)


def rwkv(g, k, f_dram, mix, ident, vec, eps):
    nc = g.nc
    with ExitStack() as st:
        tw, ta, sg = rwkv_lora(g, st, k, f_dram, vec)
        upper = g.sb(st, "rw_upper", [P, 3, CH])
        diag2 = upper[:, 2, :]
        levels = g.sb(st, "rw_levels", [P, NLEV + 1, P])
        head_ones = g.sb(st, "rw_head_ones", [P, P])
        zeros = g.sb(st, "rw_zeros", [P, CH])
        lnx_eps = g.sb(st, "rw_lnx_eps", [P, 1])
        raw = g.sb(st, "rw_raw", [P, 3, TOK + 3])
        pv = g.sb(st, "rw_pair_vec", [P, NPV])
        om = g.sb(st, "rw_pair_om", [P, 7])
        w2 = g.sb(st, "rw_w2_pair", [P, 2, P])
        g2 = g.sb(st, "rw_g2_pair", [P, 2, P])
        stacks = [[g.sb(st, f"rw_{n}{d}", [P, CHUNKS, 2, CH]) for n in ("b_k", "bh_kh", "a_v")] for d in range(2)]
        AR = [g.sb(st, f"rw_a_r{d}", [P, CHUNKS, 2, 2, CH]) for d in range(2)]
        R = [g.sb(st, f"rw_r{d}", [P, CHUNKS, CH]) for d in range(2)]
        wd = [g.sb(st, f"rw_decay{d}", [P, CHUNKS, CH]) for d in range(2)]
        aa = [g.sb(st, f"rw_iclr{d}", [P, TOK]) for d in range(2)]
        cum = [g.sb(st, f"rw_cum{d}", [P, CHUNKS, CH + 1]) for d in range(2)]
        bonus = g.sb(st, "rw_bonus", [P, LAT])
        ysum = g.sb(st, "rw_y", [P, LAT])
        tmp = g.sb(st, "rw_tmp", [P, LAT])
        Em = [g.sb(st, f"rw_pairs{d}", [P, CPB, 2, 2, CH]) for d in range(2)]
        BK = [g.sb(st, f"rw_bk_tok{d}", [P, CPB, P]) for d in range(2)]
        UV = [g.sb(st, f"rw_uv_tok{d}", [P, CPB, P]) for d in range(2)]
        Ms = [g.sb(st, f"rw_m{h}", [P, CPB, CH]) for h in range(2)]
        Ml = [[buf[:, 0:CPB * P].rearrange("p (c n) -> p c n", n=P) for buf in (wd[h][:].rearrange("p c n -> p (c n)"), aa[h][:])]
              for h in range(2)]
        X = [g.sb(st, f"rw_inverse{h}", [P, CPB, P]) for h in range(2)]
        T = [g.sb(st, f"rw_inverse_turned{h}", [P, CPB, P]) for h in range(2)]
        Y1 = [g.sb(st, f"rw_half{h}", [P, CPB, P]) for h in range(2)]
        AM = [g.sb(st, f"rw_a_mv_tok{h}", [P, CPB, P]) for h in range(2)]
        Wt = [g.sb(st, f"rw_w_tok{h}", [P, CPB, CH]) for h in range(2)]
        Gt = [g.sb(st, f"rw_g{d}", [P, CPB, CH]) for d in range(2)]
        Dg = [g.sb(st, f"rw_diag{d}", [P, CPB, CH]) for d in range(2)]
        Qt = [g.sb(st, f"rw_q{d}", [P, CPB, CH]) for d in range(2)]
        St = [g.sb(st, f"rw_state{d}", [P, CHUNKS, CH]) for d in range(2)]
        bank = [g.ps(st, f"rw_ps{j}", [P, 1024]) for j in range(4)]

        def bk(i, j):
            return bank[i][:, j * 512:j * 512 + 512]

        kinds = ("raw_in", "pair_in", "om_done", "scaled", "mixed", "gates", "sig_done", "exp_done", "sqk_done", "ss_done",
                 "ssqrt_done", "rk_done", "rk_sum", "feat_link", "feat_done", "pool_link", "seed_link",
                 "mean_done", "cent_done", "csq_done", "var_done", "std_done", "gate_done", "mixed_out", "read_link")
        S = {n: g.sems(st, "rw_" + n)[0] for n in kinds}
        per_dir = ("e_done", "e_out", "turned", "turned_out", "diag", "gq_done", "gq_out", "state_done", "state_out",
                   "y_done", "y_out", "r_done")
        per_head = ("m_done", "m_out", "mv_done", "mv_out", "seeded", "turned_x", "levels", "half_done", "half_out",
                    "join_done", "joined", "wu_done", "wu_out")
        SD = [{n: g.sems(st, f"rw_{n}{d}")[0] for n in per_dir} for d in range(2)]
        SG = [{n: g.sems(st, f"rw_{n}_h{h}")[0] for n in per_head} for h in range(2)]

        with nc.Block() as block:

            @block.sync
            def _(sp):
                for dst, name in ((upper, "mask_upper"), (levels, "mask_levels"), (head_ones, "head_ones")):
                    sp.dma_start(dst[:], k[name]).then_inc(S["raw_in"], 16)
                sp.wait_ge(S["raw_in"], 48)

            @block.vector
            def _(dve):
                dve.memset(zeros[:], 0.0)
                dve.memset(lnx_eps[:], LNX_EPS)
                dve.memset(raw[:], 0.0)
                dve.memset(g2[:], 0.0)
                for d in range(2):
                    dve.memset(AR[d][:], 0.0)
                    dve.memset(cum[d][:], 1.0)

        clear(nc, {"raw_in": S["raw_in"]})

        with nc.Fori(0, PAIRS) as p:
            pair_features(g, k, p, locals())
            pair_chunks(g, locals())
            pair_readout(g, p, mix, locals())
            clear(nc, {**S, **{f"{n}{d}": s for d in range(2) for n, s in [*SD[d].items(), *SG[d].items()]}})


def pair_features(g, k, p, L):
    nc = g.nc
    S, SD, stacks, AR, R, wd, aa, cum, raw, pv, om, w2, g2 = (L[n] for n in ("S", "SD", "stacks", "AR", "R", "wd", "aa", "cum", "raw", "pv", "om", "w2", "g2"))
    tw, ta, sg, bonus, ysum, tmp, zeros, head_ones, bk, bank, f_dram = (
        L[n] for n in ("tw", "ta", "sg", "bonus", "ysum", "tmp", "zeros", "head_ones", "bk", "bank", "f_dram"))
    c1, l1 = slice(1, CTX + 1), slice(CTX + 2, TOK + 2)
    lat = slice(CTX // CH, CHUNKS)
    cols = ((c1, slice(0, CTX // CH)), (l1, lat))
    full = slice(0, CHUNKS)
    arr = lambda d, s, c=full: R[d][:, c, :] if s is None else stacks[d][s[0]][:, c, s[1] ^ d, :]
    chunks = lambda ap: ap.rearrange("p (c n) -> p c n", n=CH)
    col = lambda n, d=0: pv[:, PV[n] + d:PV[n] + d + 1]
    RKV = (None, SL_K, SL_V)
    with nc.Block() as block:

        @block.sync
        def _(sp):
            for j, t in enumerate((RW_K, RW_V, RW_R)):
                slot = (1, 2, 0)[j]
                sp.dma_start(raw[:, slot, c1], f_dram[bass.ds(p * P + t * P, P), 0:CTX]).then_inc(S["raw_in"], 16)
                sp.dma_start(raw[:, slot, l1], f_dram[bass.ds(p * P + t * P, P), CTX:TOK]).then_inc(S["raw_in"], 16)

        @block.scalar
        def _(act):
            act.dma_start(pv[:], k["pair_vectors"][bass.ds(p, 1)].rearrange("a p n -> (a p) n")).then_inc(S["pair_in"], 16)
            act.dma_start(w2[:, 0, :], k["rw_w2"][:, bass.ts(p, P)]).then_inc(S["pair_in"], 16)
            act.dma_start(w2[:, 1, :], k["rw_a2"][:, bass.ts(p, P)]).then_inc(S["pair_in"], 16)
            act.dma_start(g2[:, 0, :], k["rw_g2"][0:P, bass.ts(p, P)]).then_inc(S["pair_in"], 16)
            act.dma_start(g2[0:32, 1, :], k["rw_g2"][P:GLORA, bass.ts(p, P)]).then_inc(S["pair_in"], 16)
            act.wait_ge(S["raw_in"], 96)
            act.wait_ge(S["om_done"], 1)
            for j in (1, 2, 0):
                for d in range(2):
                    for src, dst in cols:
                        x = raw[:, j, src]
                        act.activation(arr(d, RKV[j], dst), chunks(flip(x) if d else x), ACT.Copy,
                                       scale=om[:, 2 * j + d:2 * j + d + 1]).then_inc(S["scaled"], 1)
            for d in range(2):
                act.wait_ge(S["mixed"], 2 * d + 2)
                act.activation(arr(d, SL_A), arr(d, SL_K), ACT.Square, scale=col("k_k")).then_inc(S["sqk_done"], 1)
            for d in range(2):
                act.wait_ge(S["gates"], 2 * d + 1)
                act.activation(wd[d][:].rearrange("p c n -> p (c n)"), bank[2 * d][:, 0:TOK], ACT.Sigmoid,
                               bias=col("w0", d)).then_inc(S["sig_done"], 1)
                act.wait_ge(S["gates"], 2 * d + 2)
                act.activation(aa[d][:], bank[2 * d + 1][:, 0:TOK], ACT.Sigmoid, bias=col("a0", d)).then_inc(S["sig_done"], 1)
            for d in range(2):
                act.wait_ge(S["ss_done"], d + 1)
                act.activation(arr(d, SL_B), chunks(bank[2 * d][:, 0:TOK]), ACT.Sqrt).then_inc(S["ssqrt_done"], 1)
            act.wait_ge(S["sig_done"], 4)
            for d in range(2):
                act.activation(wd[d][:], wd[d][:], ACT.Exp, scale=-DECAY).then_inc(S["exp_done"], 1)
            for d in range(2):
                act.wait_ge(S["feat_done"], 3 * d + 2)
                for h in range(2):
                    hp = slice(h * HD, h * HD + HD)
                    act.copy(AR[d][hp, :, h, 0, :], arr(d, SL_A)[hp])
                act.wait_ge(SD[d]["r_done"], 1)
                for h in range(2):
                    hp = slice(h * HD, h * HD + HD)
                    act.copy(AR[d][hp, lat, h, 1, :], R[d][hp, lat, :])

        @block.tensor
        def _(pe):
            pe.wait_ge(S["pair_in"], 80)
            for d in range(2):
                hp = slice(d * HD, d * HD + HD)
                for j, src in enumerate((tw, ta)):
                    pe.matmul(bank[2 * d + j][:, 0:512], w2[hp, j, :], src[hp, 0:512], start=True, stop=True)
                    pe.matmul(bank[2 * d + j][:, 512:TOK], w2[hp, j, :], src[hp, 512:TOK], start=True, stop=True).then_inc(S["gates"], 1)
            for d in range(2):
                pe.wait_ge(S["sqk_done"], d + 1)
                pe.wait_ge(S["sig_done"], 2 * d + 1)
                pe.matmul(bank[2 * d][:, 0:512], head_ones[:], arr(d, SL_A, slice(0, 8)), start=True, stop=True)
                pe.matmul(bank[2 * d][:, 512:TOK], head_ones[:], arr(d, SL_A, slice(8, CHUNKS)), start=True,
                          stop=True).then_inc(S["ss_done"], 1)
            for d in range(2):
                pe.wait_ge(S["rk_done"], d + 1)
                pe.wait_ge(S["sig_done"], 2 * d + 2)
                pe.matmul(bank[2 * d + 1][:, 0:512], head_ones[:], arr(d, SL_KH, lat), start=True,
                          stop=True).then_inc(S["rk_sum"], 1)

        @block.gpsimd
        def _(pool):
            link = Link(pool, S["pool_link"])
            link(pool.memset(ysum[:], 0.0))
            for d in range(2):
                pool.wait_ge(S["feat_done"], 3 * d + 1)
                pool.tensor_tensor(arr(d, None, lat), arr(d, None, lat), cum[d][:, lat, 1:CH + 1], ALU.mult).then_inc(SD[d]["r_done"], 1)
                last = cum[d][:, :, CH:CH + 1].to_broadcast([P, CHUNKS, CH])
                pool.wait_ge(S["feat_done"], 3 * d + 2)
                pool.tensor_tensor(arr(d, SL_BH), arr(d, SL_B), last, ALU.mult)
                pool.wait_ge(S["feat_done"], 3 * d + 3)
                pool.tensor_tensor(arr(d, SL_KH), arr(d, SL_K), last, ALU.mult)

        @block.vector
        def _(dve):
            link = Link(dve, S["feat_link"])
            dve.wait_ge(S["pair_in"], 80)
            dve.tensor_scalar(om[:, 6:7], col("k_a"), -1.0, 1.0, ALU.mult, ALU.add)
            dve.tensor_scalar(om[:, 0:6], pv[:, 0:6], -1.0, 1.0, ALU.mult, ALU.add).then_inc(S["om_done"], 1)
            dve.wait_ge(S["om_done"], 1)
            n = 0
            for j in (1, 2, 0):
                for d in range(2):
                    for src, dst in cols:
                        n += 1
                        step = 1 if d else -1
                        x = raw[:, j, src.start + step:src.stop + step]
                        dve.wait_ge(S["scaled"], n)
                        y = arr(d, RKV[j], dst)
                        dve.scalar_tensor_tensor(y, chunks(flip(x) if d else x), pv[:, 2 * j + d:2 * j + d + 1], y, ALU.mult, ALU.add).then_inc(S["mixed"], 1)
            dve.wait_ge(S["mixed"], 12)
            for d in range(2):
                f3 = lambda s: arr(d, s)
                dve.wait_ge(S["ssqrt_done"], d + 1)
                link(dve.tensor_scalar(arr(d, SL_B), arr(d, SL_B), 1e-12, None, ALU.max))
                link(dve.reciprocal(arr(d, SL_B), arr(d, SL_B)))
                link(dve.scalar_tensor_tensor(arr(d, SL_A), arr(d, SL_K), col("k_k"), arr(d, SL_B), ALU.mult, ALU.mult))
                dve.wait_ge(S["sig_done"], 2 * d + 2)
                link(dve.tensor_tensor(arr(d, SL_B), arr(d, SL_A), chunks(aa[d][:]), ALU.mult))
                link(dve.tensor_scalar(aa[d][:], aa[d][:], col("k_a"), om[:, 6:7], ALU.mult, ALU.add))
                link(dve.tensor_tensor(arr(d, SL_K), arr(d, SL_K), chunks(aa[d][:]), ALU.mult))
                dve.scalar_tensor_tensor(arr(d, SL_KH, lat), arr(d, None, lat), col("r_k"),
                                         arr(d, SL_K, lat), ALU.mult, ALU.mult).then_inc(S["rk_done"], 1)
                dve.wait_ge(S["exp_done"], d + 1)
                for c in range(CHUNKS):
                    m = dve.tensor_tensor_scan(cum[d][:, c, 1:CH + 1], wd[d][:, c, :], zeros[:], 1.0, ALU.mult, ALU.add)
                link(m)
                dve.wait_ge(S["rk_sum"], d + 1)
                bon = bonus if d == 0 else tmp
                dve.tensor_tensor(chunks(bon[:]), chunks(bank[2 * d + 1][:, 0:512]), arr(d, SL_V, lat), ALU.mult).then_inc(S["feat_done"], 1)
                dve.scalar_tensor_tensor(f3(SL_A), f3(SL_A), -1.0, cum[d][:, :, 0:CH], ALU.mult, ALU.mult)
                link(dve.reciprocal(wd[d][:], cum[d][:, :, 1:CH + 1]))
                dve.tensor_tensor(f3(SL_B), f3(SL_B), wd[d][:], ALU.mult).then_inc(S["feat_done"], 1)
                dve.tensor_tensor(f3(SL_K), f3(SL_K), wd[d][:], ALU.mult).then_inc(S["feat_done"], 1)
            dve.wait_ge(S["feat_done"], 6)
            dve.tensor_tensor(bonus[:], bonus[:], flip(tmp[:]), ALU.add)


def pair_chunks(g, L):
    nc = g.nc
    S, SD, SG, stacks, AR, R, cum, Em, BK, UV, Ms, Ml, X, T, Y1, AM, Wt, Gt, Dg, Qt, St = (
        L[n] for n in ("S", "SD", "SG", "stacks", "AR", "R", "cum", "Em", "BK", "UV", "Ms", "Ml", "X", "T", "Y1", "AM", "Wt", "Gt", "Dg",
                       "Qt", "St"))
    bk, bank, upper, levels, diag2, ident, ysum = (L[n] for n in ("bk", "bank", "upper", "levels", "diag2", "ident", "ysum"))
    HP = [slice(0, HD), slice(HD, P)]
    OWN, OTH = HP, [HP[1], HP[0]]
    flat = lambda ap: ap.rearrange("p c n -> p (c n)")

    def quarter(ap, c, n=CH):
        return ap[:, c * n:(c + 1) * n]

    def stacked(d, b, c, j):
        return stacks[d][j][:, b * CPB + c, :, :].rearrange("p a n -> p (a n)")

    def arr(d, s, b, c, h):
        return stacks[d][s[0]][HP[h], b * CPB + c, s[1] ^ d, :]

    def lanes(h):
        return slice(h * CH, (h + 1) * CH)

    def wu_out(eng, copy, b, h):
        s = SG[h]
        eng.wait_ge(s["wu_done"], b + 1)
        wu = bk(2, h).rearrange("p (c a n) -> p c a n", c=CPB, a=2)
        copy(Wt[h][:], wu[:, :, 0, :])
        for d in range(2):
            m = copy(UV[d][OWN[d], :, lanes(h)], wu[OWN[d], :, 1, :])
        m.then_inc(s["wu_out"], 1)

    with nc.Block() as block:

        @block.tensor
        def _(pe):
            for b in range(NB):
                lat = b > 0
                for d in range(2):
                    s = SD[d]
                    if b:
                        pe.wait_ge(SG[d]["wu_out"], b)
                        pe.wait_ge(SG[1 - d]["wu_out"], b)
                        pe.wait_ge(s["gq_out"], b)
                    for j in (1, 2):
                        for c in range(CPB):
                            m = pe.transpose(bk(2 + d, j - 1)[:, c * P:(c + 1) * P], stacked(d, b, c, j), ident[:])
                    m.then_inc(s["turned"], 1)
                for d in range(2):
                    s = SD[d]
                    if b:
                        for e in range(2):
                            pe.wait_ge(SD[e]["state_out"], CPB * b)
                            if b > 1:
                                pe.wait_ge(SD[e]["y_out"], b - 1)
                    for c in range(CPB):
                        rhs = AR[d][:, b * CPB + c, :, :, :] if lat else AR[d][:, b * CPB + c, :, 0, :]
                        n = 2 * P if lat else P
                        m = pe.matmul(bank[d][:, c * n:(c + 1) * n], stacked(d, b, c, 0), rhs, start=True, stop=True)
                    m.then_inc(s["e_done"], 1)
                pe.wait_ge(SD[0]["e_out"], b + 1)
                for h in range(2):
                    for c in range(CPB):
                        for d in range(2):
                            m = pe.matmul(quarter(bk(0, h), c)[OWN[d]], arr(d, SL_A, b, c, h), arr(d, SL_B, b, c, h), start=True, stop=True)
                    m.then_inc(SG[h]["m_done"], 1)
                pe.wait_ge(SD[1]["e_out"], b + 1)
                for d in range(2):
                    pe.wait_ge(SD[d]["turned_out"], b + 1)
                for h in range(2):
                    for c in range(CPB):
                        for d in range(2):
                            m = pe.matmul(quarter(bk(1, h), c)[OWN[d]], Em[d][OTH[d], c, h, 0, :], UV[d][OTH[d], c, lanes(h)],
                                          start=True, stop=True)
                    m.then_inc(SG[h]["mv_done"], 1)
                for lev in range(NLEV):
                    for h in range(2):
                        s = SG[h]
                        if lev == 0:
                            pe.wait_ge(s["m_out"], b + 1)
                            pe.wait_ge(s["seeded"], b + 1)
                            pe.wait_ge(s["turned_x"], NLEV * b + 1)
                        else:
                            pe.wait_ge(s["joined"], NLEV * b + lev)
                        pe.wait_ge(s["levels"], NLEV * b + lev + 1)
                        for c in range(CPB):
                            m = pe.matmul(bk(0, h)[:, c * P:(c + 1) * P], Ml[h][lev % 2][:, c, :], X[h][:, c, :], start=True, stop=True)
                        m.then_inc(s["half_done"], 1)
                    for h in range(2):
                        s = SG[h]
                        pe.wait_ge(s["half_out"], NLEV * b + lev + 1)
                        if lev == 0:
                            pe.wait_ge(s["mv_out"], b + 1)
                        else:
                            pe.wait_ge(s["turned_x"], NLEV * b + lev + 1)
                        for c in range(CPB):
                            m = pe.matmul(bk(1, h)[:, c * P:(c + 1) * P], T[h][:, c, :], Y1[h][:, c, :], start=True, stop=True)
                        m.then_inc(s["join_done"], 1)
                for h in range(2):
                    s = SG[h]
                    pe.wait_ge(s["joined"], NLEV * (b + 1))
                    for c in range(CPB):
                        m = pe.matmul(bk(2, h)[:, c * P:(c + 1) * P], X[h][:, c, :], AM[h][:, c, :], start=True, stop=True)
                    m.then_inc(s["wu_done"], 1)
                for h in range(2):
                    pe.wait_ge(SG[h]["wu_out"], b + 1)
                for d in range(2):
                    for c in range(CPB):
                        for h in range(2):
                            m = pe.matmul(quarter(bk(3, d), c)[HP[h]], Wt[h][OWN[d], c, :], BK[d][OWN[d], c, lanes(h)],
                                          start=True, stop=True)
                            if lat:
                                m = pe.matmul(quarter(bk(3, d), CPB + c)[HP[h]], Wt[h][OWN[d], c, :], Em[d][OWN[d], c, h, 1, :],
                                              start=True, stop=True)
                    m.then_inc(SD[d]["gq_done"], 1)
                for c in range(CPB):
                    for d in range(2):
                        s = SD[d]
                        n = b * CPB + c
                        if c == 0:
                            pe.wait_ge(s["gq_out"], b + 1)
                        if n:
                            pe.wait_ge(s["state_out"], n)
                        if n < CHUNKS - 1:
                            for h in range(2):
                                m = pe.matmul(quarter(bk(0, d), c)[HP[h]], BK[d][:, c, lanes(h)], UV[d][:, c, lanes(h)],
                                              start=True, stop=(n == 0))
                                if n:
                                    m = pe.matmul(quarter(bk(0, d), c)[HP[h]], Gt[d][HP[h], c, :], St[d][HP[h], n, :],
                                                  start=False, stop=True)
                            m.then_inc(s["state_done"], 1)
                        if lat:
                            for h in range(2):
                                pe.matmul(quarter(bk(1, d), c)[HP[h]], UV[d][:, c, lanes(h)], Em[d][:, c, h, 1, :],
                                          start=True, stop=False)
                                m = pe.matmul(quarter(bk(1, d), c)[HP[h]], St[d][HP[h], n, :], Qt[d][HP[h], c, :],
                                              start=False, stop=True)
                            if c == CPB - 1:
                                m.then_inc(s["y_done"], 1)

        @block.scalar
        def _(act):
            for b in range(NB):
                for d in range(2):
                    s = SD[d]
                    act.wait_ge(s["turned"], b + 1)
                    act.copy(flat(BK[d][:]), bk(2 + d, 0))
                    act.copy(flat(UV[d][OTH[d]]), bk(2 + d, 1)[OTH[d]])
                    av = bk(2 + d, 1).rearrange("p (c h n) -> p c h n", c=CPB, h=2)
                    for h in range(2):
                        m = act.copy(AM[h][OWN[d], :, 0:CH], av[OWN[d], :, h, :])
                    m.then_inc(s["turned_out"], 1)
                for h in range(2):
                    s = SG[h]
                    act.wait_ge(s["m_done"], b + 1)
                    act.copy(flat(Ms[h][:]), bk(0, h)[:, 0:CPB * CH]).then_inc(s["m_out"], 1)
                for h in range(2):
                    s = SG[h]
                    act.wait_ge(s["mv_done"], b + 1)
                    act.copy(AM[h][:, :, CH:P], bk(1, h)[:, 0:CPB * CH].rearrange("p (c n) -> p c n", c=CPB)).then_inc(s["mv_out"], 1)
                for lev in range(NLEV):
                    for h in range(2):
                        s = SG[h]
                        act.wait_ge(s["half_done"], NLEV * b + lev + 1)
                        act.copy(flat(Y1[h][:]), bk(0, h)).then_inc(s["half_out"], 1)
                wu_out(act, act.copy, b, 0)

        @block.gpsimd
        def _(pool):
            def rep(m):
                return m.rearrange("p (a n) -> p a n", a=2).unsqueeze(1).to_broadcast([P, CPB, 2, CH])

            four = lambda ap: ap.rearrange("p c (a n) -> p c a n", a=2)
            both = lambda ap: ap.unsqueeze(2).to_broadcast([P, CPB, 2, CH])
            link = Link(pool, S["seed_link"])
            for b in range(NB):
                for h in range(2):
                    s = SG[h]
                    pool.wait_ge(s["m_out"], b + 1)
                    if b:
                        pool.wait_ge(s["wu_out"], b)
                    link(pool.tensor_tensor(four(T[h][:]), both(Ms[h][:]), rep(levels[:, 0, :]), ALU.mult))
                    pool.tensor_tensor(T[h][:], T[h][:], ident[:].unsqueeze(1).to_broadcast([P, CPB, P]), ALU.add).then_inc(s["seeded"], 1)
                    pool.tensor_tensor(four(Ml[h][0]), both(Ms[h][:]), rep(levels[:, 1, :]), ALU.mult).then_inc(s["levels"], 1)
                for lev in range(1, NLEV):
                    for h in range(2):
                        s = SG[h]
                        if lev > 1:
                            pool.wait_ge(s["half_done"], NLEV * b + lev - 1)
                        pool.tensor_tensor(four(Ml[h][lev % 2]), both(Ms[h][:]), rep(levels[:, 1 + lev, :]), ALU.mult).then_inc(s["levels"], 1)
                for d in range(2):
                    s = SD[d]
                    if b:
                        pool.wait_ge(s["gq_out"], b)
                    pool.tensor_tensor(Dg[d][:], diag2.unsqueeze(1).to_broadcast([P, CPB, CH]),
                                       cum[d][:, b * CPB:(b + 1) * CPB, CH:CH + 1].to_broadcast([P, CPB, CH]),
                                       ALU.mult).then_inc(s["diag"], 1)

        @block.vector
        def _(dve):
            for b in range(NB):
                lat = b > 0
                for d in range(2):
                    s = SD[d]
                    dve.wait_ge(s["e_done"], b + 1)
                    if lat:
                        src = bank[d][:].rearrange("p (u a n) -> p u a n", a=2, n=CH)
                        dve.tensor_tensor(Em[d][:].rearrange("p c h a n -> p (c h) a n"), src,
                                          upper[:, 0:2, :].unsqueeze(1).to_broadcast([P, 2 * CPB, 2, CH]), ALU.mult).then_inc(s["e_out"], 1)
                    else:
                        dve.tensor_tensor(Em[d][:, :, :, 0, :].rearrange("p c h n -> p (c h) n"),
                                          bank[d][:, 0:512].rearrange("p (u n) -> p u n", n=CH),
                                          upper[:, 0, :].unsqueeze(1).to_broadcast([P, 2 * CPB, CH]), ALU.mult).then_inc(s["e_out"], 1)
                for h in range(2):
                    dve.wait_ge(SG[h]["seeded"], b + 1)
                    dve.transpose(flat(X[h][:]), flat(T[h][:])).then_inc(SG[h]["turned_x"], 1)
                for lev in range(NLEV):
                    for h in range(2):
                        s = SG[h]
                        dve.wait_ge(s["join_done"], NLEV * b + lev + 1)
                        dve.tensor_tensor(flat(X[h][:]), flat(X[h][:]), bk(1, h), ALU.add).then_inc(s["joined"], 1)
                        if lev < NLEV - 1:
                            dve.wait_ge(s["joined"], NLEV * b + lev + 1)
                            dve.transpose(flat(T[h][:]), flat(X[h][:])).then_inc(s["turned_x"], 1)
                wu_out(dve, dve.tensor_copy, b, 1)
                for d in range(2):
                    s = SD[d]
                    dve.wait_ge(s["gq_done"], b + 1)
                    dve.wait_ge(s["diag"], b + 1)
                    m = dve.tensor_tensor(flat(Gt[d][:]), bk(3, d)[:, 0:CPB * CH], flat(Dg[d][:]), ALU.add)
                    if lat:
                        m = dve.tensor_tensor(flat(Qt[d][:]), bk(3, d)[:, CPB * CH:512],
                                              flat(R[d][:, b * CPB:(b + 1) * CPB, :]), ALU.add)
                    m.then_inc(s["gq_out"], 1)
                for c in range(CPB):
                    for d in range(2):
                        s = SD[d]
                        n = b * CPB + c
                        if n < CHUNKS - 1:
                            dve.wait_ge(s["state_done"], n + 1)
                            dve.tensor_copy(St[d][:, n + 1, :], quarter(bk(0, d), c)).then_inc(s["state_out"], 1)
                if lat:
                    for d in range(2):
                        s = SD[d]
                        dve.wait_ge(s["y_done"], b)
                        if b == 2 or d == 1:
                            dve.wait_ge(SD[1 - d]["y_out"], b if d == 1 else b - 1)
                        if b == 2:
                            dve.wait_ge(s["y_out"], b - 1)
                        y = ysum[:, (b - 1) * BT:b * BT]
                        if d:
                            y = flip(ysum[:])[:, (b - 1) * BT:b * BT]
                        dve.tensor_tensor(y, y, bk(1, d)[:, 0:CPB * CH], ALU.add).then_inc(s["y_out"], 1)


def pair_readout(g, p, mix, L):
    nc = g.nc
    S, bk, ysum, tmp, bonus, head_ones, g2, sg, pv, lnx_eps, wd = (
        L[n] for n in ("S", "bk", "ysum", "tmp", "bonus", "head_ones", "g2", "sg", "pv", "lnx_eps", "wd"))
    col = lambda n: pv[:, PV[n]:PV[n] + 1]
    sq, rs = (wd[d][:, 0:LAT // CH, :].rearrange("p c n -> p (c n)") for d in range(2))
    with nc.Block() as block:

        @block.tensor
        def _(pe):
            pe.matmul(bk(0, 0), head_ones[:], ysum[:], start=True, stop=True).then_inc(S["mean_done"], 1)
            for j in range(2):
                m = pe.matmul(bk(2, 0), g2[:, j, :], sg[:, j, :], start=(j == 0), stop=(j == 1))
            m.then_inc(S["gate_done"], 1)
            pe.wait_ge(S["csq_done"], 1)
            pe.matmul(bk(1, 0), head_ones[:], sq, start=True, stop=True).then_inc(S["var_done"], 1)

        @block.scalar
        def _(act):
            act.wait_ge(S["cent_done"], 1)
            act.activation(sq, tmp[:], ACT.Square).then_inc(S["csq_done"], 1)
            act.wait_ge(S["var_done"], 1)
            act.activation(rs, bk(1, 0), ACT.Sqrt, bias=lnx_eps[:, 0:1], scale=1.0 / HD).then_inc(S["std_done"], 1)

        @block.vector
        def _(dve):
            link = Link(dve, S["read_link"])
            dve.wait_ge(S["mean_done"], 1)
            dve.scalar_tensor_tensor(tmp[:], bk(0, 0), -1.0 / HD, ysum[:], ALU.mult, ALU.add).then_inc(S["cent_done"], 1)
            dve.wait_ge(S["std_done"], 1)
            link(dve.reciprocal(rs, rs))
            link(dve.scalar_tensor_tensor(tmp[:], tmp[:], col("lnx_g"), rs, ALU.mult, ALU.mult))
            link(dve.scalar_tensor_tensor(tmp[:], tmp[:], col("lnx_b"), bonus[:], ALU.add, ALU.add))
            dve.wait_ge(S["gate_done"], 1)
            dve.tensor_tensor(mix[:, bass.ds(p + 8, 1), :].rearrange("p a n -> p (a n)"), tmp[:], bk(2, 0),
                              ALU.mult).then_inc(S["mixed_out"], 1)


def clear(nc, sems):
    with nc.Block() as block:

        @block.gpsimd
        def _(pool):
            for s in sems.values():
                pool.sem_clear(s)


def group_norm(g, mix, vec, ones, eps, hi, lo):
    nc = g.nc
    GROUPS = ((0, 4), (4, 8), (8, 16))
    with ExitStack() as st:
        sq = g.sb(st, "grp_sq", [P, 2, LAT])
        inv = g.sb(st, "grp_inv", [P, 3, LAT])
        acc = [g.ps(st, f"grp_acc{j}", [P, 512]) for j in range(3)]
        sq_done, summed, rms_done, inv_done, normed, hi_done = g.sems(
            st, *["grp_" + x for x in ("sq_done", "summed", "rms_done", "inv_done", "normed", "hi_done")])
        with nc.Block() as block:

            @block.scalar
            def _(act):
                for t in range(KT):
                    if t >= 2:
                        act.wait_ge(summed, t - 1)
                    act.activation(sq[:, t % 2, :], mix[:, t, :], ACT.Square).then_inc(sq_done, 1)
                for j, (a, b) in enumerate(GROUPS):
                    act.wait_ge(summed, b)
                    act.activation(inv[:, j, :], acc[j][:], ACT.Sqrt, bias=eps[:, 0:1], scale=1.0 / ((b - a) * P)).then_inc(rms_done, 1)
                for t in range(KT):
                    act.wait_ge(normed, t + 1)
                    act.copy(hi[:, t, :], mix[:, t, :]).then_inc(hi_done, 1)

            @block.tensor
            def _(pe):
                for j, (a, b) in enumerate(GROUPS):
                    for t in range(a, b):
                        pe.wait_ge(sq_done, t + 1)
                        pe.matmul(acc[j][:], ones[:], sq[:, t % 2, :], start=(t == a), stop=(t == b - 1)).then_inc(summed, 1)

            def part(dve, t):
                dve.wait_ge(normed, t + 1)
                dve.wait_ge(hi_done, t + 1)
                dve.tensor_tensor(lo[:, t, :], mix[:, t, :], hi[:, t, :].bitcast(F32), ALU.subtract)

            @block.vector
            def _(dve):
                for j, (a, b) in enumerate(GROUPS):
                    dve.wait_ge(rms_done, j + 1)
                    dve.reciprocal(inv[:, j, :], inv[:, j, :]).then_inc(inv_done, 1)
                dve.wait_ge(inv_done, 3)
                for t in range(KT):
                    j = 0 if t < 4 else 1 if t < 8 else 2
                    dve.scalar_tensor_tensor(mix[:, t, :], mix[:, t, :], vec[:, VEC["grp_g"] + t:VEC["grp_g"] + t + 1],
                                             inv[:, j, :], ALU.mult, ALU.mult).then_inc(normed, 1)
                    if t >= 2:
                        part(dve, t - 2)
                part(dve, KT - 2)
                part(dve, KT - 1)


def output_projection(g, k, mhi, mlo, h, mod):
    nc = g.nc
    w = k["w_out"].rearrange("(k p) n -> p k n", p=P)
    gate = mod[:, 0, 2 * KT:3 * KT]
    with ExitStack() as st:
        ws = WeightStream(g, st, "wout")
        acc = [g.ps(st, f"wout_acc{i}", [P, 512]) for i in range(2)]
        (added,) = g.sems(st, "wout_added")
        with nc.Block() as block:

            @block.sync
            def _(sp):
                ws.credits(sp)
                sp.sem_inc(added, 2)
                with sp.Fori(0, KT // 2) as i:
                    for s in range(2):
                        ws.load(sp, i * 2, s, w[:, :, bass.ds(i * 2 * P + s * P, P)])
                ws.load(sp, KT, 0, w[:, :, 0:P])

            @block.scalar
            def _(act):
                ws.split_hi(act, 0, 0, 0)
                with act.Fori(0, KT // 2) as i:
                    for s in range(2):
                        ws.split_hi(act, i, i * 2, s + 1)

            @block.vector
            def _(dve):
                ws.split_lo(dve, 0, 0)
                with dve.Fori(0, KT // 2) as i:
                    for s in range(2):
                        ws.split_lo(dve, i * 2, s + 1)
                        dve.wait_ge(ws.used, i * 2 + (s + 3))
                        x = h[:, bass.ds(i * 2 + s, 1), :].rearrange("p a n -> p (a n)")
                        gt = gate[:, bass.ds(i * 2 + s, 1)]
                        dve.scalar_tensor_tensor(x, acc[s][:], gt, x, ALU.mult, ALU.add).then_inc(added, 1)

            @block.tensor
            def _(pe):
                with pe.Fori(0, KT // 2) as i:
                    for s in range(2):
                        ws.ready(pe, i * 2, s)
                        pe.wait_ge(added, i * 2 + (s + 1))
                        for kk in range(KT):
                            a, b = (x[s][:, kk * P:(kk + 1) * P] for x in (ws.hi, ws.lo))
                            m = three_passes(pe, acc[s][:], a, b, mhi[:, kk, :], mlo[:, kk, :], kk == 0, kk == KT - 1)
                        m.then_inc(ws.used, 1)


FC = 4
CHUNKS_FF = FT // FC


def conv_glu(g, k, xhi, xlo, h, mod, vec):
    nc = g.nc
    up = k["ffn_up"].rearrange("(k p) n -> p k n", p=P)
    down = k["ffn_down"].rearrange("(j p) n -> p j n", p=P)
    gate = mod[:, 0, 5 * KT:6 * KT]
    UPS = 2 * FC
    DOWNS = KT // 4
    PER = UPS + DOWNS
    with ExitStack() as st:
        ws = WeightStream(g, st, "ffn")
        conv = g.sb(st, "ffn_conv", [P, 2, LAT])
        act_hi = g.sb(st, "ffn_act_hi", [P, FC, LAT], F32R)
        act_lo = g.sb(st, "ffn_act_lo", [P, FC, LAT], F32R)
        up_acc = [g.ps(st, f"ffn_up_acc{i}", [P, 512]) for i in range(4)]
        dn_acc = [g.ps(st, f"ffn_dn_acc{i}", [P, 512]) for i in range(4)]
        tapped, taps, gelu_done, glu_done, act_hi_done, act_lo_done, dn_done, added, v_free = g.sems(
            st, *["ffn_" + x for x in ("tapped", "taps", "gelu_done", "glu_done", "act_hi_done", "act_lo_done", "dn_done",
                                       "added", "v_free")])

        def vcol(name, i, j):
            return vec[:, bass.ds(i * FC + (VEC[name] + j), 1)]

        with nc.Block() as block:

            @block.sync
            def _(sp):
                ws.credits(sp)
                sp.sem_inc(glu_done, 2)
                sp.sem_inc(added, 4)
                with sp.Fori(0, CHUNKS_FF) as i:
                    for s in range(UPS):
                        ws.load(sp, i * PER, s, up[:, :, bass.ds(i * FC * P + (s % 2 * DFF + s // 2 * P), P)])
                    for s in range(DOWNS):
                        ws.load(sp, i * PER, UPS + s, down[:, bass.ds(i * FC, FC), s * 512:(s + 1) * 512])
                ws.load(sp, CHUNKS_FF * PER, 0, up[:, :, 0:P])

            @block.scalar
            def _(act):
                ws.split_hi(act, 0, 0, 0)
                with act.Fori(0, CHUNKS_FF) as i:
                    for s in range(PER):
                        ws.split_hi(act, i * (PER // 2), i * PER, s + 1)
                        if s >= UPS:
                            continue
                        j = s // 2
                        if s % 2 == 0:
                            act.wait_ge(ws.used, i * PER + (s + 3))
                            act.activation(conv[:, j % 2, :], up_acc[j % 2 * 2][:], ACT.Identity, bias=vcol("conv_b", i, j),
                                           scale=vcol("conv_w1", i, j)).then_inc(tapped, 1)
                        else:
                            act.wait_ge(taps, i * 2 * FC + (2 * j + 2))
                            act.activation(conv[:, j % 2, :], conv[:, j % 2, :], ACT.Gelu).then_inc(gelu_done, 1)
                            act.wait_ge(glu_done, i * FC + (j + 3))
                            act.copy(act_hi[:, j, :], conv[:, j % 2, :]).then_inc(act_hi_done, 1)

            @block.vector
            def _(dve):
                ws.split_lo(dve, 0, 0)
                with dve.Fori(0, CHUNKS_FF) as i:
                    for s in range(PER):
                        ws.split_lo(dve, i * PER, s + 1)
                        if s < UPS and s % 2 == 0:
                            j = s // 2
                            c, u = conv[:, j % 2, :], up_acc[j % 2 * 2]
                            dve.wait_ge(tapped, i * FC + (j + 1))
                            dve.scalar_tensor_tensor(c[:, 1:LAT], u[:, 0:LAT - 1], vcol("conv_w0", i, j), c[:, 1:LAT], ALU.mult,
                                                     ALU.add).then_inc(taps, 1)
                            dve.wait_ge(taps, i * 2 * FC + (2 * j + 1))
                            dve.scalar_tensor_tensor(c[:, 0:LAT - 1], u[:, 1:LAT], vcol("conv_w2", i, j), c[:, 0:LAT - 1],
                                                     ALU.mult, ALU.add).then_inc(taps, 1)
                        elif s < UPS:
                            j = s // 2
                            c = conv[:, j % 2, :]
                            dve.wait_ge(gelu_done, i * FC + (j + 1))
                            dve.wait_ge(ws.used, i * PER + (s + 3))
                            dve.tensor_tensor(c, c, up_acc[j % 2 * 2 + 1][:], ALU.mult).then_inc(glu_done, 1)
                            dve.wait_ge(act_hi_done, i * FC + (j + 1))
                            dve.tensor_tensor(act_lo[:, j, :], c, act_hi[:, j, :].bitcast(F32), ALU.subtract).then_inc(act_lo_done, 1)
                        else:
                            for o in range(4):
                                t = (s - UPS) * 4 + o
                                if o < 3:
                                    dve.wait_ge(dn_done, i * (3 * DOWNS) + (3 * (s - UPS) + o + 1))
                                else:
                                    dve.wait_ge(ws.used, i * PER + (s + 3))
                                dve.scalar_tensor_tensor(h[:, t, :], dn_acc[o][:], gate[:, t:t + 1], h[:, t, :], ALU.mult,
                                                         ALU.add).then_inc(added, 1)

            @block.tensor
            def _(pe):
                with pe.Fori(0, CHUNKS_FF) as i:
                    for s in range(UPS):
                        j = s // 2
                        ws.ready(pe, i * PER, s)
                        pe.wait_ge(glu_done, i * FC + (j + 1))
                        for kk in range(KT):
                            a, b = (x[s % 2][:, kk * P:(kk + 1) * P] for x in (ws.hi, ws.lo))
                            m = three_passes(pe, up_acc[j % 2 * 2 + s % 2][:], a, b, xhi[:, kk, :], xlo[:, kk, :], kk == 0,
                                             kk == KT - 1)
                        m.then_inc(ws.used, 1)
                    for s in range(DOWNS):
                        ws.ready(pe, i * PER, UPS + s)
                        for js in (range(FC - 1), (FC - 1,)):
                            if js[0] == FC - 1:
                                pe.wait_ge(act_lo_done, i * FC + FC)
                            for o in range(4):
                                if js[0] == 0:
                                    if s == 0 and o == 0:
                                        pe.wait_ge(act_lo_done, i * FC + (FC - 1))
                                    pe.wait_ge(added, i * KT + (4 * s + o + 1))
                                for j in js:
                                    c0 = j * 512 + o * P
                                    a, b = (x[s % 2][:, c0:c0 + P] for x in (ws.hi, ws.lo))
                                    m = three_passes(pe, dn_acc[o][:], a, b, act_hi[:, j, :], act_lo[:, j, :], j == 0, j == FC - 1)
                                if js[0] == FC - 1 and o < 3:
                                    m.then_inc(dn_done, 1)
                        m.then_inc(ws.used, 1)


def store_transposed(g, src, dst, ident):
    nc = g.nc
    with ExitStack() as st:
        rows = [g.sb(st, f"out_rows{i}", [P, D]) for i in range(2)]
        tp = [g.ps(st, f"out_tp{i}", [P, 4, P]) for i in range(4)]
        turned, act_out, dve_out = g.sems(st, "out_turned", "out_act_copied", "out_dve_copied")
        stored = g.sems(st, "out_stored0", "out_stored1")
        NT = LAT // P
        with nc.Block() as block:

            @block.tensor
            def _(pe):
                for t in range(NT):
                    for q in range(4):
                        if t:
                            pe.wait_ge((act_out, dve_out)[q % 2], 2 * (t - 1) + q // 2 + 1)
                        for j in range(4):
                            m = pe.transpose(tp[q][:, j, :], src[:, 4 * q + j, t * P:(t + 1) * P], ident[:])
                        m.then_inc(turned, 1)

            def copies(eng, copy, par, out):
                for t in range(NT):
                    if t >= 2:
                        eng.wait_ge(stored[t % 2], 16)
                    for q in (par, par + 2):
                        eng.wait_ge(turned, 4 * t + q + 1)
                        copy(rows[t % 2][:, q * 512:(q + 1) * 512], tp[q][:].rearrange("p a b -> p (a b)")).then_inc(out, 1)

            @block.scalar
            def _(act):
                copies(act, act.copy, 0, act_out)

            @block.vector
            def _(dve):
                copies(dve, dve.tensor_copy, 1, dve_out)

            @block.sync
            def _(sp):
                for t in range(NT):
                    sp.wait_ge(act_out, 2 * t + 2)
                    sp.wait_ge(dve_out, 2 * t + 2)
                    sp.dma_start(dst[t * P:(t + 1) * P, :], rows[t % 2][:]).then_inc(stored[t % 2], 16)
                for s in range(2):
                    sp.wait_ge(stored[s], 16 * (NT // 2))


INS = ("x", "ctx", "ada_w", "w_in", "na_rpb", "rw_w2", "rw_a2", "rw_g2", "w_out", "ffn_up", "ffn_down", "vectors",
       "pair_vectors")


def build(nc, k, out, stop=99, kind="Internal"):
    g = Ctx(nc)
    const = shape_constants()
    const["sum_parts"] = np.array([[1, 0], [1, 0], [0, 1], [0, 1]], np.float32)
    k = dict(k)
    for name, a in const.items():
        k[name] = nc.inline_tensor(np.ascontiguousarray(a), "const_" + name).ap()
    f_dram = nc.dram_tensor("f_scratch", [F_ROWS, TOK], F32, kind=kind).ap()
    with ExitStack() as st:
        vec = g.sb(st, "vec", [P, NVEC])
        ident = g.sb(st, "ident", [P, P])
        ones = g.sb(st, "ones", [P, P])
        eps = g.sb(st, "eps", [P, 1])
        mod = g.sb(st, "mod", [P, 2, 96])
        gain = g.sb(st, "gain", [P, 3, KT])
        (setup_in, setup_done) = g.sems(st, "setup_in", "setup_done")
        with nc.Block() as block:

            @block.sync
            def _(sp):
                sp.dma_start(vec[:], k["vectors"]).then_inc(setup_in, 16)
                sp.dma_start(ident[:], k["ident"]).then_inc(setup_in, 16)
                sp.wait_ge(setup_in, 32)

            @block.vector
            def _(dve):
                dve.memset(ones[:], 1.0)
                dve.memset(eps[:], EPS)

        modulation(g, k, vec, None, ident, mod)
        h_dram = nc.dram_tensor("h_scratch", [P, KT, LAT], F32, kind="Internal").ap()
        hst = st.enter_context(ExitStack())
        h = g.sb(hst, "h", [P, KT, LAT])
        load_transposed(g, k["x"], LAT // 256, h, ident, "x")
        with nc.Block() as block:

            @block.vector
            def _(dve):
                for n, (s, j, name) in enumerate(((0, 1, "norm1_g"), (0, 4, "norm2_g"), (1, 1, "norm1_g"))):
                    dve.scalar_tensor_tensor(gain[:, n, :], mod[:, s, j * KT:(j + 1) * KT], 1.0,
                                             vec[:, VEC[name]:VEC[name] + KT], ALU.add, ALU.mult)

        with ExitStack() as st1:
            xhi = g.sb(st1, "xhi", [P, KT, LAT], F32R)
            xlo = g.sb(st1, "xlo", [P, KT, LAT], F32R)
            chi = g.sb(st1, "chi", [P, KT, CTX], F32R)
            clo = g.sb(st1, "clo", [P, KT, CTX], F32R)
            with ExitStack() as st2:
                hc = g.sb(st2, "hc", [P, KT, CTX])
                load_transposed(g, k["ctx"], CTX // 256, hc, ident, "ctx")
                norm_split(g, hc, CTX, ones, eps, gain[:, 2, :], mod[:, 1, 0:KT], chi, clo, "nc")
            norm_split(g, h, LAT, ones, eps, gain[:, 0, :], mod[:, 0, 0:KT], xhi, xlo, "n1")
            input_projection(g, k, xhi, xlo, chi, clo, f_dram)
        if stop <= 1:
            return
        move(nc, h_dram, h[:])
        hst.close()
        mst = st.enter_context(ExitStack())
        mix = g.sb(mst, "mix", [P, KT, LAT])
        attention(g, k, f_dram, mix, ident, vec, eps)
        if stop != 2:
            rwkv(g, k, f_dram, mix, ident, vec, eps)
        if stop == 3:
            return dump(nc, mix, out)
        if stop == 2:
            return dump(nc, mix, out, 8)
        mhi = g.sb(mst, "mix_hi", [P, KT, LAT], F32R)
        mlo = g.sb(mst, "mix_lo", [P, KT, LAT], F32R)
        group_norm(g, mix, vec, ones, eps, mhi, mlo)
        h = mix
        move(nc, h[:], h_dram)
        output_projection(g, k, mhi, mlo, h, mod)
        if stop == 5:
            return dump(nc, h, out)
        norm_split(g, h, LAT, ones, eps, gain[:, 1, :], mod[:, 0, 3 * KT:4 * KT], mhi, mlo, "n2")
        conv_glu(g, k, mhi, mlo, h, mod, vec)
        if stop == 6:
            return dump(nc, h, out)
        norm_split(g, h, LAT, ones, eps, vec[:, VEC["final_g"]:VEC["final_g"] + KT], None, None, None, "nf", out=mix)
        store_transposed(g, mix, out[0], ident)


def move(nc, dst, src):
    with nc.semaphore("moved") as moved:
        with nc.Block() as block:

            @block.sync
            def _(sp):
                sp.dma_start(dst, src).then_inc(moved, 16)
                sp.wait_ge(moved, 16)

        clear(nc, {"moved": moved})


def dump(nc, buf, out, nt=KT):
    with nc.semaphore("dumped") as d, nc.Block() as block:

        @block.sync
        def _(sp):
            sp.dma_start(out[0].rearrange("a b -> (a b)").rearrange("(t p n) -> p t n", p=P, n=LAT)[:, 0:nt], buf[:, 0:nt]).then_inc(d, 16)
            sp.wait_ge(d, 16)


def layout(inputs):
    a = {n: np.ascontiguousarray(np.asarray(v)) for n, v in inputs.items()}
    col = lambda v: v.reshape(-1, P).T
    both = lambda v: np.concatenate([v, v]).reshape(P, 1)
    g2 = lambda v: np.stack([v[:P], np.concatenate([v[P:], np.zeros(96, v.dtype)])], 1)
    conv = a["ffn_conv_w"][0]
    vectors = np.concatenate(
        [col(a["norm1_g"][0]), col(a["norm2_g"][0]), col(a["final_g"]), col(a["c"][0]), col(a["c_ctx"]), col(a["ada_b"][0]),
         col(a["grp_g"][0]), col(conv[0]), col(conv[1]), col(conv[2]), col(a["ffn_conv_b"][0]), both(a["q_gain"][0]),
         both(a["k_gain"][0]), a["rw_mu_w"][0].reshape(P, 1), a["rw_mu_a"][0].reshape(P, 1), g2(a["rw_mu_g"][0, 0]),
         g2(a["rw_mu_g"][0, 1])], 1)
    mu = a["rw_mu_rkv"][0].reshape(2, 3, PAIRS, P)
    per = [mu[d, j] for j in range(3) for d in range(2)]
    per += [a["rw_w0"][0, d].reshape(PAIRS, P) for d in range(2)] + [a["rw_a0"][0, d].reshape(PAIRS, P) for d in range(2)]
    per += [a[n][0].reshape(PAIRS, P) for n in ("rw_k_k", "rw_k_a", "rw_r_k", "rw_lnx_g", "rw_lnx_b")]
    arrays = {
        "x": a["x"][0], "ctx": a["ctx"][0], "ada_w": a["ada_w"][0], "w_in": a["w_in"][0], "na_rpb": np.pad(a["na_rpb"][0][:, :, ::-1].reshape(-1), RPB_PAD),
        "rw_w2": a["rw_w2"][0].reshape(2 * HD, CW), "rw_a2": a["rw_a2"][0].reshape(2 * HD, CW),
        "rw_g2": a["rw_g2"][0], "w_out": a["w_out"][0], "ffn_up": a["ffn_up"][0], "ffn_down": a["ffn_down"][0],
        "vectors": vectors, "pair_vectors": np.stack(per, 2),
    }
    return {n: np.ascontiguousarray(v) for n, v in arrays.items()}


def kernel(**inputs):
    import concourse.bacc as bacc
    from concourse.bass_utils import run_bass_kernel_spmd

    nc = bacc.Bacc("TRN2", target_bir_lowering=False, num_devices=1)
    arrays = layout(inputs)
    k = {n: nc.dram_tensor(f"in_{n}", a.shape, mybir.dt.from_np(a.dtype), kind="ExternalInput").ap() for n, a in arrays.items()}
    out = nc.dram_tensor("out_h", (1, LAT, D), F32, kind="ExternalOutput").ap()
    build(nc, k, out)
    r = run_bass_kernel_spmd(nc, [{f"in_{n}": a for n, a in arrays.items()}], core_ids=[0])
    return r.results[0]["out_h"]
```

```python
from contextlib import ExitStack

import numpy as np

import concourse.bass as bass
from concourse import mybir

F32 = mybir.dt.float32
F32R = mybir.dt.float32r
ALU = mybir.AluOpType
ACT = mybir.ActivationFunctionType
AX_X = mybir.AxisListType.X

P = 128
D = 2048
KT = D // P
LAT = 512
CTX = 256
TOK = CTX + LAT
HD = 64
GRID = 64
ROWS = LAT // GRID
NAW = 16
RPB_C = 2 * NAW - 1
RPB_R = 15
AH = 8
BH = 8
CW = 1024
PAIRS = CW // P
DFF = 5632
FT = DFF // P
GLORA = 160
IN_COLS = 5792
EPS = 1e-6
LNX_EPS = 64e-5
CH = 64
BT = 256
CPB = BT // CH
NB = TOK // BT
NLEV = 5

QA, KA, VA, QB, KVB, RW_R, RW_K, RW_V, RW_WD, RW_AD, RW_GD = 0, 4, 8, 12, 16, 18, 26, 34, 42, 43, 44
F_ROWS = 46 * P

VEC = {}
_at = 0
for _n, _w in (("norm1_g", KT), ("norm2_g", KT), ("final_g", KT), ("c", KT), ("c_ctx", KT), ("ada_b", 96), ("grp_g", KT),
               ("conv_w0", FT), ("conv_w1", FT), ("conv_w2", FT), ("conv_b", FT), ("q_gain", 1), ("k_gain", 1),
               ("mu_w", 1), ("mu_a", 1), ("mu_g0", 2), ("mu_g1", 2)):
    VEC[_n] = _at
    _at += _w
NVEC = _at
PV = {}
_at = 0
for _n, _w in (("mu_r", 2), ("mu_k", 2), ("mu_v", 2), ("w0", 2), ("a0", 2), ("k_k", 1), ("k_a", 1), ("r_k", 1),
               ("lnx_g", 1), ("lnx_b", 1)):
    PV[_n] = _at
    _at += _w
NPV = _at


def shape_constants():
    out = {}
    eye = np.eye(P, dtype=np.float32)
    out["ident"] = eye
    block = np.zeros((P, P), np.float32)
    block[:HD, :HD] = 1.0
    block[HD:, HD:] = 1.0
    out["head_ones"] = block
    pairs = HD // 4
    inv = np.float32(10000.0) ** (-np.arange(pairs, dtype=np.float32) / np.float32(pairs))
    t = np.arange(LAT)
    pos = np.stack([t // GRID, t % GRID]).astype(np.float32)
    cos = np.zeros((P, LAT), np.float32)
    sin = np.zeros((P, LAT), np.float32)
    swap = np.zeros((P, P), np.float32)
    for p in range(P):
        axis, half, i = (p % HD) // 32, (p % 32) // pairs, p % pairs
        ang = pos[axis] * inv[i]
        cos[p], sin[p] = np.cos(ang), np.sin(ang)
        if half == 0:
            swap[p + pairs, p] = -1.0
        else:
            swap[p - pairs, p] = 1.0
    out["rope"] = np.stack([cos, sin], 1)
    out["rope_swap"] = swap
    x = np.arange(GRID)[:, None]
    y = np.arange(GRID)[None, :]
    start = np.clip(x - NAW // 2, 0, GRID - NAW)
    inside = (y >= start) & (y < start + NAW)
    win = np.where(inside, np.float32(0.0), np.float32(-1e30)).astype(np.float32)
    out["window"] = np.concatenate([win, win], 0)
    s = np.arange(CH)[:, None]
    u = np.arange(CH)[None, :]
    masks = [(s < u), (s <= u), (s == u)]
    for lev in range(NLEV + 1):
        w = 1 << lev
        masks.append((s // (2 * w) == u // (2 * w)) & (s // w % 2 == 0) & (u // w % 2 == 1))
    upper = np.stack([m.astype(np.float32) for m in masks[:3]], 1)
    out["mask_upper"] = np.concatenate([upper, upper], 0)
    lower = np.zeros((P, NLEV + 1, P), np.float32)
    for lev, m in enumerate(masks[3:]):
        for d in range(2):
            lower[d * CH:(d + 1) * CH, lev, d * CH:(d + 1) * CH] = m.T
    out["mask_levels"] = lower
    return out


class Ctx:

    def __init__(self, nc):
        self.nc = nc
        self.held = {}

    def sb(self, stack, name, shape, dt=F32):
        return stack.enter_context(self.nc.sbuf_tensor(name, shape, dt))

    def ps(self, stack, name, shape):
        return stack.enter_context(self.nc.psum_tensor(name, shape, F32))

    def sems(self, stack, *names):
        if id(stack) not in self.held:
            self.held[id(stack)] = []
            stack.callback(self.clear_held, id(stack))
        got = [stack.enter_context(self.nc.semaphore(n)) for n in names]
        self.held[id(stack)] += got
        return got

    def clear_held(self, key):
        clear(self.nc, dict(enumerate(self.held.pop(key))))


def condition(g, vec, cond, tag):
    nc = g.nc
    with ExitStack() as st:
        sig = g.sb(st, f"{tag}_sigmoid", [P, 2 * KT])
        silu = g.sb(st, f"{tag}_silu", [P, 2 * KT])
        sig_done, silu_done, cond_done = g.sems(st, f"{tag}_sig_done", f"{tag}_silu_done", f"{tag}_done")
        with nc.Block() as block:

            @block.scalar
            def _(act):
                act.activation(sig[:], vec[:, VEC["c"]:VEC["c"] + 2 * KT], ACT.Sigmoid).then_inc(sig_done, 1)
                act.wait_ge(silu_done, 2)
                for s in range(2):
                    act.copy(cond[:, :, 2 * s], silu[:, s * KT:(s + 1) * KT]).then_inc(cond_done, 1)

            @block.vector
            def _(dve):
                dve.memset(cond.bitcast(F32), 0.0).then_inc(silu_done, 1)
                dve.wait_ge(sig_done, 1)
                dve.tensor_tensor(silu[:], sig[:], vec[:, VEC["c"]:VEC["c"] + 2 * KT], ALU.mult).then_inc(silu_done, 1)
                dve.wait_ge(cond_done, 2)
                for s in range(2):
                    dve.tensor_tensor(cond[:, :, 2 * s + 1], silu[:, s * KT:(s + 1) * KT],
                                      cond[:, :, 2 * s].bitcast(F32), ALU.subtract).then_inc(cond_done, 1)


ADA_FIRST = 2


def modulation(g, k, vec, cond, sel, mod):
    nc = g.nc
    NBLK = ADA_FIRST * D // 512
    COLS = NBLK * 512 // P
    UNR = 4
    QK = KT // 4
    aw = k["ada_w"].rearrange("(q p) n -> p q n", p=P)
    with ExitStack() as st:
        raw = [g.sb(st, f"ada_raw{i}", [P, 4, 512]) for i in range(4)]
        hi = [g.sb(st, f"ada_hi{i}", [P, 4, 512], F32R) for i in range(4)]
        lo = [g.sb(st, f"ada_lo{i}", [P, 4, 512], F32R) for i in range(4)]
        rows = g.sb(st, "ada_rows", [4, NBLK * 512])
        acc = [g.ps(st, f"ada_acc{i}", [P, 512]) for i in range(2)]
        colp = g.ps(st, "ada_cols", [P, 2 * COLS])
        rows_done, col_ready, mod_done, sel_in = g.sems(st, "ada_rows_done", "ada_col_ready", "mod_done", "ada_sel_in")
        landed = g.sems(st, *[f"ada_landed{i}" for i in range(4)])
        hi_done, lo_done, used = g.sems(st, "ada_hi_done", "ada_lo_done", "ada_used")
        with nc.Block() as block:

            @block.sync
            def _(sp):
                sp.dma_start(sel[:], k["sum_parts"]).then_inc(sel_in, 16)
                sp.sem_inc(lo_done, 4)
                with sp.Fori(0, NBLK) as b:
                    for q in range(QK):
                        sp.wait_ge(lo_done, b * QK + (q + 1))
                        sp.dma_start(raw[q][:], aw[:, 4 * q:4 * q + 4, bass.ts(b, 512)]).then_inc(landed[q], 16)

            @block.scalar
            def _(act):
                with act.Fori(0, NBLK) as b:
                    for q in range(QK):
                        act.wait_ge(landed[q], b * 16 + 16)
                        act.wait_ge(used, b * QK + (q + 1))
                        act.copy(hi[q][:], raw[q][:]).then_inc(hi_done, 1)

            @block.vector
            def _(dve):
                def row(i, j):
                    dve.wait_ge(used, i * (UNR * QK) + ((j + 1) * QK + 4))
                    dve.tensor_copy(rows[:, bass.ds(i * (UNR * 512) + j * 512, 512)], acc[j % 2][0:4, :]).then_inc(rows_done, 1)

                with dve.Fori(0, NBLK // UNR) as i:
                    for j in range(UNR):
                        for q in range(QK):
                            dve.wait_ge(hi_done, i * (UNR * QK) + (j * QK + q + 1))
                            dve.tensor_tensor(lo[q][:], raw[q][:], hi[q][:].bitcast(F32), ALU.subtract).then_inc(lo_done, 1)
                            if q == 1 and j:
                                row(i, j - 1)
                    row(i, UNR - 1)
                dve.wait_ge(col_ready, 1)
                dve.tensor_tensor(mod[:, :, 0:COLS], colp[:].rearrange("p (j s) -> p s j", s=2),
                                  vec[:, VEC["ada_b"]:VEC["ada_b"] + COLS].unsqueeze(1).to_broadcast([P, 2, COLS]),
                                  ALU.add).then_inc(mod_done, 1)

            @block.tensor
            def _(pe):
                pe.sem_inc(used, 4)
                pe.sem_inc(rows_done, 2)
                with pe.Fori(0, NBLK // UNR) as i:
                    for n in range(UNR):
                        for q in range(QK):
                            if q == 0:
                                pe.wait_ge(rows_done, i * UNR + (n + 1))
                            pe.wait_ge(lo_done, i * (UNR * QK) + (n * QK + q + 5))
                            for j in range(4):
                                for part, w in enumerate((hi, lo)):
                                    m = pe.matmul(acc[n % 2][:], cond[:, 4 * q + j, :], w[q][:, j, :],
                                                  start=(q == 0 and j == 0 and part == 0),
                                                  stop=(q == QK - 1 and j == 3 and part == 1))
                            m.then_inc(used, 1)
                pe.wait_ge(rows_done, NBLK + 2)
                pe.wait_ge(sel_in, 16)
                for j in range(COLS):
                    m = pe.matmul(colp[:, 2 * j:2 * j + 2], rows[:, j * P:(j + 1) * P], sel[:], start=True, stop=True)
                m.then_inc(col_ready, 1)


def load_transposed(g, src, n_pairs, dst, ident, tag):
    nc = g.nc
    with ExitStack() as st:
        rows = [g.sb(st, f"{tag}_rows{i}", [P, D]) for i in range(2)]
        tp = [g.ps(st, f"{tag}_tp{i}", [P, 4, P]) for i in range(4)]
        landed = g.sems(st, f"{tag}_landed0", f"{tag}_landed1")
        turned, (act_out, dve_out) = g.sems(st, f"{tag}_turned")[0], g.sems(st, f"{tag}_act_out", f"{tag}_dve_out")
        with nc.Block() as block:

            @block.sync
            def _(sp):
                sp.sem_inc(turned, 4 * 2)
                with sp.Fori(0, n_pairs) as i:
                    for u in range(2):
                        sp.wait_ge(turned, i * 8 + (4 * u + 4))
                        sp.dma_start(rows[u][:], src[bass.ds(i * 256 + u * P, P), :]).then_inc(landed[u], 16)

            @block.tensor
            def _(pe):
                with pe.Fori(0, n_pairs) as i:
                    for u in range(2):
                        pe.wait_ge(landed[u], i * 16 + 16)
                        for q in range(4):
                            pe.wait_ge((act_out, dve_out)[q % 2], i * 4 + (2 * u + q // 2 + 1))
                            for j in range(4):
                                m = pe.transpose(tp[q][:, j, :], rows[u][:, (4 * q + j) * P:(4 * q + j + 1) * P], ident[:])
                            m.then_inc(turned, 1)

            def copies(eng, copy, par, out):
                eng.sem_inc(out, 2)
                with eng.Fori(0, n_pairs) as i:
                    for u in range(2):
                        for q in (par, par + 2):
                            eng.wait_ge(turned, i * 8 + (4 * u + q + 9))
                            copy(dst[:, 4 * q:4 * q + 4, bass.ds(i * 256 + u * P, P)], tp[q][:]).then_inc(out, 1)

            @block.scalar
            def _(act):
                copies(act, act.copy, 0, act_out)

            @block.vector
            def _(dve):
                copies(dve, dve.tensor_copy, 1, dve_out)


def square_sums(block, src, n, groups, ones, sq, parts, acc, sems):
    even_in, added, odd_in, summed = sems
    firsts = [a for a, _ in groups]
    evens = [t for t in range(0, groups[-1][1], 2) if t not in firsts]
    odds = list(range(1, groups[-1][1], 2))

    def squares(act):
        for j, (a, b) in enumerate(groups):
            for t in range(a, b):
                x = src[:, t, :]
                if t == a:
                    act.activation(parts[:, j, :], x, ACT.Square).then_inc(even_in, 1)
                elif t in evens:
                    e = evens.index(t)
                    if e >= 2:
                        act.wait_ge(added, e - 1)
                    act.activation(sq[:, e % 2, :], x, ACT.Square).then_inc(even_in, 1)
                else:
                    o = odds.index(t)
                    if o >= 2:
                        act.wait_ge(summed, o - 1)
                    act.activation(sq[:, 2 + o % 2, :], x, ACT.Square).then_inc(odd_in, 1)

    def additions(dve):
        for e, t in enumerate(evens):
            j = max(i for i, a in enumerate(firsts) if a <= t)
            dve.wait_ge(even_in, t // 2 + 1)
            if e and evens[e - 1] > firsts[j]:
                dve.wait_ge(added, e)
            dve.tensor_tensor(parts[:, j, :], parts[:, j, :], sq[:, e % 2, :], ALU.add).then_inc(added, 1)

    def products(pe, total):
        for o, t in enumerate(odds):
            j = max(i for i, a in enumerate(firsts) if a <= t)
            pe.wait_ge(odd_in, o + 1)
            pe.matmul(acc[j][:, 0:n], ones[:], sq[:, 2 + o % 2, :], start=(t == firsts[j] + 1), stop=False).then_inc(summed, 1)
            if t == groups[j][1] - 1:
                pe.wait_ge(added, sum(e < t for e in evens))
                pe.matmul(acc[j][:, 0:n], ones[:], parts[:, j, :], start=False, stop=True).then_inc(total, 1)

    return squares, additions, products


def norm_split(g, src, n, ones, eps, gain, shift, hi, lo, tag, out=None):
    nc = g.nc
    with ExitStack() as st:
        sq = g.sb(st, f"{tag}_sq", [P, 4, n])
        parts = g.sb(st, f"{tag}_parts", [P, 1, n])
        scaled = g.sb(st, f"{tag}_scaled", [P, 4, n])
        rms = g.sb(st, f"{tag}_rms", [P, n])
        inv = g.sb(st, f"{tag}_inv", [P, n])
        acc = g.ps(st, f"{tag}_acc", [P, 512])
        total, rms_done, inv_done, scaled_done, shifted, hi_done, lo_even, lo_odd = g.sems(
            st, *[f"{tag}_{x}" for x in ("total", "rms_done", "inv_done", "scaled_done", "shifted", "hi_done", "lo_even", "lo_odd")])
        sums = g.sems(st, *[f"{tag}_{x}" for x in ("even_in", "added", "odd_in", "summed")])
        with nc.Block() as block:
            squares, additions, products = square_sums(block, src, n, ((0, KT),), ones, sq, parts, [acc], sums)

            @block.scalar
            def _(act):
                squares(act)
                act.wait_ge(total, 1)
                act.activation(rms[:], acc[:, 0:n], ACT.Sqrt, bias=eps[:, 0:1], scale=1.0 / D).then_inc(rms_done, 1)
                if out is None:
                    for k in range(KT):
                        act.wait_ge(scaled_done, k + 1)
                        x = scaled[:, k % 4, :]
                        if k % 2:
                            act.activation(x, x, ACT.Identity, bias=shift[:, k:k + 1]).then_inc(shifted, 1)
                            act.wait_ge(shifted, k // 2 + 1)
                            act.copy(hi[:, k, :], x).then_inc(hi_done, 1)
                        else:
                            act.activation(hi[:, k, :], x, ACT.Identity, bias=shift[:, k:k + 1]).then_inc(hi_done, 1)

            @block.tensor
            def _(pe):
                products(pe, total)

            @block.gpsimd
            def _(pool):
                if out is None:
                    for k in range(1, KT, 2):
                        pool.wait_ge(hi_done, k + 1)
                        pool.tensor_tensor(lo[:, k, :], scaled[:, k % 4, :], hi[:, k, :].bitcast(F32), ALU.subtract).then_inc(lo_odd, 1)

            @block.vector
            def _(dve):
                additions(dve)
                dve.wait_ge(rms_done, 1)
                dve.reciprocal(inv[:], rms[:]).then_inc(inv_done, 1)
                dve.wait_ge(inv_done, 1)
                for k in range(KT):
                    if out is not None:
                        dve.scalar_tensor_tensor(out[:, k, :], src[:, k, :], gain[:, k:k + 1], inv[:], ALU.mult,
                                                 ALU.mult).then_inc(scaled_done, 1)
                        continue
                    if k >= 4:
                        dve.wait_ge(lo_odd if k % 2 else lo_even, k // 2 - 1)
                    dve.scalar_tensor_tensor(scaled[:, k % 4, :], src[:, k, :], gain[:, k:k + 1], inv[:], ALU.mult,
                                             ALU.mult).then_inc(scaled_done, 1)
                    if k % 2:
                        dve.wait_ge(hi_done, k)
                        dve.scalar_tensor_tensor(lo[:, k - 1, :], scaled[:, (k - 1) % 4, :], shift[:, k - 1:k],
                                                 hi[:, k - 1, :].bitcast(F32), ALU.add, ALU.subtract).then_inc(lo_even, 1)


class WeightStream:

    def __init__(self, g, st, tag):
        self.raw = [g.sb(st, f"{tag}_raw{i}", [P, 2048]) for i in range(2)]
        self.hi = [g.sb(st, f"{tag}_whi{i}", [P, 2048], F32R) for i in range(2)]
        self.lo = [g.sb(st, f"{tag}_wlo{i}", [P, 2048], F32R) for i in range(2)]
        self.landed = g.sems(st, f"{tag}_w_landed0", f"{tag}_w_landed1")
        self.hi_done, self.lo_done, self.used = g.sems(st, f"{tag}_w_hi_done", f"{tag}_w_lo_done", f"{tag}_w_used")

    def credits(self, sp):
        sp.sem_inc(self.lo_done, 2)
        sp.sem_inc(self.used, 2)

    def load(self, sp, n, s, src):
        sp.wait_ge(self.lo_done, n + (s + 1))
        dst = self.raw[s % 2][:]
        if len(src.shape) == 3:
            dst = dst.rearrange("p (a b) -> p a b", a=src.shape[1])
        sp.dma_start(dst, src).then_inc(self.landed[s % 2], 16)

    def split_hi(self, act, half, n, s):
        act.wait_ge(self.landed[s % 2], half * 16 + (s // 2 + 1) * 16)
        act.wait_ge(self.used, n + (s + 1))
        act.copy(self.hi[s % 2][:], self.raw[s % 2][:]).then_inc(self.hi_done, 1)

    def split_lo(self, dve, n, s):
        dve.wait_ge(self.hi_done, n + (s + 1))
        dve.tensor_tensor(self.lo[s % 2][:], self.raw[s % 2][:], self.hi[s % 2][:].bitcast(F32),
                          ALU.subtract).then_inc(self.lo_done, 1)

    def ready(self, pe, n, s):
        pe.wait_ge(self.lo_done, n + (s + 3))


def three_passes(pe, out, whi, wlo, xhi, xlo, first, last):
    pe.matmul(out, whi, xhi, start=first, stop=False)
    pe.matmul(out, whi, xlo, start=False, stop=False)
    return pe.matmul(out, wlo, xhi, start=False, stop=last)


def input_projection(g, k, xhi, xlo, chi, clo, f_dram, h, h_dram):
    nc = g.nc
    segs = [(QA, 4, False), (KA, 8, True), (QB, 4, False), (KVB, 2, True), (RW_R, 8, False), (RW_K, 18, True)]
    total = 46
    w = k["w_in"].rearrange("(k p) n -> p k n", p=P)
    with ExitStack() as st:
        ws = WeightStream(g, st, "win")
        res = [g.sb(st, f"f_tile{i}", [P, TOK]) for i in range(2)]
        lat = [g.ps(st, f"f_lat{i}", [P, 512]) for i in range(2)]
        ctx = [g.ps(st, f"f_ctx{i}", [P, 512]) for i in range(2)]
        lat_out, ctx_out = g.sems(st, "f_lat_out", "f_ctx_out")
        stored = g.sems(st, "f_stored0", "f_stored1")
        (h_saved,) = g.sems(st, "f_h_saved")

        def tiles():
            base = 0
            for t0, n, both in segs:
                yield base, t0, n, both
                base += n

        with nc.Block() as block:

            @block.sync
            def _(sp):
                ws.credits(sp)
                sp.sem_inc(stored[0], 16)
                sp.sem_inc(stored[1], 16)
                sp.sem_inc(lat_out, 2)
                sp.sem_inc(ctx_out, 2)
                for base, t0, n, both in tiles():
                    with sp.Fori(0, n // 2) as i:
                        for s in range(2):
                            ws.load(sp, i * 2 + base, s, w[:, :, bass.ds(i * 2 * P + (t0 + s) * P, P)])
                    if base == 0:
                        sp.dma_start(h_dram, h[:]).then_inc(h_saved, 16)
                for s, c0 in enumerate((44 * P, IN_COLS - P)):
                    ws.load(sp, total - 2, s, w[:, :, c0:c0 + P])
                sp.wait_ge(h_saved, 16)
                ws.load(sp, total, 0, w[:, :, 0:P])

            def act_slot(act, i, base, s, row, both):
                ws.split_hi(act, i + base // 2, i * 2 + base, s + 1)
                act.wait_ge(ws.used, i * 2 + (base + s + 3))
                act.wait_ge(stored[s], i * 16 + (base // 2 + 1) * 16)
                act.copy(res[s][:, CTX:TOK], lat[s][:]).then_inc(lat_out, 1)
                act.wait_ge(lat_out, i * 2 + (base + s + 3))
                act.wait_ge(ctx_out, i * 2 + (base + s + 3))
                act.dma_start(f_dram[row, :], res[s][:]).then_inc(stored[s], 16)

            @block.scalar
            def _(act):
                ws.split_hi(act, 0, 0, 0)
                for base, t0, n, both in tiles():
                    with act.Fori(0, n // 2) as i:
                        for s in range(2):
                            act_slot(act, i, base, s, bass.ds(i * 2 * P + (t0 + s) * P, P), both)
                for s in range(2):
                    act_slot(act, 0, total - 2, s, bass.ds((44 + s) * P, P), False)
                for s in range(2):
                    act.wait_ge(stored[s], 16 + total // 2 * 16)

            def dve_slot(dve, i, base, s):
                ws.split_lo(dve, i * 2 + base, s + 1)
                dve.wait_ge(ws.used, i * 2 + (base + s + 3))
                dve.wait_ge(stored[s], i * 16 + (base // 2 + 1) * 16)
                return res[s][:, 0:CTX], ctx[s][:, 0:CTX]

            @block.vector
            def _(dve):
                ws.split_lo(dve, 0, 0)
                for base, t0, n, both in tiles():
                    with dve.Fori(0, n // 2) as i:
                        for s in range(2):
                            dst, src = dve_slot(dve, i, base, s)
                            if both:
                                dve.tensor_copy(dst, src).then_inc(ctx_out, 1)
                            else:
                                dve.memset(dst, 0.0).then_inc(ctx_out, 1)
                for s in range(2):
                    dst, _ = dve_slot(dve, 0, total - 2, s)
                    dve.memset(dst, 0.0).then_inc(ctx_out, 1)

            def pe_slot(pe, i, base, s, both):
                ws.ready(pe, i * 2 + base, s)
                pe.wait_ge(lat_out, i * 2 + (base + s + 1))
                if both:
                    pe.wait_ge(ctx_out, i * 2 + (base + s + 1))
                for kk in range(KT):
                    a, b = (x[s][:, kk * P:(kk + 1) * P] for x in (ws.hi, ws.lo))
                    m = three_passes(pe, lat[s][:], a, b, xhi[:, kk, :], xlo[:, kk, :], kk == 0, kk == KT - 1)
                if both:
                    for kk in range(KT):
                        a, b = (x[s][:, kk * P:(kk + 1) * P] for x in (ws.hi, ws.lo))
                        m = three_passes(pe, ctx[s][:, 0:CTX], a, b, chi[:, kk, :], clo[:, kk, :], kk == 0, kk == KT - 1)
                m.then_inc(ws.used, 1)

            @block.tensor
            def _(pe):
                for base, t0, n, both in tiles():
                    with pe.Fori(0, n // 2) as i:
                        for s in range(2):
                            pe_slot(pe, i, base, s, both)
                for s in range(2):
                    pe_slot(pe, 0, total - 2, s, False)


LAT_ALL = slice(0, LAT)
KEYS = LAT + CTX
KEY_TILES = KEYS // P
QT = LAT // P
BIAS_ROWS = 14
RPB_PAD = 64


def attention(g, k, f_dram, mix, ident, vec, eps, cond, sel, mod):
    nc = g.nc
    UNITS = 4 * QT
    PIECES = [("q", 0, LAT, True), ("k", 0, LAT, True), ("k", LAT, CTX, False)]
    rpb = k["na_rpb"]
    with ExitStack() as st:
        raw = {n: g.sb(st, f"att_{n}", [P, KEYS if n[1] != "q" else LAT]) for n in ("aq", "ak", "av", "bq", "bk", "bv")}
        qs = g.sb(st, "att_aq_scaled", [P, LAT])
        bqn = g.sb(st, "att_bq_ready", [P, LAT])
        bkn = g.sb(st, "att_bk_ready", [P, KEYS])
        gains = g.sb(st, "att_gains", [P, 2])
        bias = g.sb(st, "att_bias", [P, AH, BIAS_ROWS, GRID])
        bias_now = g.sb(st, "att_bias_now", [P, 2, BIAS_ROWS, GRID])
        window = g.sb(st, "att_window", [P, GRID])
        rope = g.sb(st, "att_rope", [P, 2, LAT])
        swap = g.sb(st, "att_swap", [P, P])
        head_ones = g.sb(st, "att_head_ones", [P, P])
        sq = g.sb(st, "att_sq", [P, LAT])
        rms = g.sb(st, "att_rms", [P, LAT])
        normed = g.sb(st, "att_normed", [P, LAT])
        turned = g.sb(st, "att_turned", [P, LAT])
        vtok = [g.sb(st, f"att_{n}_tok", [P, KEY_TILES, P]) for n in "ab"]
        prob = [g.sb(st, f"att_prob{i}", [P, KEYS]) for i in range(2)]
        pt = [g.sb(st, f"att_prob_t{i}", [P, KEY_TILES, LAT]) for i in range(2)]
        mx = g.sb(st, "att_max", [P, UNITS, 2])
        nm = g.sb(st, "att_negmax", [P, UNITS])
        den = g.sb(st, "att_sum", [P, UNITS])
        rden = g.sb(st, "att_recip", [P, UNITS])
        sc = [g.ps(st, f"att_scores{i}", [P, 1024]) for i in range(2)]
        tp = g.ps(st, "att_tp", [P, 2, 512])
        outp = g.ps(st, "att_out", [P, 512])
        prep = g.ps(st, "att_prep", [P, 512])
        aw = k["ada_w"].rearrange("(q p) n -> p q n", p=P)
        ada_b = vec[:, VEC["ada_b"]:VEC["ada_b"] + 96]
        PIECES_ADA = KT // 2
        ADA_BUF = 4
        ADA_RAW = 6
        araw = [g.sb(st, f"att_ada_raw{j}", [P, 2, 512]) for j in range(ADA_RAW)]
        ahi = [g.sb(st, f"att_ada_hi{j}", [P, 2, 512], F32R) for j in range(ADA_BUF)]
        alo = [g.sb(st, f"att_ada_lo{j}", [P, 2, 512], F32R) for j in range(ADA_BUF)]
        rows = [buf[0:4, :] for buf in (sq, rms, normed, turned)]
        landed = [f"ada_landed{j}" for j in range(ADA_RAW)]
        names = (*landed, "ada_hi", "ada_lo", "ada_used", "ada_rows", "ada_cols", "ada_mod", "const_in", "bias_done", "qkv_a_in", "qkv_b_in", "qs_done", "sq_done", "ss_done", "rms_done",
                 "inv_done", "normed_done", "swapped", "turn_parts", "prep_done", "scored", "maxed", "neg_done", "exp_done",
                 "recip_done", "prob_done", "tp_done", "tp_act", "tp_dve", "pv_done", "out_copied")
        S = dict(zip(names, g.sems(st, *["att_" + n for n in names])))
        gains_done, bias_in = g.sems(st, "att_setup_done", "att_bias_in")
        with nc.Block() as block:

            @block.sync
            def _(sp):
                for dst, name in ((window, "window"), (rope, "rope"), (swap, "rope_swap"), (head_ones, "head_ones")):
                    sp.dma_start(dst[:], k[name]).then_inc(S["const_in"], 16)
                for h in range(AH):
                    for half in range(2):
                        off = RPB_PAD + h * RPB_R * RPB_C + (1 - half) * RPB_C + NAW - GRID
                        src = bass.AP(rpb.tensor, off, [[1, GRID], [RPB_C, BIAS_ROWS], [1, GRID]])
                        sp.dma_start(bias[half * HD:(half + 1) * HD, h, :, :], src).then_inc(bias_in, 16)
                sp.wait_ge(S["const_in"], 64)
                sp.wait_ge(bias_in, 16 * 2 * AH)

            @block.vector
            def _(dve):
                dve.tensor_scalar(gains[:, 0:1], vec[:, VEC["q_gain"]:VEC["q_gain"] + 1], float(HD) ** -0.5, None, ALU.mult)
                dve.tensor_copy(gains[:, 1:2], vec[:, VEC["k_gain"]:VEC["k_gain"] + 1]).then_inc(gains_done, 1)
                dve.wait_ge(gains_done, 1)

        def unit(u):
            return u // 8, u // 4 % 2, u % 4

        def keys_in(sp, dst, rows, sem, lo=0, hi=P):
            sp.dma_start(dst[lo:hi, 0:LAT], f_dram[rows, CTX:TOK]).then_inc(sem, 16)
            sp.dma_start(dst[lo:hi, LAT:KEYS], f_dram[rows, 0:CTX]).then_inc(sem, 16)

        with nc.Fori(0, 4) as i:
            with nc.Block() as block:

                @block.sync
                def _(sp):
                    sem = S["qkv_a_in"]
                    sp.dma_start(raw["aq"][:], f_dram[bass.ds(i * P + QA * P, P), CTX:TOK]).then_inc(sem, 16)
                    keys_in(sp, raw["ak"], bass.ds(i * P + KA * P, P), sem)
                    keys_in(sp, raw["av"], bass.ds(i * P + VA * P, P), sem)
                    sem = S["qkv_b_in"]
                    sp.dma_start(raw["bq"][:], f_dram[bass.ds(i * P + QB * P, P), CTX:TOK]).then_inc(sem, 16)
                    for half in range(2):
                        kv = (i // 2) * HD
                        keys_in(sp, raw["bk"], bass.ds(kv + KVB * P, HD), sem, half * HD, half * HD + HD)
                        keys_in(sp, raw["bv"], bass.ds(kv + (KVB + 1) * P, HD), sem, half * HD, half * HD + HD)
                    for q in range(4 * PIECES_ADA):
                        if q >= ADA_RAW:
                            sp.wait_ge(S["ada_lo"], q - ADA_RAW + 1)
                        blk, pc = q // PIECES_ADA, q % PIECES_ADA
                        cols = bass.ds(i * 2048 + (ADA_FIRST * D + blk * 512), 512)
                        sp.dma_start(araw[q % ADA_RAW][:], aw[:, 2 * pc:2 * pc + 2, cols]).then_inc(S[landed[q % ADA_RAW]], 16)

                @block.gpsimd
                def _(pool):
                    for hh in range(2):
                        table = bias[:, bass.ds(i * 2 + hh, 1), :, :].rearrange("p o a b -> p (o a) b")
                        pool.tensor_tensor(flip(bias_now[:, hh, :, :]), table,
                                           flip(window[:].unsqueeze(1).to_broadcast([P, BIAS_ROWS, GRID])),
                                           ALU.add).then_inc(S["bias_done"], 1)

                def scores(pe, u):
                    grp, hh, t = unit(u)
                    if u == 0:
                        pe.wait_ge(S["qs_done"], 1)
                    if u == 8:
                        pe.wait_ge(S["prep_done"], 3)
                    if u >= 2:
                        pe.wait_ge(S["exp_done"], u - 1)
                    q, kk = ((qs, raw["ak"]), (bqn, bkn))[grp]
                    hp = slice(hh * HD, hh * HD + HD)
                    pe.matmul(sc[u % 2][:, 0:LAT], q[hp, t * P:(t + 1) * P], kk[hp, 0:LAT], start=True, stop=True)
                    pe.matmul(sc[u % 2][:, LAT:KEYS], q[hp, t * P:(t + 1) * P], kk[hp, LAT:KEYS], start=True,
                              stop=True).then_inc(S["scored"], 1)

                def turn(pe, j, src):
                    if j >= 1:
                        pe.wait_ge(S["tp_act"], j)
                        pe.wait_ge(S["tp_dve"], j)
                    for b in range(KEY_TILES):
                        m = pe.transpose(tp[:, b // 3, b % 3 * P:(b % 3 + 1) * P], src[:, b * P:(b + 1) * P], ident[:])
                    m.then_inc(S["tp_done"], 1)

                def weigh(pe, head):
                    grp, hh = head // 2, head % 2
                    hp = slice(hh * HD, hh * HD + HD)
                    pe.wait_ge(S["tp_act"], 2 + 4 * head + 4)
                    pe.wait_ge(S["tp_dve"], 2 + 4 * head + 4)
                    if head == 2:
                        pe.wait_ge(S["out_copied"], 1)
                    for b in range(KEY_TILES):
                        m = pe.matmul(outp[hp, :], vtok[grp][:, b, hp], pt[head % 2][:, b, :], start=(b == 0),
                                      stop=(b == KEY_TILES - 1))
                    m.then_inc(S["pv_done"], 1)

                def prep_pe(pe, u):
                    if u % 2 == 1 and u // 2 < 3:
                        _, _, n, _ = PIECES[u // 2]
                        pe.wait_ge(S["sq_done"], u // 2 + 1)
                        if u > 1:
                            pe.wait_ge(S["prep_done"], u // 2)
                        pe.matmul(prep[:, 0:n], head_ones[:], sq[:, 0:n], start=True, stop=True).then_inc(S["ss_done"], 1)
                    if u % 2 == 0 and 0 < u // 2 <= 3 and PIECES[u // 2 - 1][3]:
                        pe.wait_ge(S["normed_done"], u // 2)
                        pe.matmul(prep[:, :], swap[:], normed[:], start=True, stop=True).then_inc(S["swapped"], 1)

                def ada_of(u):
                    return range(4 * (u - 7), 4 * (u - 7) + 4) if 7 <= u < 15 else ()

                def ada_pe(pe, u):
                    for q in ada_of(u):
                        blk, pc = q // PIECES_ADA, q % PIECES_ADA
                        if pc == 0:
                            pe.wait_ge(S["ada_rows"] if blk else S["prep_done"], blk or 3)
                        pe.wait_ge(S["ada_lo"], q + 1)
                        for kk in range(2):
                            for part, w in enumerate((ahi, alo)):
                                m = pe.matmul(prep[:, :], cond[:, 2 * pc + kk, :], w[q % ADA_BUF][:, kk, :],
                                              start=(pc == 0 and kk == 0 and part == 0),
                                              stop=(pc == PIECES_ADA - 1 and kk == 1 and part == 1))
                        m.then_inc(S["ada_used"], 1)

                def ada_dve(dve, u):
                    if u >= 9 and u % 2:
                        blk = (u - 9) // 2
                        dve.wait_ge(S["ada_used"], (blk + 1) * PIECES_ADA)
                        dve.tensor_copy(rows[blk], prep[0:4, :]).then_inc(S["ada_rows"], 1)
                    for q in ada_of(u):
                        dve.wait_ge(S["ada_hi"], q + 1)
                        dve.tensor_tensor(alo[q % ADA_BUF][:], araw[q % ADA_RAW][:], ahi[q % ADA_BUF][:].bitcast(F32),
                                          ALU.subtract).then_inc(S["ada_lo"], 1)

                def ada_act(act, u):
                    for q in ada_of(u):
                        act.wait_ge(S[landed[q % ADA_RAW]], 16 * (q // ADA_RAW + 1))
                        if q >= ADA_BUF:
                            act.wait_ge(S["ada_used"], q - ADA_BUF + 1)
                        act.copy(ahi[q % ADA_BUF][:], araw[q % ADA_RAW][:]).then_inc(S["ada_hi"], 1)

                @block.tensor
                def _(pe):
                    pe.wait_ge(S["qkv_a_in"], 80)
                    turn(pe, 0, raw["av"])
                    pe.wait_ge(S["qkv_b_in"], 144)
                    turn(pe, 1, raw["bv"])
                    scores(pe, 0)
                    scores(pe, 1)
                    for u in range(UNITS):
                        prep_pe(pe, u)
                        if u + 2 < UNITS:
                            scores(pe, u + 2)
                        ada_pe(pe, u)
                        pe.wait_ge(S["prob_done"], u + 1)
                        turn(pe, u + 2, prob[u % 2])
                        if u % 4 == 0 and u:
                            weigh(pe, u // 4 - 1)
                    pe.wait_ge(S["ada_rows"], 4)
                    for j in range(16):
                        m = pe.matmul(prep[:, 2 * j:2 * j + 2], rows[j // 4][:, j % 4 * P:(j % 4 + 1) * P], sel[:], start=True, stop=True)
                    m.then_inc(S["ada_cols"], 1)
                    weigh(pe, 3)

                @block.scalar
                def _(act):
                    act.wait_ge(S["qkv_a_in"], 80)
                    act.mul(qs[:], raw["aq"][:], float(HD) ** -0.5).then_inc(S["qs_done"], 1)

                    def copy_out(j):
                        act.wait_ge(S["tp_done"], j + 1)
                        if j < 2:
                            dst = vtok[j][:, 0:3, :]
                        else:
                            head, t = (j - 2) // 4, (j - 2) % 4
                            if head >= 2 and t == 0:
                                act.wait_ge(S["pv_done"], head - 1)
                            dst = pt[head % 2][:, 0:3, t * P:(t + 1) * P]
                        act.copy(dst, tp[:, 0, 0:3 * P].rearrange("p (a b) -> p a b", a=3)).then_inc(S["tp_act"], 1)

                    copy_out(0)
                    copy_out(1)
                    for u in range(UNITS):
                        act.wait_ge(S["neg_done"], u + 1)
                        if u >= 2:
                            act.wait_ge(S["tp_done"], u + 1)
                        act.activation(prob[u % 2][:], sc[u % 2][:, 0:KEYS], ACT.Exp, bias=nm[:, u:u + 1],
                                       accum_out=den[:, u:u + 1]).then_inc(S["exp_done"], 1)
                        if u >= 1:
                            copy_out(u + 1)
                        ada_act(act, u + 1)
                        j = u // 2
                        if u % 2 == 0 and j < 3:
                            name, c0, n, _ = PIECES[j]
                            if j == 0:
                                act.wait_ge(S["qkv_b_in"], 144)
                            act.activation(sq[:, 0:n], raw["b" + name][:, c0:c0 + n], ACT.Square).then_inc(S["sq_done"], 1)
                        if u % 2 == 1 and j < 3:
                            n = PIECES[j][2]
                            act.wait_ge(S["ss_done"], j + 1)
                            act.activation(rms[:, 0:n], prep[:, 0:n], ACT.Sqrt, bias=eps[:, 0:1],
                                           scale=1.0 / HD).then_inc(S["rms_done"], 1)
                    copy_out(UNITS + 1)

                @block.vector
                def _(dve):
                    def copy_out(j):
                        dve.wait_ge(S["tp_done"], j + 1)
                        if j < 2:
                            dst = vtok[j][:, 3:6, :]
                        else:
                            head, t = (j - 2) // 4, (j - 2) % 4
                            if head >= 2 and t == 0:
                                dve.wait_ge(S["pv_done"], head - 1)
                            dst = pt[head % 2][:, 3:6, t * P:(t + 1) * P]
                        dve.tensor_copy(dst, tp[:, 1, 0:3 * P].rearrange("p (a b) -> p a b", a=3)).then_inc(S["tp_dve"], 1)

                    def maximum(u):
                        grp, hh, t = unit(u)
                        dve.wait_ge(S["scored"], u + 1)
                        if grp == 0:
                            if u == 0:
                                dve.wait_ge(S["bias_done"], 2)
                            s = sc[u % 2][:, 0:LAT]
                            b = bias_now[:, hh, 6 - 2 * t:14 - 2 * t, :].rearrange("p a b -> p (a b)")
                            dve.tensor_tensor_reduce(out=s, in0=s, in1=b, scale=1.0, scalar=-3e38, op0=ALU.add, op1=ALU.max,
                                                     accum_out=mx[:, u, 0:1]).then_inc(S["maxed"], 1)
                            dve.reduce_max(mx[:, u, 1:2], sc[u % 2][:, LAT:KEYS], AX_X).then_inc(S["maxed"], 1)
                            dve.wait_ge(S["maxed"], 2 * u + 2)
                            dve.tensor_reduce(nm[:, u:u + 1], mx[:, u, :], AX_X, ALU.max, negate=True).then_inc(S["neg_done"], 1)
                        else:
                            dve.tensor_reduce(nm[:, u:u + 1], sc[u % 2][:, 0:KEYS], AX_X, ALU.max,
                                              negate=True).then_inc(S["neg_done"], 1)

                    def divide(u):
                        dve.wait_ge(S["exp_done"], u + 1)
                        dve.reciprocal(rden[:, u:u + 1], den[:, u:u + 1]).then_inc(S["recip_done"], 1)
                        dve.wait_ge(S["recip_done"], u + 1)
                        dve.tensor_scalar(prob[u % 2][:], prob[u % 2][:], rden[:, u:u + 1], None, ALU.mult).then_inc(S["prob_done"], 1)

                    def prep_dve(u):
                        j = u // 2
                        if u % 2 == 1 and j < 3:
                            name, c0, n, turned_too = PIECES[j]
                            dve.wait_ge(S["rms_done"], j + 1)
                            if j:
                                dve.wait_ge(S["prep_done"], j)
                            dve.reciprocal(sq[:, 0:n], rms[:, 0:n]).then_inc(S["inv_done"], 1)
                            dve.wait_ge(S["inv_done"], j + 1)
                            dst = normed[:, 0:n] if turned_too else bkn[:, c0:c0 + n]
                            gcol = 0 if name == "q" else 1
                            dve.scalar_tensor_tensor(dst, raw["b" + name][:, c0:c0 + n], gains[:, gcol:gcol + 1], sq[:, 0:n],
                                                     ALU.mult, ALU.mult).then_inc(S["normed_done" if turned_too else "prep_done"], 1)
                        j = u // 2 - 1
                        if u % 2 == 0 and 0 <= j < 3 and PIECES[j][3]:
                            dst = (bqn if PIECES[j][0] == "q" else bkn)[:, 0:LAT]
                            dve.wait_ge(S["normed_done"], j + 1)
                            dve.tensor_tensor(dst, normed[:], rope[:, 0, :], ALU.mult).then_inc(S["turn_parts"], 1)
                            dve.wait_ge(S["swapped"], j + 1)
                            dve.tensor_tensor(turned[:], prep[:, :], rope[:, 1, :], ALU.mult).then_inc(S["turn_parts"], 1)
                            dve.wait_ge(S["turn_parts"], 2 * j + 2)
                            dve.tensor_tensor(dst, dst, turned[:], ALU.add).then_inc(S["prep_done"], 1)

                    def copy_result(grp):
                        dve.wait_ge(S["pv_done"], 2 * grp + 2)
                        dve.tensor_copy(mix[:, bass.ds(i + 4 * grp, 1), :].rearrange("p a n -> p (a n)"),
                                        outp[:]).then_inc(S["out_copied"], 1)

                    copy_out(0)
                    copy_out(1)
                    for u in range(UNITS + 1):
                        if u < UNITS:
                            maximum(u)
                        if u >= 1:
                            divide(u - 1)
                        if u >= 2:
                            copy_out(u)
                        if u == 10:
                            copy_result(0)
                        if u < UNITS:
                            ada_dve(dve, u)
                        prep_dve(u)
                    copy_out(UNITS + 1)
                    dve.wait_ge(S["ada_cols"], 1)
                    at = bass.ds(i * 16 + ADA_FIRST * KT, 16)
                    dve.tensor_tensor(mod[:, :, at], prep[:, 0:32].rearrange("p (j s) -> p s j", s=2),
                                      ada_b[:, bass.ds(i * 16 + ADA_FIRST * KT, 16)].unsqueeze(1).to_broadcast([P, 2, 16]),
                                      ALU.add).then_inc(S["ada_mod"], 1)
                    copy_result(1)
                    dve.wait_ge(S["out_copied"], 2)
                    dve.wait_ge(S["ada_mod"], 1)

            clear(nc, S)


CHUNKS = TOK // CH
DECAY = float(np.exp(-0.5))
SL_B, SL_K, SL_BH, SL_KH, SL_A, SL_V = ((0, 0), (0, 1), (1, 0), (1, 1), (2, 0), (2, 1))


def rwkv_lora(g, st, k, f_dram, vec):
    nc = g.nc
    tw = g.sb(st, "rw_tanh_wd", [P, TOK])
    ta = g.sb(st, "rw_ad", [P, TOK])
    sg = g.sb(st, "rw_sig_gd", [P, 2, LAT])
    with ExitStack() as s2:
        pad = [g.sb(s2, f"rw_pad{j}", [P, TOK + 3]) for j in range(4)]
        mixed = g.sb(s2, "rw_mixed", [P, 4, TOK])
        om = g.sb(s2, "rw_one_minus_mu", [P, 4])
        sems = g.sems(s2, "lora_in", "lora_padded", "lora_dve", "lora_scaled", "lora_mixed")
        came, padded, link_sem, scaled, mixed_done = sems
        c1 = slice(1, CTX + 1)
        l1 = slice(CTX + 2, TOK + 2)
        with nc.Block() as block:

            @block.sync
            def _(sp):
                sp.wait_ge(padded, 4)
                for j, t in enumerate((RW_WD, RW_AD)):
                    sp.dma_start(pad[j][:, c1], f_dram[t * P:(t + 1) * P, 0:CTX]).then_inc(came, 16)
                    sp.dma_start(pad[j][:, l1], f_dram[t * P:(t + 1) * P, CTX:TOK]).then_inc(came, 16)
                sp.dma_start(pad[2][:, l1], f_dram[RW_GD * P:(RW_GD + 1) * P, CTX:TOK]).then_inc(came, 16)
                sp.dma_start(pad[3][0:32, l1], f_dram[(RW_GD + 1) * P + 96:(RW_GD + 2) * P, CTX:TOK]).then_inc(came, 16)

            @block.gpsimd
            def _(pool):
                for j in range(4):
                    pool.memset(pad[j][:], 0.0).then_inc(padded, 1)

            @block.vector
            def _(dve):
                link = Link(dve, link_sem)
                mu = vec[:, VEC["mu_w"]:VEC["mu_w"] + 2]
                dve.tensor_scalar(om[:, 0:2], mu, -1.0, 1.0, ALU.mult, ALU.add)
                g0, g1 = vec[:, VEC["mu_g0"]:VEC["mu_g0"] + 2], vec[:, VEC["mu_g1"]:VEC["mu_g1"] + 2]
                link(dve.tensor_tensor(om[:, 2:4], g0, g1, ALU.add))
                link(dve.tensor_scalar(om[:, 2:4], om[:, 2:4], -1.0, 1.0, ALU.mult, ALU.add))
                dve.wait_ge(came, 16 * 6)
                for j in range(2):
                    m = vec[:, VEC["mu_w"] + j:VEC["mu_w"] + j + 1]
                    for sl, o in ((c1, slice(0, CTX)), (l1, slice(CTX, TOK))):
                        link(dve.tensor_scalar(mixed[:, j, o], pad[j][:, sl], om[:, j:j + 1], None, ALU.mult))
                        for half, step in ((0, -1), (1, 1)):
                            hp = slice(half * HD, half * HD + HD)
                            nb = pad[j][hp, sl.start + step:sl.stop + step]
                            link(dve.scalar_tensor_tensor(mixed[hp, j, o], nb, m[hp], mixed[hp, j, o], ALU.mult, ALU.add))
                for j in (2, 3):
                    link(dve.tensor_scalar(mixed[:, j, 0:LAT], pad[j][:, l1], om[:, j:j + 1], None, ALU.mult))
                    for name, step in (("mu_g0", -1), ("mu_g1", 1)):
                        m = vec[:, VEC[name] + j - 2:VEC[name] + j - 1]
                        link(dve.scalar_tensor_tensor(mixed[:, j, 0:LAT], pad[j][:, l1.start + step:l1.stop + step], m,
                                                      mixed[:, j, 0:LAT], ALU.mult, ALU.add))
                dve.nop().then_inc(mixed_done, 1)

            @block.scalar
            def _(act):
                act.wait_ge(mixed_done, 1)
                for dst, j, fn in ((tw, 0, ACT.Tanh), (ta, 1, ACT.Copy)):
                    act.activation(dst[0:HD, :], mixed[0:HD, j, :], fn)
                    for o in (slice(0, CTX), slice(CTX, TOK)):
                        act.activation(flip(dst[HD:P, o]), mixed[HD:P, j, o], fn)
                for j in (0, 1):
                    act.activation(sg[:, j, :], mixed[:, 2 + j, 0:LAT], ACT.Sigmoid)

    return tw, ta, sg


def flip(ap):
    return ap[tuple([slice(None)] * (len(ap.shape) - 1) + [slice(None, None, -1)])]


class Link:

    def __init__(self, eng, sem):
        self.eng, self.sem, self.n = eng, sem, 0

    def __call__(self, ins):
        self.n += 1
        ins.then_inc(self.sem, 1)
        self.eng.wait_ge(self.sem, self.n)


def rwkv(g, k, f_dram, mix, ident, vec, eps):
    nc = g.nc
    with ExitStack() as st:
        tw, ta, sg = rwkv_lora(g, st, k, f_dram, vec)
        upper = g.sb(st, "rw_upper", [P, 3, CH])
        diag2 = upper[:, 2, :]
        levels = g.sb(st, "rw_levels", [P, NLEV + 1, P])
        head_ones = g.sb(st, "rw_head_ones", [P, P])
        starts = g.sb(st, "rw_starts", [P, CHUNKS, CH + 1])
        lnx_eps = g.sb(st, "rw_lnx_eps", [P, 1])
        raw = g.sb(st, "rw_raw", [P, 3, TOK + 3])
        pv = g.sb(st, "rw_pair_vec", [P, NPV])
        om = g.sb(st, "rw_pair_om", [P, 7])
        w2 = g.sb(st, "rw_w2_pair", [P, 2, P])
        g2 = g.sb(st, "rw_g2_pair", [P, 2, P])
        pv_next = g.sb(st, "rw_pair_vec_next", [P, NPV])
        g2_next = g.sb(st, "rw_g2_next", [P, 2, P])
        stacks = [[g.sb(st, f"rw_{n}{d}", [P, CHUNKS, 2, CH]) for n in ("b_k", "bh_kh", "a_v")] for d in range(2)]
        AR = [g.sb(st, f"rw_a_r{d}", [P, CHUNKS, 2, 2, CH]) for d in range(2)]
        R = [g.sb(st, f"rw_r{d}", [P, CHUNKS, CH]) for d in range(2)]
        wd = [g.sb(st, f"rw_decay{d}", [P, CHUNKS, CH + 1]) for d in range(2)]
        aa = [g.sb(st, f"rw_iclr{d}", [P, TOK]) for d in range(2)]
        cum = [g.sb(st, f"rw_cum{d}", [P, CHUNKS, CH + 1]) for d in range(2)]
        bonus = g.sb(st, "rw_bonus", [P, LAT])
        ysum = g.sb(st, "rw_y", [P, LAT])
        tmp = g.sb(st, "rw_tmp", [P, LAT])
        Em = [g.sb(st, f"rw_pairs{d}", [P, CPB, 2, 2, CH]) for d in range(2)]
        BK = [g.sb(st, f"rw_bk_tok{d}", [P, CPB, P]) for d in range(2)]
        UV = [g.sb(st, f"rw_uv_tok{d}", [P, CPB, P]) for d in range(2)]
        Ms = [g.sb(st, f"rw_m{h}", [P, CPB, CH]) for h in range(2)]
        Ml = [[buf[:, 0:CPB * P].rearrange("p (c n) -> p c n", n=P) for buf in (wd[h][:].rearrange("p c n -> p (c n)"), aa[h][:])]
              for h in range(2)]
        X = [g.sb(st, f"rw_inverse{h}", [P, CPB, P]) for h in range(2)]
        T = [g.sb(st, f"rw_inverse_turned{h}", [P, CPB, P]) for h in range(2)]
        Y1 = [g.sb(st, f"rw_half{h}", [P, CPB, P]) for h in range(2)]
        AM = [g.sb(st, f"rw_a_mv_tok{h}", [P, CPB, P]) for h in range(2)]
        Wt = [g.sb(st, f"rw_w_tok{h}", [P, CPB, CH]) for h in range(2)]
        Gt = [g.sb(st, f"rw_g{d}", [P, CPB, CH]) for d in range(2)]
        Dg = [g.sb(st, f"rw_diag{d}", [P, CPB, CH]) for d in range(2)]
        Qt = [g.sb(st, f"rw_q{d}", [P, CPB, CH]) for d in range(2)]
        St = [g.sb(st, f"rw_state{d}", [P, CHUNKS, CH + 1]) for d in range(2)]
        bank = [g.ps(st, f"rw_ps{j}", [P, 1024]) for j in range(4)]

        def bk(i, j):
            return bank[i][:, j * 512:j * 512 + 512]

        kinds = ("raw_in", "pair_in", "padded", "om_done", "scaled", "mixed", "gates", "sig_done", "exp_done", "sqk_done", "ss_done",
                 "ssqrt_done", "rk_done", "rk_sum", "kk_done", "k_done", "feat_link", "feat_done", "pool_link",
                 "mean_done", "cent_done", "csq_done", "var_done", "std_done", "gate_done", "mixed_out", "read_link")
        S = {n: g.sems(st, "rw_" + n)[0] for n in kinds}
        per_dir = ("e_done", "e_out", "turned", "turned_out", "diag", "gq_done", "gq_out", "state_done", "state_out",
                   "y_done", "y_out", "r_done")
        per_head = ("m_done", "m_out", "mv_done", "mv_out", "paired", "seeded", "turned_x", "levels", "half_done", "half_out",
                    "join_done", "joined", "wu_done", "wu_out")
        SD = [{n: g.sems(st, f"rw_{n}{d}")[0] for n in per_dir} for d in range(2)]
        SG = [{n: g.sems(st, f"rw_{n}_h{h}")[0] for n in per_head} for h in range(2)]

        with nc.Block() as block:

            @block.sync
            def _(sp):
                for dst, name in ((upper, "mask_upper"), (levels, "mask_levels"), (head_ones, "head_ones")):
                    sp.dma_start(dst[:], k[name]).then_inc(S["raw_in"], 16)
                sp.wait_ge(S["padded"], 2)
                load_pair(sp, k, f_dram, 0, {"raw": raw, "w2": w2, "pv_next": pv_next, "g2_next": g2_next}, S["pair_in"])
                sp.wait_ge(S["raw_in"], 48)

            @block.vector
            def _(dve):
                dve.memset(raw[:], 0.0).then_inc(S["padded"], 1)
                dve.memset(g2_next[:], 0.0).then_inc(S["padded"], 1)
                dve.memset(starts[:], 0.0).then_inc(S["feat_link"], 1)
                dve.wait_ge(S["feat_link"], 1)
                dve.memset(starts[:, :, 0:1], 1.0)
                dve.memset(lnx_eps[:], LNX_EPS)
                dve.memset(AR[0][:], 0.0)

            @block.gpsimd
            def _(pool):
                pool.memset(AR[1][:], 0.0)

        clear(nc, {n: S[n] for n in ("raw_in", "pair_in", "padded", "feat_link")})

        with nc.Fori(0, PAIRS) as p:
            pair_features(g, k, p, locals())
            pair_chunks(g, k, f_dram, p, locals())
            pair_readout(g, p, mix, locals())
            clear(nc, {**S, **{f"{n}{d}": s for d in range(2) for n, s in [*SD[d].items(), *SG[d].items()]}})


def load_pair(sp, k, f_dram, p, L, loaded):
    raw, w2, pv_next, g2_next = (L[n] for n in ("raw", "w2", "pv_next", "g2_next"))
    for j, t in enumerate((RW_K, RW_V, RW_R)):
        slot = (1, 2, 0)[j]
        sp.dma_start(raw[:, slot, 1:CTX + 1], f_dram[bass.ds(p * P + t * P, P), 0:CTX]).then_inc(loaded, 16)
        sp.dma_start(raw[:, slot, CTX + 2:TOK + 2], f_dram[bass.ds(p * P + t * P, P), CTX:TOK]).then_inc(loaded, 16)
    sp.dma_start(pv_next[:], k["pair_vectors"][bass.ds(p, 1)].rearrange("a p n -> (a p) n")).then_inc(loaded, 16)
    sp.dma_start(w2[:, 0, :], k["rw_w2"][:, bass.ts(p, P)]).then_inc(loaded, 16)
    sp.dma_start(w2[:, 1, :], k["rw_a2"][:, bass.ts(p, P)]).then_inc(loaded, 16)
    sp.dma_start(g2_next[:, 0, :], k["rw_g2"][0:P, bass.ts(p, P)]).then_inc(loaded, 16)
    sp.dma_start(g2_next[0:32, 1, :], k["rw_g2"][P:GLORA, bass.ts(p, P)]).then_inc(loaded, 16)
    sp.wait_ge(loaded, 11 * 16)


def pair_features(g, k, p, L):
    nc = g.nc
    S, SD, St, stacks, AR, R, wd, aa, cum, raw, pv, om, w2, g2 = (L[n] for n in ("S", "SD", "St", "stacks", "AR", "R", "wd", "aa", "cum", "raw", "pv", "om", "w2", "g2"))
    tw, ta, sg, bonus, ysum, tmp, starts, head_ones, bk, bank, f_dram = (
        L[n] for n in ("tw", "ta", "sg", "bonus", "ysum", "tmp", "starts", "head_ones", "bk", "bank", "f_dram"))
    pv_next, g2_next = L["pv_next"], L["g2_next"]
    c1, l1 = slice(1, CTX + 1), slice(CTX + 2, TOK + 2)
    lat = slice(CTX // CH, CHUNKS)
    cols = ((c1, slice(0, CTX // CH)), (l1, lat))
    full = slice(0, CHUNKS)
    arr = lambda d, s, c=full: R[d][:, c, :] if s is None else stacks[d][s[0]][:, c, s[1] ^ d, :]
    chunks = lambda ap: ap.rearrange("p (c n) -> p c n", n=CH)
    col = lambda n, d=0: pv[:, PV[n] + d:PV[n] + d + 1]
    RKV = (None, SL_K, SL_V)
    line = lambda buf: buf[:].rearrange("p c n -> p (c n)")
    with nc.Block() as block:

        @block.scalar
        def _(act):
            act.wait_ge(S["om_done"], 1)
            for j in (1, 2, 0):
                for d in range(2):
                    for src, dst in cols:
                        x = raw[:, j, src]
                        act.activation(arr(d, RKV[j], dst), chunks(flip(x) if d else x), ACT.Copy,
                                       scale=om[:, 2 * j + d:2 * j + d + 1]).then_inc(S["scaled"], 1)
                if j == 1:
                    for d in range(2):
                        act.wait_ge(S["mixed"], 2 * d + 2)
                        act.activation(arr(d, SL_A), arr(d, SL_K), ACT.Square, scale=col("k_k")).then_inc(S["sqk_done"], 1)
            for d in range(2):
                act.wait_ge(S["ss_done"], d + 1)
                act.activation(arr(d, SL_B), chunks(bank[2 * d][:, 0:TOK]), ACT.Sqrt).then_inc(S["ssqrt_done"], 1)
            for d in range(2):
                act.wait_ge(S["gates"], d + 1)
                act.activation(aa[d][:], bank[2 * d + 1][:, 0:TOK], ACT.Sigmoid, bias=col("a0", d)).then_inc(S["sig_done"], 1)
            for d in range(2):
                act.wait_ge(S["gates"], d + 3)
                act.activation(wd[d][:, :, 1:], chunks(bank[2 * d][:, 0:TOK]), ACT.Sigmoid,
                               bias=col("w0", d)).then_inc(S["sig_done"], 1)
            for d in range(2):
                act.wait_ge(S["sig_done"], 3 + d)
                act.activation(St[d][:, :, 1:], wd[d][:, :, 1:], ACT.Exp, scale=-DECAY).then_inc(S["exp_done"], 1)
                act.wait_ge(S["exp_done"], 2 * d + 1)
                act.activation(wd[d][:, :, 1:], wd[d][:, :, 1:], ACT.Exp, scale=DECAY).then_inc(S["exp_done"], 1)
            for d in range(2):
                act.wait_ge(S["feat_done"], 3 * d + 2)
                for h in range(2):
                    hp = slice(h * HD, h * HD + HD)
                    act.copy(AR[d][hp, :, h, 0, :], arr(d, SL_A)[hp])
                act.wait_ge(SD[d]["r_done"], 1)
                for h in range(2):
                    hp = slice(h * HD, h * HD + HD)
                    act.copy(AR[d][hp, lat, h, 1, :], R[d][hp, lat, :])

        @block.tensor
        def _(pe):
            def gate(d, j, src):
                hp = slice(d * HD, d * HD + HD)
                out = bank[2 * d + j]
                pe.matmul(out[:, 0:512], w2[hp, j, :], src[hp, 0:512], start=True, stop=True)
                pe.matmul(out[:, 512:TOK], w2[hp, j, :], src[hp, 512:TOK], start=True, stop=True).then_inc(S["gates"], 1)

            for d in range(2):
                gate(d, 1, ta)
            for d in range(2):
                pe.wait_ge(S["sqk_done"], d + 1)
                pe.matmul(bank[2 * d][:, 0:512], head_ones[:], arr(d, SL_A, slice(0, 8)), start=True, stop=True)
                pe.matmul(bank[2 * d][:, 512:TOK], head_ones[:], arr(d, SL_A, slice(8, CHUNKS)), start=True,
                          stop=True).then_inc(S["ss_done"], 1)
            for d in range(2):
                pe.wait_ge(S["ssqrt_done"], d + 1)
                gate(d, 0, tw)
            for d in range(2):
                pe.wait_ge(S["rk_done"], d + 1)
                pe.wait_ge(S["sig_done"], d + 1)
                pe.matmul(bank[2 * d + 1][:, 0:512], head_ones[:], arr(d, SL_KH, lat), start=True,
                          stop=True).then_inc(S["rk_sum"], 1)

        @block.gpsimd
        def _(pool):
            link = Link(pool, S["pool_link"])
            link(pool.memset(ysum[:], 0.0))
            link(pool.tensor_copy(g2[:], g2_next[:]))
            for d in range(2):
                link(pool.memset(St[d][:, :, 0:1], 0.0))
                link(pool.memset(wd[d][:, :, 0:1], 0.0))
            pool.wait_ge(S["mixed"], 12)
            for d in range(2):
                pool.wait_ge(S["sig_done"], d + 1)
                link(pool.tensor_scalar(cum[d][:, :, 1:CH + 1], chunks(aa[d][:]), col("k_a"), om[:, 6:7], ALU.mult, ALU.add))
                pool.wait_ge(S["kk_done"], d + 1)
                pool.tensor_tensor(arr(d, SL_K), arr(d, SL_K), cum[d][:, :, 1:CH + 1], ALU.mult).then_inc(S["k_done"], 1)
            for d in range(2):
                pool.wait_ge(S["feat_done"], 3 * d + 1)
                pool.tensor_tensor(arr(d, None, lat), arr(d, None, lat), cum[d][:, lat, 1:CH + 1], ALU.mult).then_inc(SD[d]["r_done"], 1)
                last = cum[d][:, :, CH:CH + 1].to_broadcast([P, CHUNKS, CH])
                pool.wait_ge(S["feat_done"], 3 * d + 2)
                pool.tensor_tensor(arr(d, SL_BH), arr(d, SL_B), last, ALU.mult)
                pool.wait_ge(S["feat_done"], 3 * d + 3)
                pool.wait_ge(S["rk_sum"], d + 1)
                pool.tensor_tensor(arr(d, SL_KH), arr(d, SL_K), last, ALU.mult)

        @block.vector
        def _(dve):
            link = Link(dve, S["feat_link"])
            link(dve.tensor_copy(pv[:], pv_next[:]))
            dve.tensor_scalar(om[:, 6:7], col("k_a"), -1.0, 1.0, ALU.mult, ALU.add)
            dve.tensor_scalar(om[:, 0:6], pv[:, 0:6], -1.0, 1.0, ALU.mult, ALU.add).then_inc(S["om_done"], 1)
            dve.wait_ge(S["om_done"], 1)
            n = 0
            for j in (1, 2, 0):
                for d in range(2):
                    for src, dst in cols:
                        n += 1
                        step = 1 if d else -1
                        x = raw[:, j, src.start + step:src.stop + step]
                        dve.wait_ge(S["scaled"], n)
                        y = arr(d, RKV[j], dst)
                        dve.scalar_tensor_tensor(y, chunks(flip(x) if d else x), pv[:, 2 * j + d:2 * j + d + 1], y, ALU.mult, ALU.add).then_inc(S["mixed"], 1)
            dve.wait_ge(S["mixed"], 12)
            for d in range(2):
                f3 = lambda s: arr(d, s)
                dve.wait_ge(S["ssqrt_done"], d + 1)
                link(dve.tensor_scalar(arr(d, SL_B), arr(d, SL_B), 1e-12, None, ALU.max))
                link(dve.reciprocal(arr(d, SL_B), arr(d, SL_B)))
                dve.scalar_tensor_tensor(arr(d, SL_A), arr(d, SL_K), col("k_k"), arr(d, SL_B), ALU.mult, ALU.mult).then_inc(S["kk_done"], 1)
                dve.wait_ge(S["kk_done"], d + 1)
                dve.wait_ge(S["sig_done"], d + 1)
                dve.tensor_tensor(arr(d, SL_B), arr(d, SL_A), chunks(aa[d][:]), ALU.mult)
                dve.wait_ge(S["k_done"], d + 1)
                dve.scalar_tensor_tensor(arr(d, SL_KH, lat), arr(d, None, lat), col("r_k"),
                                         arr(d, SL_K, lat), ALU.mult, ALU.mult).then_inc(S["rk_done"], 1)
                dve.wait_ge(S["exp_done"], 2 * d + 2)
                dve.wait_ge(S["pool_link"], 6)
                link(dve.tensor_tensor_scan(line(cum[d]), line(St[d]), line(starts), 0.0, ALU.mult, ALU.add))
                dve.tensor_tensor_scan(line(St[d]), line(wd[d]), line(starts), 0.0, ALU.mult, ALU.add).then_inc(S["feat_done"], 1)
                dve.scalar_tensor_tensor(f3(SL_A), f3(SL_A), -1.0, cum[d][:, :, 0:CH], ALU.mult, ALU.mult)
                dve.wait_ge(S["feat_done"], 3 * d + 1)
                dve.tensor_tensor(f3(SL_B), f3(SL_B), St[d][:, :, 1:], ALU.mult).then_inc(S["feat_done"], 1)
                dve.tensor_tensor(f3(SL_K), f3(SL_K), St[d][:, :, 1:], ALU.mult).then_inc(S["feat_done"], 1)
                dve.wait_ge(S["rk_sum"], d + 1)
                bon = bonus if d == 0 else tmp
                link(dve.tensor_tensor(chunks(bon[:]), chunks(bank[2 * d + 1][:, 0:512]), arr(d, SL_V, lat), ALU.mult))
            dve.wait_ge(S["feat_done"], 6)
            dve.tensor_tensor(bonus[:], bonus[:], flip(tmp[:]), ALU.add)


def pair_chunks(g, k, f_dram, p, L):
    nc = g.nc
    S, SD, SG, stacks, AR, R, cum, Em, BK, UV, Ms, Ml, X, T, Y1, AM, Wt, Gt, Dg, Qt, St = (
        L[n] for n in ("S", "SD", "SG", "stacks", "AR", "R", "cum", "Em", "BK", "UV", "Ms", "Ml", "X", "T", "Y1", "AM", "Wt", "Gt", "Dg",
                       "Qt", "St"))
    bk, bank, upper, levels, diag2, ident, ysum = (L[n] for n in ("bk", "bank", "upper", "levels", "diag2", "ident", "ysum"))
    HP = [slice(0, HD), slice(HD, P)]
    OWN, OTH = HP, [HP[1], HP[0]]
    flat = lambda ap: ap.rearrange("p c n -> p (c n)")

    def quarter(ap, c, n=CH):
        return ap[:, c * n:(c + 1) * n]

    def stacked(d, b, c, j):
        return stacks[d][j][:, b * CPB + c, :, :].rearrange("p a n -> p (a n)")

    def arr(d, s, b, c, h):
        return stacks[d][s[0]][HP[h], b * CPB + c, s[1] ^ d, :]

    def lanes(h):
        return slice(h * CH, (h + 1) * CH)

    def wu_out(eng, copy, b, h):
        s = SG[h]
        eng.wait_ge(s["wu_done"], b + 1)
        wu = bk(2, h).rearrange("p (c a n) -> p c a n", c=CPB, a=2)
        copy(Wt[h][:], wu[:, :, 0, :])
        for d in range(2):
            m = copy(UV[d][OWN[d], :, lanes(h)], wu[OWN[d], :, 1, :])
        m.then_inc(s["wu_out"], 1)

    with nc.Block() as block:

        @block.sync
        def _(sp):
            load_pair(sp, k, f_dram, (p + 1) % PAIRS, L, S["pair_in"])

        @block.tensor
        def _(pe):
            for b in range(NB):
                lat = b > 0
                for d in range(2):
                    s = SD[d]
                    if b:
                        pe.wait_ge(SG[d]["wu_out"], b)
                        pe.wait_ge(SG[1 - d]["wu_out"], b)
                        pe.wait_ge(s["gq_out"], b)
                    for j in (1, 2):
                        for c in range(CPB):
                            m = pe.transpose(bk(2 + d, j - 1)[:, c * P:(c + 1) * P], stacked(d, b, c, j), ident[:])
                    m.then_inc(s["turned"], 1)
                for d in range(2):
                    s = SD[d]
                    if b:
                        for e in range(2):
                            pe.wait_ge(SD[e]["state_out"], CPB * b)
                            if b > 1:
                                pe.wait_ge(SD[e]["y_out"], b - 1)
                    for c in range(CPB):
                        rhs = AR[d][:, b * CPB + c, :, :, :] if lat else AR[d][:, b * CPB + c, :, 0, :]
                        n = 2 * P if lat else P
                        m = pe.matmul(bank[d][:, c * n:(c + 1) * n], stacked(d, b, c, 0), rhs, start=True, stop=True)
                    m.then_inc(s["e_done"], 1)
                pe.wait_ge(SD[0]["e_out"], b + 1)
                for h in range(2):
                    for c in range(CPB):
                        for d in range(2):
                            m = pe.matmul(quarter(bk(0, h), c)[OWN[d]], arr(d, SL_A, b, c, h), arr(d, SL_B, b, c, h), start=True, stop=True)
                    m.then_inc(SG[h]["m_done"], 1)
                pe.wait_ge(SD[1]["e_out"], b + 1)
                for d in range(2):
                    pe.wait_ge(SD[d]["turned_out"], b + 1)
                for h in range(2):
                    for c in range(CPB):
                        for d in range(2):
                            m = pe.matmul(quarter(bk(1, h), c)[OWN[d]], Em[d][OTH[d], c, h, 0, :], UV[d][OTH[d], c, lanes(h)],
                                          start=True, stop=True)
                    m.then_inc(SG[h]["mv_done"], 1)
                for lev in range(NLEV):
                    for h in range(2):
                        s = SG[h]
                        if lev == 0:
                            pe.wait_ge(s["m_out"], b + 1)
                            pe.wait_ge(s["turned_x"], NLEV * b + 1)
                        else:
                            pe.wait_ge(s["joined"], NLEV * b + lev)
                        pe.wait_ge(s["levels"], NLEV * b + lev + 1)
                        for c in range(CPB):
                            m = pe.matmul(bk(0, h)[:, c * P:(c + 1) * P], Ml[h][lev % 2][:, c, :], X[h][:, c, :], start=True, stop=True)
                        m.then_inc(s["half_done"], 1)
                    for h in range(2):
                        s = SG[h]
                        pe.wait_ge(s["half_out"], NLEV * b + lev + 1)
                        if lev == 0:
                            pe.wait_ge(s["mv_out"], b + 1)
                        else:
                            pe.wait_ge(s["turned_x"], NLEV * b + lev + 1)
                        for c in range(CPB):
                            m = pe.matmul(bk(1, h)[:, c * P:(c + 1) * P], T[h][:, c, :], Y1[h][:, c, :], start=True, stop=True)
                        m.then_inc(s["join_done"], 1)
                for h in range(2):
                    s = SG[h]
                    pe.wait_ge(s["joined"], NLEV * (b + 1))
                    for c in range(CPB):
                        m = pe.matmul(bk(2, h)[:, c * P:(c + 1) * P], X[h][:, c, :], AM[h][:, c, :], start=True, stop=True)
                    m.then_inc(s["wu_done"], 1)
                for h in range(2):
                    pe.wait_ge(SG[h]["wu_out"], b + 1)
                for d in range(2):
                    for c in range(CPB):
                        for h in range(2):
                            m = pe.matmul(quarter(bk(3, d), c)[HP[h]], Wt[h][OWN[d], c, :], BK[d][OWN[d], c, lanes(h)],
                                          start=True, stop=True)
                            if lat:
                                m = pe.matmul(quarter(bk(3, d), CPB + c)[HP[h]], Wt[h][OWN[d], c, :], Em[d][OWN[d], c, h, 1, :],
                                              start=True, stop=True)
                    m.then_inc(SD[d]["gq_done"], 1)
                for c in range(CPB):
                    for d in range(2):
                        s = SD[d]
                        n = b * CPB + c
                        if c == 0:
                            pe.wait_ge(s["gq_out"], b + 1)
                        if n:
                            pe.wait_ge(s["state_out"], n)
                        if n < CHUNKS - 1:
                            for h in range(2):
                                m = pe.matmul(quarter(bk(0, d), c)[HP[h]], BK[d][:, c, lanes(h)], UV[d][:, c, lanes(h)],
                                              start=True, stop=(n == 0))
                                if n:
                                    m = pe.matmul(quarter(bk(0, d), c)[HP[h]], Gt[d][HP[h], c, :], St[d][HP[h], n, 1:],
                                                  start=False, stop=True)
                            m.then_inc(s["state_done"], 1)
                        if lat:
                            for h in range(2):
                                pe.matmul(quarter(bk(1, d), c)[HP[h]], UV[d][:, c, lanes(h)], Em[d][:, c, h, 1, :],
                                          start=True, stop=False)
                                m = pe.matmul(quarter(bk(1, d), c)[HP[h]], St[d][HP[h], n, 1:], Qt[d][HP[h], c, :],
                                              start=False, stop=True)
                            if c == CPB - 1:
                                m.then_inc(s["y_done"], 1)

        @block.scalar
        def _(act):
            for b in range(NB):
                for d in range(2):
                    s = SD[d]
                    act.wait_ge(s["turned"], b + 1)
                    act.copy(flat(BK[d][:]), bk(2 + d, 0))
                    act.copy(flat(UV[d][OTH[d]]), bk(2 + d, 1)[OTH[d]])
                    av = bk(2 + d, 1).rearrange("p (c h n) -> p c h n", c=CPB, h=2)
                    for h in range(2):
                        m = act.copy(AM[h][OWN[d], :, 0:CH], av[OWN[d], :, h, :])
                    m.then_inc(s["turned_out"], 1)
                for h in range(2):
                    s = SG[h]
                    act.wait_ge(s["m_done"], b + 1)
                    act.copy(flat(Ms[h][:]), bk(0, h)[:, 0:CPB * CH]).then_inc(s["m_out"], 1)
                for h in range(2):
                    s = SG[h]
                    act.wait_ge(s["mv_done"], b + 1)
                    act.copy(AM[h][:, :, CH:P], bk(1, h)[:, 0:CPB * CH].rearrange("p (c n) -> p c n", c=CPB)).then_inc(s["mv_out"], 1)
                for lev in range(NLEV):
                    for h in range(2):
                        s = SG[h]
                        act.wait_ge(s["half_done"], NLEV * b + lev + 1)
                        act.copy(flat(Y1[h][:]), bk(0, h)).then_inc(s["half_out"], 1)
                wu_out(act, act.copy, b, 0)

        def masked(eng, dst, h, lev):
            return eng.tensor_tensor(dst.rearrange("p c (a n) -> p c a n", a=2),
                                     Ms[h][:].unsqueeze(2).to_broadcast([P, CPB, 2, CH]),
                                     levels[:, lev, :].rearrange("p (a n) -> p a n", a=2).unsqueeze(1).to_broadcast([P, CPB, 2, CH]),
                                     ALU.mult)

        @block.gpsimd
        def _(pool):
            for b in range(NB):
                for lev in range(NLEV):
                    for h in range(2):
                        s = SG[h]
                        if lev == 0:
                            pool.wait_ge(s["m_out"], b + 1)
                            if b:
                                pool.wait_ge(s["wu_done"], b)
                        if lev > 1:
                            pool.wait_ge(s["half_done"], NLEV * b + lev - 1)
                        masked(pool, Ml[h][lev % 2], h, 1 + lev).then_inc(s["levels"], 1)
                for d in range(2):
                    s = SD[d]
                    if b:
                        pool.wait_ge(s["gq_out"], b)
                    pool.tensor_tensor(Dg[d][:], diag2.unsqueeze(1).to_broadcast([P, CPB, CH]),
                                       cum[d][:, b * CPB:(b + 1) * CPB, CH:CH + 1].to_broadcast([P, CPB, CH]),
                                       ALU.mult).then_inc(s["diag"], 1)

        @block.vector
        def _(dve):
            for b in range(NB):
                lat = b > 0
                for d in range(2):
                    s = SD[d]
                    dve.wait_ge(s["e_done"], b + 1)
                    if lat:
                        src = bank[d][:].rearrange("p (u a n) -> p u a n", a=2, n=CH)
                        dve.tensor_tensor(Em[d][:].rearrange("p c h a n -> p (c h) a n"), src,
                                          upper[:, 0:2, :].unsqueeze(1).to_broadcast([P, 2 * CPB, 2, CH]), ALU.mult).then_inc(s["e_out"], 1)
                    else:
                        dve.tensor_tensor(Em[d][:, :, :, 0, :].rearrange("p c h n -> p (c h) n"),
                                          bank[d][:, 0:512].rearrange("p (u n) -> p u n", n=CH),
                                          upper[:, 0, :].unsqueeze(1).to_broadcast([P, 2 * CPB, CH]), ALU.mult).then_inc(s["e_out"], 1)
                for h in range(2):
                    s = SG[h]
                    dve.wait_ge(s["m_out"], b + 1)
                    masked(dve, T[h][:], h, 0).then_inc(s["paired"], 1)
                    dve.wait_ge(s["paired"], b + 1)
                    dve.tensor_tensor(T[h][:], T[h][:], ident[:].unsqueeze(1).to_broadcast([P, CPB, P]), ALU.add).then_inc(s["seeded"], 1)
                    dve.wait_ge(s["seeded"], b + 1)
                    dve.transpose(flat(X[h][:]), flat(T[h][:])).then_inc(s["turned_x"], 1)
                for lev in range(NLEV):
                    for h in range(2):
                        s = SG[h]
                        dve.wait_ge(s["join_done"], NLEV * b + lev + 1)
                        dve.tensor_tensor(flat(X[h][:]), flat(X[h][:]), bk(1, h), ALU.add).then_inc(s["joined"], 1)
                        if lev < NLEV - 1:
                            dve.wait_ge(s["joined"], NLEV * b + lev + 1)
                            dve.transpose(flat(T[h][:]), flat(X[h][:])).then_inc(s["turned_x"], 1)
                wu_out(dve, dve.tensor_copy, b, 1)
                for d in range(2):
                    s = SD[d]
                    dve.wait_ge(s["gq_done"], b + 1)
                    dve.wait_ge(s["diag"], b + 1)
                    m = dve.tensor_tensor(flat(Gt[d][:]), bk(3, d)[:, 0:CPB * CH], flat(Dg[d][:]), ALU.add)
                    if lat:
                        m = dve.tensor_tensor(flat(Qt[d][:]), bk(3, d)[:, CPB * CH:512],
                                              flat(R[d][:, b * CPB:(b + 1) * CPB, :]), ALU.add)
                    m.then_inc(s["gq_out"], 1)
                for c in range(CPB):
                    for d in range(2):
                        s = SD[d]
                        n = b * CPB + c
                        if n < CHUNKS - 1:
                            dve.wait_ge(s["state_done"], n + 1)
                            dve.tensor_copy(St[d][:, n + 1, 1:], quarter(bk(0, d), c)).then_inc(s["state_out"], 1)
                if lat:
                    for d in range(2):
                        s = SD[d]
                        dve.wait_ge(s["y_done"], b)
                        if b == 2 or d == 1:
                            dve.wait_ge(SD[1 - d]["y_out"], b if d == 1 else b - 1)
                        if b == 2:
                            dve.wait_ge(s["y_out"], b - 1)
                        y = ysum[:, (b - 1) * BT:b * BT]
                        if d:
                            y = flip(ysum[:])[:, (b - 1) * BT:b * BT]
                        dve.tensor_tensor(y, y, bk(1, d)[:, 0:CPB * CH], ALU.add).then_inc(s["y_out"], 1)


def pair_readout(g, p, mix, L):
    nc = g.nc
    S, bk, ysum, tmp, bonus, head_ones, g2, sg, pv, lnx_eps, wd = (
        L[n] for n in ("S", "bk", "ysum", "tmp", "bonus", "head_ones", "g2", "sg", "pv", "lnx_eps", "wd"))
    col = lambda n: pv[:, PV[n]:PV[n] + 1]
    sq, rs = (wd[d][:].rearrange("p c n -> p (c n)")[:, 0:LAT] for d in range(2))
    with nc.Block() as block:

        @block.tensor
        def _(pe):
            pe.matmul(bk(0, 0), head_ones[:], ysum[:], start=True, stop=True).then_inc(S["mean_done"], 1)
            for j in range(2):
                m = pe.matmul(bk(2, 0), g2[:, j, :], sg[:, j, :], start=(j == 0), stop=(j == 1))
            m.then_inc(S["gate_done"], 1)
            pe.wait_ge(S["csq_done"], 1)
            pe.matmul(bk(1, 0), head_ones[:], sq, start=True, stop=True).then_inc(S["var_done"], 1)

        @block.scalar
        def _(act):
            act.wait_ge(S["cent_done"], 1)
            act.activation(sq, tmp[:], ACT.Square).then_inc(S["csq_done"], 1)
            act.wait_ge(S["var_done"], 1)
            act.activation(rs, bk(1, 0), ACT.Sqrt, bias=lnx_eps[:, 0:1], scale=1.0 / HD).then_inc(S["std_done"], 1)

        @block.vector
        def _(dve):
            link = Link(dve, S["read_link"])
            dve.wait_ge(S["mean_done"], 1)
            dve.scalar_tensor_tensor(tmp[:], bk(0, 0), -1.0 / HD, ysum[:], ALU.mult, ALU.add).then_inc(S["cent_done"], 1)
            dve.wait_ge(S["std_done"], 1)
            link(dve.reciprocal(rs, rs))
            link(dve.scalar_tensor_tensor(tmp[:], tmp[:], col("lnx_g"), rs, ALU.mult, ALU.mult))
            link(dve.scalar_tensor_tensor(tmp[:], tmp[:], col("lnx_b"), bonus[:], ALU.add, ALU.add))
            dve.wait_ge(S["gate_done"], 1)
            dve.tensor_tensor(mix[:, bass.ds(p + 8, 1), :].rearrange("p a n -> p (a n)"), tmp[:], bk(2, 0),
                              ALU.mult).then_inc(S["mixed_out"], 1)


def clear(nc, sems):
    numbers = sorted(s.num for s in sems.values())
    starts = [n for n in numbers if n - 1 not in numbers]
    with nc.Block() as block:

        @block.gpsimd
        def _(pool):
            for n in starts:
                end = n
                while end in numbers:
                    end += 1
                pool.sem_clear(range(n, end))


def group_norm(g, mix, vec, ones, eps, hi, lo):
    nc = g.nc
    GROUPS = ((0, 4), (4, 8), (8, 16))
    with ExitStack() as st:
        sq = g.sb(st, "grp_sq", [P, 4, LAT])
        parts = g.sb(st, "grp_parts", [P, 3, LAT])
        inv = g.sb(st, "grp_inv", [P, 3, LAT])
        acc = [g.ps(st, f"grp_acc{j}", [P, 512]) for j in range(3)]
        total, rms_done, inv_done, normed, hi_done = g.sems(
            st, *["grp_" + x for x in ("total", "rms_done", "inv_done", "normed", "hi_done")])
        sums = g.sems(st, *["grp_" + x for x in ("even_in", "added", "odd_in", "summed")])
        with nc.Block() as block:
            squares, additions, products = square_sums(block, mix, LAT, GROUPS, ones, sq, parts, acc, sums)

            @block.scalar
            def _(act):
                squares(act)
                for j, (a, b) in enumerate(GROUPS):
                    act.wait_ge(total, j + 1)
                    act.activation(inv[:, j, :], acc[j][:], ACT.Sqrt, bias=eps[:, 0:1], scale=1.0 / ((b - a) * P)).then_inc(rms_done, 1)
                for t in range(KT):
                    act.wait_ge(normed, t + 1)
                    act.copy(hi[:, t, :], mix[:, t, :]).then_inc(hi_done, 1)

            @block.tensor
            def _(pe):
                products(pe, total)

            def lo_part(eng, t):
                eng.wait_ge(normed, t + 1)
                eng.wait_ge(hi_done, t + 1)
                eng.tensor_tensor(lo[:, t, :], mix[:, t, :], hi[:, t, :].bitcast(F32), ALU.subtract)

            @block.gpsimd
            def _(pool):
                for t in range(1, KT, 2):
                    lo_part(pool, t)

            @block.vector
            def _(dve):
                additions(dve)
                for j, (a, b) in enumerate(GROUPS):
                    dve.wait_ge(rms_done, j + 1)
                    dve.reciprocal(inv[:, j, :], inv[:, j, :]).then_inc(inv_done, 1)
                for t in range(KT):
                    j = 0 if t < 4 else 1 if t < 8 else 2
                    dve.wait_ge(inv_done, 3)
                    dve.scalar_tensor_tensor(mix[:, t, :], mix[:, t, :], vec[:, VEC["grp_g"] + t:VEC["grp_g"] + t + 1],
                                             inv[:, j, :], ALU.mult, ALU.mult).then_inc(normed, 1)
                    if t >= 3 and t % 2:
                        lo_part(dve, t - 3)
                lo_part(dve, KT - 2)


def output_projection(g, k, mhi, mlo, h, h_dram, mod):
    nc = g.nc
    w = k["w_out"].rearrange("(k p) n -> p k n", p=P)
    gate = mod[:, 0, 2 * KT:3 * KT]
    with ExitStack() as st:
        ws = WeightStream(g, st, "wout")
        acc = [g.ps(st, f"wout_acc{i}", [P, 512]) for i in range(2)]
        added, h_back = g.sems(st, "wout_added", "wout_h_back")
        with nc.Block() as block:

            @block.sync
            def _(sp):
                ws.credits(sp)
                sp.sem_inc(added, 2)
                with sp.Fori(0, KT // 2) as i:
                    for s in range(2):
                        ws.load(sp, i * 2, s, w[:, :, bass.ds(i * 2 * P + s * P, P)])
                ws.load(sp, KT, 0, w[:, :, 0:P])

            @block.scalar
            def _(act):
                ws.split_hi(act, 0, 0, 0)
                act.dma_start(h[:], h_dram).then_inc(h_back, 16)
                with act.Fori(0, KT // 2) as i:
                    for s in range(2):
                        ws.split_hi(act, i, i * 2, s + 1)

            @block.vector
            def _(dve):
                ws.split_lo(dve, 0, 0)
                dve.wait_ge(h_back, 16)
                with dve.Fori(0, KT // 2) as i:
                    for s in range(2):
                        ws.split_lo(dve, i * 2, s + 1)
                        dve.wait_ge(ws.used, i * 2 + (s + 3))
                        x = h[:, bass.ds(i * 2 + s, 1), :].rearrange("p a n -> p (a n)")
                        gt = gate[:, bass.ds(i * 2 + s, 1)]
                        dve.scalar_tensor_tensor(x, acc[s][:], gt, x, ALU.mult, ALU.add).then_inc(added, 1)

            @block.tensor
            def _(pe):
                with pe.Fori(0, KT // 2) as i:
                    for s in range(2):
                        ws.ready(pe, i * 2, s)
                        pe.wait_ge(added, i * 2 + (s + 1))
                        for kk in range(KT):
                            a, b = (x[s][:, kk * P:(kk + 1) * P] for x in (ws.hi, ws.lo))
                            m = three_passes(pe, acc[s][:], a, b, mhi[:, kk, :], mlo[:, kk, :], kk == 0, kk == KT - 1)
                        m.then_inc(ws.used, 1)


FC = 4
CHUNKS_FF = FT // FC


def conv_glu(g, k, xhi, xlo, h, mod, vec):
    nc = g.nc
    up = k["ffn_up"].rearrange("(k p) n -> p k n", p=P)
    down = k["ffn_down"].rearrange("(j p) n -> p j n", p=P)
    gate = mod[:, 0, 5 * KT:6 * KT]
    UPS = 2 * FC
    DOWNS = KT // 4
    PER = UPS + DOWNS
    with ExitStack() as st:
        ws = WeightStream(g, st, "ffn")
        conv = g.sb(st, "ffn_conv", [P, 2, LAT])
        act_hi = g.sb(st, "ffn_act_hi", [P, FC, LAT], F32R)
        act_lo = g.sb(st, "ffn_act_lo", [P, FC, LAT], F32R)
        up_acc = [g.ps(st, f"ffn_up_acc{i}", [P, 512]) for i in range(4)]
        dn_acc = [g.ps(st, f"ffn_dn_acc{i}", [P, 512]) for i in range(4)]
        tapped, taps, gelu_done, glu_done, act_hi_done, act_lo_done, dn_done, added, v_free = g.sems(
            st, *["ffn_" + x for x in ("tapped", "taps", "gelu_done", "glu_done", "act_hi_done", "act_lo_done", "dn_done",
                                       "added", "v_free")])

        def vcol(name, i, j):
            return vec[:, bass.ds(i * FC + (VEC[name] + j), 1)]

        with nc.Block() as block:

            @block.sync
            def _(sp):
                ws.credits(sp)
                sp.sem_inc(glu_done, 2)
                sp.sem_inc(added, 4)
                with sp.Fori(0, CHUNKS_FF) as i:
                    for s in range(UPS):
                        ws.load(sp, i * PER, s, up[:, :, bass.ds(i * FC * P + (s % 2 * DFF + s // 2 * P), P)])
                    for s in range(DOWNS):
                        ws.load(sp, i * PER, UPS + s, down[:, bass.ds(i * FC, FC), s * 512:(s + 1) * 512])
                ws.load(sp, CHUNKS_FF * PER, 0, up[:, :, 0:P])

            @block.scalar
            def _(act):
                ws.split_hi(act, 0, 0, 0)
                with act.Fori(0, CHUNKS_FF) as i:
                    for s in range(PER):
                        ws.split_hi(act, i * (PER // 2), i * PER, s + 1)
                        if s >= UPS:
                            continue
                        j = s // 2
                        if s % 2 == 0:
                            act.wait_ge(ws.used, i * PER + (s + 3))
                            act.activation(conv[:, j % 2, :], up_acc[j % 2 * 2][:], ACT.Identity, bias=vcol("conv_b", i, j),
                                           scale=vcol("conv_w1", i, j)).then_inc(tapped, 1)
                        else:
                            act.wait_ge(taps, i * 2 * FC + (2 * j + 2))
                            act.activation(conv[:, j % 2, :], conv[:, j % 2, :], ACT.Gelu).then_inc(gelu_done, 1)
                            act.wait_ge(glu_done, i * FC + (j + 3))
                            act.copy(act_hi[:, j, :], conv[:, j % 2, :]).then_inc(act_hi_done, 1)

            @block.vector
            def _(dve):
                ws.split_lo(dve, 0, 0)
                with dve.Fori(0, CHUNKS_FF) as i:
                    for s in range(PER):
                        ws.split_lo(dve, i * PER, s + 1)
                        if s < UPS and s % 2 == 0:
                            j = s // 2
                            c, u = conv[:, j % 2, :], up_acc[j % 2 * 2]
                            dve.wait_ge(tapped, i * FC + (j + 1))
                            dve.scalar_tensor_tensor(c[:, 1:LAT], u[:, 0:LAT - 1], vcol("conv_w0", i, j), c[:, 1:LAT], ALU.mult,
                                                     ALU.add).then_inc(taps, 1)
                            dve.wait_ge(taps, i * 2 * FC + (2 * j + 1))
                            dve.scalar_tensor_tensor(c[:, 0:LAT - 1], u[:, 1:LAT], vcol("conv_w2", i, j), c[:, 0:LAT - 1],
                                                     ALU.mult, ALU.add).then_inc(taps, 1)
                        elif s < UPS:
                            j = s // 2
                            c = conv[:, j % 2, :]
                            dve.wait_ge(gelu_done, i * FC + (j + 1))
                            dve.wait_ge(ws.used, i * PER + (s + 3))
                            dve.tensor_tensor(c, c, up_acc[j % 2 * 2 + 1][:], ALU.mult).then_inc(glu_done, 1)
                            dve.wait_ge(act_hi_done, i * FC + (j + 1))
                            dve.tensor_tensor(act_lo[:, j, :], c, act_hi[:, j, :].bitcast(F32), ALU.subtract).then_inc(act_lo_done, 1)
                        else:
                            for o in range(4):
                                t = (s - UPS) * 4 + o
                                if o < 3:
                                    dve.wait_ge(dn_done, i * (3 * DOWNS) + (3 * (s - UPS) + o + 1))
                                else:
                                    dve.wait_ge(ws.used, i * PER + (s + 3))
                                dve.scalar_tensor_tensor(h[:, t, :], dn_acc[o][:], gate[:, t:t + 1], h[:, t, :], ALU.mult,
                                                         ALU.add).then_inc(added, 1)

            @block.tensor
            def _(pe):
                with pe.Fori(0, CHUNKS_FF) as i:
                    for s in range(UPS):
                        j = s // 2
                        ws.ready(pe, i * PER, s)
                        pe.wait_ge(glu_done, i * FC + (j + 1))
                        for kk in range(KT):
                            a, b = (x[s % 2][:, kk * P:(kk + 1) * P] for x in (ws.hi, ws.lo))
                            m = three_passes(pe, up_acc[j % 2 * 2 + s % 2][:], a, b, xhi[:, kk, :], xlo[:, kk, :], kk == 0,
                                             kk == KT - 1)
                        m.then_inc(ws.used, 1)
                    for s in range(DOWNS):
                        ws.ready(pe, i * PER, UPS + s)
                        for js in (range(FC - 1), (FC - 1,)):
                            if js[0] == FC - 1:
                                pe.wait_ge(act_lo_done, i * FC + FC)
                            for o in range(4):
                                if js[0] == 0:
                                    if s == 0 and o == 0:
                                        pe.wait_ge(act_lo_done, i * FC + (FC - 1))
                                    pe.wait_ge(added, i * KT + (4 * s + o + 1))
                                for j in js:
                                    c0 = j * 512 + o * P
                                    a, b = (x[s % 2][:, c0:c0 + P] for x in (ws.hi, ws.lo))
                                    m = three_passes(pe, dn_acc[o][:], a, b, act_hi[:, j, :], act_lo[:, j, :], j == 0, j == FC - 1)
                                if js[0] == FC - 1 and o < 3:
                                    m.then_inc(dn_done, 1)
                        m.then_inc(ws.used, 1)


def store_transposed(g, src, dst, ident):
    nc = g.nc
    with ExitStack() as st:
        rows = [g.sb(st, f"out_rows{i}", [P, D]) for i in range(2)]
        tp = [g.ps(st, f"out_tp{i}", [P, 4, P]) for i in range(4)]
        turned, act_out, dve_out = g.sems(st, "out_turned", "out_act_copied", "out_dve_copied")
        stored = g.sems(st, "out_stored0", "out_stored1")
        NT = LAT // P
        with nc.Block() as block:

            @block.tensor
            def _(pe):
                for t in range(NT):
                    for q in range(4):
                        if t:
                            pe.wait_ge((act_out, dve_out)[q % 2], 2 * (t - 1) + q // 2 + 1)
                        for j in range(4):
                            m = pe.transpose(tp[q][:, j, :], src[:, 4 * q + j, t * P:(t + 1) * P], ident[:])
                        m.then_inc(turned, 1)

            def copies(eng, copy, par, out):
                for t in range(NT):
                    if t >= 2:
                        eng.wait_ge(stored[t % 2], 16)
                    for q in (par, par + 2):
                        eng.wait_ge(turned, 4 * t + q + 1)
                        copy(rows[t % 2][:, q * 512:(q + 1) * 512], tp[q][:].rearrange("p a b -> p (a b)")).then_inc(out, 1)

            @block.scalar
            def _(act):
                copies(act, act.copy, 0, act_out)

            @block.vector
            def _(dve):
                copies(dve, dve.tensor_copy, 1, dve_out)

            @block.sync
            def _(sp):
                for t in range(NT):
                    sp.wait_ge(act_out, 2 * t + 2)
                    sp.wait_ge(dve_out, 2 * t + 2)
                    sp.dma_start(dst[t * P:(t + 1) * P, :], rows[t % 2][:]).then_inc(stored[t % 2], 16)
                for s in range(2):
                    sp.wait_ge(stored[s], 16 * (NT // 2))


INS = ("x", "ctx", "ada_w", "w_in", "na_rpb", "rw_w2", "rw_a2", "rw_g2", "w_out", "ffn_up", "ffn_down", "vectors",
       "pair_vectors")


def build(nc, k, out):
    g = Ctx(nc)
    const = shape_constants()
    const["sum_parts"] = np.array([[1, 0], [1, 0], [0, 1], [0, 1]], np.float32)
    k = dict(k)
    for name, a in const.items():
        k[name] = nc.inline_tensor(np.ascontiguousarray(a), "const_" + name).ap()
    f_dram = nc.dram_tensor("f_scratch", [F_ROWS, TOK], F32, kind="Internal").ap()
    with ExitStack() as st:
        vec = g.sb(st, "vec", [P, NVEC])
        ident = g.sb(st, "ident", [P, P])
        ones = g.sb(st, "ones", [P, P])
        eps = g.sb(st, "eps", [P, 1])
        mod = g.sb(st, "mod", [P, 2, 96])
        gain = g.sb(st, "gain", [P, 3, KT])
        (setup_in, setup_done) = g.sems(st, "setup_in", "setup_done")
        with nc.Block() as block:

            @block.sync
            def _(sp):
                sp.dma_start(vec[:], k["vectors"]).then_inc(setup_in, 16)
                sp.dma_start(ident[:], k["ident"]).then_inc(setup_in, 16)
                sp.wait_ge(setup_in, 32)

            @block.vector
            def _(dve):
                dve.memset(ones[:], 1.0)
                dve.memset(eps[:], EPS)

        sel = g.sb(st, "sum_parts", [4, 2])
        with ExitStack() as st1:
            cond = g.sb(st1, "cond_parts", [P, KT, P], F32R)
            condition(g, vec, cond[:], "cond")
            modulation(g, k, vec, cond, sel, mod)
        h_dram = nc.dram_tensor("h_scratch", [P, KT, LAT], F32, kind="Internal").ap()
        hst = st.enter_context(ExitStack())
        h = g.sb(hst, "h", [P, KT, LAT])
        load_transposed(g, k["x"], LAT // 256, h, ident, "x")
        with nc.Block() as block:

            @block.vector
            def _(dve):
                for n, s, j, name in ((0, 0, 1, "norm1_g"), (2, 1, 1, "norm1_g")):
                    dve.scalar_tensor_tensor(gain[:, n, :], mod[:, s, j * KT:(j + 1) * KT], 1.0,
                                             vec[:, VEC[name]:VEC[name] + KT], ALU.add, ALU.mult)

        with ExitStack() as st1:
            xhi = g.sb(st1, "xhi", [P, KT, LAT], F32R)
            xlo = g.sb(st1, "xlo", [P, KT, LAT], F32R)
            chi = g.sb(st1, "chi", [P, KT, CTX], F32R)
            clo = g.sb(st1, "clo", [P, KT, CTX], F32R)
            with ExitStack() as st2:
                hc = g.sb(st2, "hc", [P, KT, CTX])
                load_transposed(g, k["ctx"], CTX // 256, hc, ident, "ctx")
                norm_split(g, hc, CTX, ones, eps, gain[:, 2, :], mod[:, 1, 0:KT], chi, clo, "nc")
            norm_split(g, h, LAT, ones, eps, gain[:, 0, :], mod[:, 0, 0:KT], xhi, xlo, "n1")
            input_projection(g, k, xhi, xlo, chi, clo, f_dram, h, h_dram)
        hst.close()
        mst = st.enter_context(ExitStack())
        mix = g.sb(mst, "mix", [P, KT, LAT])
        with ExitStack() as st1:
            cond = g.sb(st1, "cond_parts_again", [P, KT, P], F32R)
            condition(g, vec, cond[:], "cond2")
            attention(g, k, f_dram, mix, ident, vec, eps, cond, sel, mod)
        with nc.Block() as block:

            @block.vector
            def _(dve):
                dve.scalar_tensor_tensor(gain[:, 1, :], mod[:, 0, 4 * KT:5 * KT], 1.0, vec[:, VEC["norm2_g"]:VEC["norm2_g"] + KT],
                                         ALU.add, ALU.mult)

        rwkv(g, k, f_dram, mix, ident, vec, eps)
        mhi = g.sb(mst, "mix_hi", [P, KT, LAT], F32R)
        mlo = g.sb(mst, "mix_lo", [P, KT, LAT], F32R)
        group_norm(g, mix, vec, ones, eps, mhi, mlo)
        h = mix
        output_projection(g, k, mhi, mlo, h, h_dram, mod)
        norm_split(g, h, LAT, ones, eps, gain[:, 1, :], mod[:, 0, 3 * KT:4 * KT], mhi, mlo, "n2")
        conv_glu(g, k, mhi, mlo, h, mod, vec)
        norm_split(g, h, LAT, ones, eps, vec[:, VEC["final_g"]:VEC["final_g"] + KT], None, None, None, "nf", out=mix)
        store_transposed(g, mix, out[0], ident)


def layout(inputs):
    a = {n: np.ascontiguousarray(np.asarray(v)) for n, v in inputs.items()}
    col = lambda v: v.reshape(-1, P).T
    both = lambda v: np.concatenate([v, v]).reshape(P, 1)
    g2 = lambda v: np.stack([v[:P], np.concatenate([v[P:], np.zeros(96, v.dtype)])], 1)
    conv = a["ffn_conv_w"][0]
    vectors = np.concatenate(
        [col(a["norm1_g"][0]), col(a["norm2_g"][0]), col(a["final_g"]), col(a["c"][0]), col(a["c_ctx"]), col(a["ada_b"][0]),
         col(a["grp_g"][0]), col(conv[0]), col(conv[1]), col(conv[2]), col(a["ffn_conv_b"][0]), both(a["q_gain"][0]),
         both(a["k_gain"][0]), a["rw_mu_w"][0].reshape(P, 1), a["rw_mu_a"][0].reshape(P, 1), g2(a["rw_mu_g"][0, 0]),
         g2(a["rw_mu_g"][0, 1])], 1)
    mu = a["rw_mu_rkv"][0].reshape(2, 3, PAIRS, P)
    per = [mu[d, j] for j in range(3) for d in range(2)]
    per += [a["rw_w0"][0, d].reshape(PAIRS, P) for d in range(2)] + [a["rw_a0"][0, d].reshape(PAIRS, P) for d in range(2)]
    per += [a[n][0].reshape(PAIRS, P) for n in ("rw_k_k", "rw_k_a", "rw_r_k", "rw_lnx_g", "rw_lnx_b")]
    arrays = {
        "x": a["x"][0], "ctx": a["ctx"][0], "ada_w": a["ada_w"][0], "w_in": a["w_in"][0], "na_rpb": np.pad(a["na_rpb"][0][:, :, ::-1].reshape(-1), RPB_PAD),
        "rw_w2": a["rw_w2"][0].reshape(2 * HD, CW), "rw_a2": a["rw_a2"][0].reshape(2 * HD, CW),
        "rw_g2": a["rw_g2"][0], "w_out": a["w_out"][0], "ffn_up": a["ffn_up"][0], "ffn_down": a["ffn_down"][0],
        "vectors": vectors, "pair_vectors": np.stack(per, 2),
    }
    return {n: np.ascontiguousarray(v) for n, v in arrays.items()}


def kernel(**inputs):
    import concourse.bacc as bacc
    from concourse.bass_utils import run_bass_kernel_spmd

    nc = bacc.Bacc("TRN2", target_bir_lowering=False, num_devices=1)
    arrays = layout(inputs)
    k = {n: nc.dram_tensor(f"in_{n}", a.shape, mybir.dt.from_np(a.dtype), kind="ExternalInput").ap() for n, a in arrays.items()}
    out = nc.dram_tensor("out_h", (1, LAT, D), F32, kind="ExternalOutput").ap()
    build(nc, k, out)
    r = run_bass_kernel_spmd(nc, [{f"in_{n}": a for n, a in arrays.items()}], core_ids=[0])
    return r.results[0]["out_h"]
```
